# Optimizing a Trainium2 kernel written in Bass

```python
import math
import jax, jax.numpy as jnp
from jax import lax
import numpy as np

D_MODEL = 1024
BATCH = 1
SEQ = 1024
DEPTH = 1

S5_WIDTH = 512
S5_GROUP = 16
S5_GROUPS = S5_WIDTH // S5_GROUP
S5_STATE = 64
SGU_WIDTH = 512
SGU_HEADS = 4
SGU_HEAD_DIM = SGU_WIDTH // SGU_HEADS
SGU_CHUNK = 128
N_GROUPS = 4
EXPERTS_PER_GROUP = 8
N_EXPERTS = N_GROUPS * EXPERTS_PER_GROUP
TOP_K = 2
D_EXPERT = 512
MOE_BLOCK = 128
PLE_DIM = 256
IN_COLS = S5_WIDTH + 2 * SGU_WIDTH + 2 * D_MODEL
EPS = 1e-6

kernel_name = "hybrid_s5_sgu_hiermoe_ple"

def rms_norm(x, g):
    xf = x.astype(jnp.float32)
    y = xf * lax.rsqrt(jnp.mean(xf * xf, axis=-1, keepdims=True) + EPS)
    return (y * g.astype(jnp.float32)).astype(x.dtype)

def _complex_combine(c1, c2):
    a1r, a1i, b1r, b1i = c1
    a2r, a2i, b2r, b2i = c2
    ar = a1r * a2r - a1i * a2i
    ai = a1r * a2i + a1i * a2r
    a2rb, a2ib = a2r[:, None], a2i[:, None]
    br = a2rb * b1r - a2ib * b1i + b2r
    bi = a2rb * b1i + a2ib * b1r + b2i
    return (ar, ai, br, bi)

def s5_branch(u, a_re, a_im, log_dt, b_re, b_im, c_re, c_im, d_skip, w_glu):
    bsz, seq, _ = u.shape
    f32 = jnp.float32
    uf = u.astype(f32)
    ug = uf.reshape(bsz, seq, S5_GROUPS, S5_GROUP)
    a_re, a_im = a_re.astype(f32), a_im.astype(f32)
    b_re, b_im = b_re.astype(f32), b_im.astype(f32)
    c_re, c_im = c_re.astype(f32), c_im.astype(f32)
    dt = jnp.exp(log_dt.astype(f32))[:, None]
    mag = jnp.exp(a_re * dt)
    ang = a_im * dt
    lb_re, lb_im = mag * jnp.cos(ang), mag * jnp.sin(ang)
    den = a_re * a_re + a_im * a_im
    nr = lb_re - 1.0
    coef_re = (nr * a_re + lb_im * a_im) / den
    coef_im = (lb_im * a_re - nr * a_im) / den
    bb_re = coef_re[..., None] * b_re - coef_im[..., None] * b_im
    bb_im = coef_re[..., None] * b_im + coef_im[..., None] * b_re
    bu_re = jnp.einsum('blgc,gnc->lbgn', ug, bb_re)
    bu_im = jnp.einsum('blgc,gnc->lbgn', ug, bb_im)
    lam_re = jnp.broadcast_to(lb_re, (seq,) + lb_re.shape)
    lam_im = jnp.broadcast_to(lb_im, (seq,) + lb_im.shape)
    _, _, h_re, h_im = lax.associative_scan(_complex_combine, (lam_re, lam_im, bu_re, bu_im), axis=0)
    y = jnp.einsum('lbgn,gcn->blgc', h_re, c_re) - jnp.einsum('lbgn,gcn->blgc', h_im, c_im)
    y = y.reshape(bsz, seq, S5_WIDTH) + d_skip.astype(f32) * uf
    y = jax.nn.gelu(y).astype(u.dtype)
    z = y @ w_glu
    return z[..., :D_MODEL] * jax.nn.sigmoid(z[..., D_MODEL:])

def sgu_branch(u, v, norm_w, w_s, b_s, w_proj):
    bsz, seq, _ = v.shape
    u = jax.nn.gelu(u)
    v = jax.nn.gelu(v)
    vh = rms_norm(v.reshape(bsz, seq, SGU_HEADS, SGU_HEAD_DIM), norm_w.reshape(SGU_HEADS, SGU_HEAD_DIM))
    vc = vh.reshape(bsz, seq // SGU_CHUNK, SGU_CHUNK, SGU_HEADS, SGU_HEAD_DIM)
    mask = jnp.tril(jnp.ones((SGU_CHUNK, SGU_CHUNK), dtype=bool))
    ws = jnp.where(mask[None], w_s, jnp.zeros_like(w_s))
    s = jnp.einsum('hts,bcshd->bcthd', ws, vc) + b_s.T[None, None, :, :, None]
    s = s.reshape(bsz, seq, SGU_WIDTH)
    return (u * s) @ w_proj

def hier_moe(xn, w_rg, b_rg, w_re, b_re, w_gate, w_up, w_down):
    bsz, seq, d = xn.shape
    n_tok = bsz * seq
    xt = xn.reshape(n_tok, d)
    gl = (xt @ w_rg + b_rg).astype(jnp.float32)
    gp = jax.nn.softmax(gl, axis=-1)
    g = jnp.argmax(gl, axis=-1)
    g_w = jnp.take_along_axis(gp, g[:, None], axis=1)[:, 0]
    el = (xt @ w_re + b_re).astype(jnp.float32).reshape(n_tok, N_GROUPS, EXPERTS_PER_GROUP)
    el_g = jnp.take_along_axis(el, g[:, None, None], axis=1)[:, 0]
    top_v, top_i = lax.top_k(el_g, TOP_K)
    w = jax.nn.softmax(top_v, axis=-1) * g_w[:, None]
    eid = (g[:, None] * EXPERTS_PER_GROUP + top_i).reshape(-1).astype(jnp.int32)
    wts = w.reshape(-1)
    tok = jnp.repeat(jnp.arange(n_tok, dtype=jnp.int32), TOP_K)
    n_assign = n_tok * TOP_K
    counts = jax.ops.segment_sum(jnp.ones((n_assign,), jnp.int32), eid, num_segments=N_EXPERTS)
    padded = ((counts + MOE_BLOCK - 1) // MOE_BLOCK) * MOE_BLOCK
    pad_end = jnp.cumsum(padded)
    pad_start = pad_end - padded
    raw_start = jnp.cumsum(counts) - counts
    order = jnp.argsort(eid)
    se = eid[order]
    dest = pad_start[se] + jnp.arange(n_assign, dtype=jnp.int32) - raw_start[se]
    n_rows = (-(-n_assign // MOE_BLOCK)) * MOE_BLOCK + N_EXPERTS * MOE_BLOCK
    n_blocks = n_rows // MOE_BLOCK
    row_tok = jnp.zeros((n_rows,), jnp.int32).at[dest].set(tok[order])
    row_w = jnp.zeros((n_rows,), wts.dtype).at[dest].set(wts[order])
    blk_e = jnp.minimum(jnp.searchsorted(pad_end, jnp.arange(n_blocks, dtype=jnp.int32) * MOE_BLOCK, side='right'),
                        N_EXPERTS - 1).astype(jnp.int32)
    xr = xt[row_tok].reshape(n_blocks, MOE_BLOCK, d)

    def expert_block(args):
        xb, e = args
        hid = jax.nn.silu(xb @ w_gate[e]) * (xb @ w_up[e])
        return hid @ w_down[e]

    yr = lax.map(expert_block, (xr, blk_e)).reshape(n_rows, d)
    y = jax.ops.segment_sum(yr * row_w[:, None].astype(yr.dtype), row_tok, num_segments=n_tok)
    return y.reshape(bsz, seq, d)

def setup_inputs(seed: int = 0) -> dict:
    key = jax.random.key(seed)
    ks = jax.random.split(key, 32)
    f32 = jnp.float32
    nrm = lambda k, shape, s: jax.random.normal(k, shape, f32) * s
    L = DEPTH
    n_idx = jnp.arange(S5_STATE, dtype=f32)
    inp = {}
    inp["x"] = nrm(ks[0], (BATCH, SEQ, D_MODEL), 1.0)
    inp["p"] = nrm(ks[1], (DEPTH, BATCH, SEQ, PLE_DIM), 1.0)
    inp["norm_mix"] = 1.0 + nrm(ks[2], (L, D_MODEL), 0.05)
    inp["w_in"] = nrm(ks[3], (L, D_MODEL, IN_COLS), D_MODEL ** -0.5)
    inp["s5_a_re"] = -0.5 + nrm(ks[4], (L, S5_GROUPS, S5_STATE), 0.01)
    inp["s5_a_im"] = math.pi * n_idx[None, None, :] + nrm(ks[5], (L, S5_GROUPS, S5_STATE), 0.01)
    inp["s5_log_dt"] = jax.random.uniform(ks[6], (L, S5_GROUPS), f32, math.log(1e-3), math.log(1e-1))
    inp["s5_b_re"] = nrm(ks[7], (L, S5_GROUPS, S5_STATE, S5_GROUP), (2 * S5_GROUP) ** -0.5)
    inp["s5_b_im"] = nrm(ks[8], (L, S5_GROUPS, S5_STATE, S5_GROUP), (2 * S5_GROUP) ** -0.5)
    inp["s5_c_re"] = nrm(ks[9], (L, S5_GROUPS, S5_GROUP, S5_STATE), (2 * S5_STATE) ** -0.5 * 4.0)
    inp["s5_c_im"] = nrm(ks[10], (L, S5_GROUPS, S5_GROUP, S5_STATE), (2 * S5_STATE) ** -0.5 * 4.0)
    inp["s5_d"] = nrm(ks[11], (L, S5_WIDTH), 1.0)
    inp["w_glu"] = nrm(ks[12], (L, S5_WIDTH, 2 * D_MODEL), S5_WIDTH ** -0.5)
    inp["sgu_norm"] = 1.0 + nrm(ks[13], (L, SGU_WIDTH), 0.05)
    inp["sgu_w"] = nrm(ks[14], (L, SGU_HEADS, SGU_CHUNK, SGU_CHUNK), SGU_CHUNK ** -0.5)
    inp["sgu_b"] = 1.0 + nrm(ks[15], (L, SGU_HEADS, SGU_CHUNK), 0.1)
    inp["w_sgu_proj"] = nrm(ks[16], (L, SGU_WIDTH, D_MODEL), SGU_WIDTH ** -0.5)
    inp["w_out"] = nrm(ks[17], (L, D_MODEL, D_MODEL), D_MODEL ** -0.5)
    inp["norm_ffn"] = 1.0 + nrm(ks[18], (L, D_MODEL), 0.05)
    inp["w_router_group"] = nrm(ks[19], (L, D_MODEL, N_GROUPS), D_MODEL ** -0.5)
    inp["b_router_group"] = nrm(ks[20], (L, N_GROUPS), 0.01)
    inp["w_router_expert"] = nrm(ks[21], (L, D_MODEL, N_EXPERTS), D_MODEL ** -0.5)
    inp["b_router_expert"] = nrm(ks[22], (L, N_EXPERTS), 0.01)
    inp["w_expert_gate"] = nrm(ks[23], (L, N_EXPERTS, D_MODEL, D_EXPERT), D_MODEL ** -0.5)
    inp["w_expert_up"] = nrm(ks[24], (L, N_EXPERTS, D_MODEL, D_EXPERT), D_MODEL ** -0.5)
    inp["w_expert_down"] = nrm(ks[25], (L, N_EXPERTS, D_EXPERT, D_MODEL), D_EXPERT ** -0.5)
    inp["norm_ple"] = 1.0 + nrm(ks[26], (L, D_MODEL), 0.05)
    inp["w_ple_gate"] = nrm(ks[27], (L, D_MODEL, D_MODEL), D_MODEL ** -0.5)
    inp["w_ple_proj"] = nrm(ks[28], (L, PLE_DIM, D_MODEL), PLE_DIM ** -0.5)
    inp["norm_final"] = 1.0 + nrm(ks[29], (D_MODEL,), 0.05)
    return inp

def reference(x, p, norm_mix, w_in, s5_a_re, s5_a_im, s5_log_dt, s5_b_re, s5_b_im, s5_c_re, s5_c_im,
              s5_d, w_glu, sgu_norm, sgu_w, sgu_b, w_sgu_proj, w_out, norm_ffn, w_router_group,
              b_router_group, w_router_expert, b_router_expert, w_expert_gate, w_expert_up,
              w_expert_down, norm_ple, w_ple_gate, w_ple_proj, norm_final):
    h = x
    split_at = [S5_WIDTH, S5_WIDTH + SGU_WIDTH, S5_WIDTH + 2 * SGU_WIDTH, S5_WIDTH + 2 * SGU_WIDTH + D_MODEL]
    for i in range(DEPTH):
        xn = rms_norm(h, norm_mix[i])
        proj = xn @ w_in[i]
        x_s5, u_sgu, v_sgu, g_s5, g_sgu = jnp.split(proj, split_at, axis=-1)
        out_a = s5_branch(x_s5, s5_a_re[i], s5_a_im[i], s5_log_dt[i], s5_b_re[i], s5_b_im[i],
                          s5_c_re[i], s5_c_im[i], s5_d[i], w_glu[i])
        out_b = sgu_branch(u_sgu, v_sgu, sgu_norm[i], sgu_w[i], sgu_b[i], w_sgu_proj[i])
        merged = jax.nn.sigmoid(g_s5) * out_a + jax.nn.sigmoid(g_sgu) * out_b
        h = h + merged @ w_out[i]
        h = h + hier_moe(rms_norm(h, norm_ffn[i]), w_router_group[i], b_router_group[i],
                         w_router_expert[i], b_router_expert[i], w_expert_gate[i],
                         w_expert_up[i], w_expert_down[i])
        gate = jax.nn.sigmoid(rms_norm(h, norm_ple[i]) @ w_ple_gate[i])
        h = h + (p[i] @ w_ple_proj[i]) * gate
    return rms_norm(h, norm_final)


_drawn_inputs = setup_inputs


def setup_inputs(seed=0):
    import zlib

    import numpy as np

    out = dict(_drawn_inputs(seed))
    spreads = {}
    factors = {'s5_a_re': 6.01, 'b_router_group': 4.52, 'b_router_expert': 4.762, 'norm_ple': 6.665}
    for name, (base, spread) in spreads.items():
        noise = np.random.default_rng([zlib.crc32(name.encode()), seed]).standard_normal(out[name].shape)
        drawn = base * np.exp(spread * noise) if base else spread * noise
        out[name] = __import__('jax').numpy.asarray(drawn.astype(out[name].dtype))
    for name, factor in factors.items():
        out[name] = (out[name] * factor).astype(out[name].dtype)
    return out
```

```python
import math
from contextlib import ExitStack

import concourse.bass as bass
from concourse import mybir
from concourse.alu_op_type import AluOpType as ALU

F32, F32R, I32, U32 = mybir.dt.float32, mybir.dt.float32r, mybir.dt.int32, mybir.dt.uint32
ACT = mybir.ActivationFunctionType
AX = mybir.AxisListType

P = 128
D = 1024
KD = D // P
SEQ = 1024
NT = SEQ // P
HALF = 512
S5W, GROUPS, GC, NS = 512, 32, 16, 64
PAIRS = GROUPS // 2
FT = S5W // P
HEADS = 4
SC = P // NT
EXPERTS, NGRP, EPG, FE = 32, 4, 8, 512
KF = FE // P
BLK = 128
OVER = 2 * SEQ // BLK - 1
NBLK = EXPERTS + OVER
PLE = 256
KP = PLE // P
EPS = 1e-6
MAGIC = 12582912.0
LN2HI, LN2LO = 0.693359375, -2.12194440e-4
PI2A, PI2B, PI2C = 6.28125, 1.9350051879882812e-3, 3.0199159819e-7
GELU_A, GELU_B = 0.044715, 2.0 * math.sqrt(2.0 / math.pi)


class Counted:

    def __init__(self, eng, sem):
        self.eng, self.sem, self.base, self.n = eng, sem, 0, 0

    def did(self, ins):
        self.n += 1
        return ins.then_inc(self.sem, 1)

    def settle(self):
        self.eng.wait_ge(self.sem, self.base + self.n)

    def loop_body(self, i, per):
        self.start, self.base, self.n, self.per = self.base + self.n, self.base + self.n + i * per, 0, per

    def loop_end(self, turns):
        assert self.n == self.per, (self.n, self.per)
        self.base, self.n = self.start + turns * self.per, 0


class Map:

    def __init__(self, nc):
        self.nc, self.sems = nc, []
        self.origin = (nc.sbuf_base + 31) // 32 * 32

    def at(self, name, shape, kib, dt=F32):
        return self.nc.alloc_sbuf_tensor_at(name, shape, dt, offset=self.origin + int(kib * 1024))

    def sem(self, name):
        self.sems.append(self.nc.alloc_semaphore(name))
        return self.sems[-1]

    def reuse_semaphores(self):
        self.nc.clear_and_free_semaphores(self.sems)
        self.nc.all_engine_barrier()
        self.sems = []


def bc(ap, shape):
    return ap.to_broadcast(shape)


def tile_pair_loop(eng, first, second, counted=None, per=0):
    first(0, 0)
    with eng.Fori(0, NT // 2 - 1) as i:
        if counted:
            counted.loop_body(i, per)
        first(i * 2 + 1, 1)
        second(i * 2, 0)
        first(i * 2 + 2, 0)
        second(i * 2 + 1, 1)
    if counted:
        counted.loop_end(NT // 2 - 1)
    first(NT - 1, 1)
    second(NT - 2, 0)
    second(NT - 1, 1)


def complex_product(eng, step, out_re, out_im, a_re, a_im, b_re, b_im, tmp0, tmp1):
    step.did(eng.tensor_tensor(tmp0, a_re, b_re, ALU.mult))
    step.did(eng.tensor_tensor(tmp1, a_im, b_im, ALU.mult))
    step.settle()
    step.did(eng.tensor_tensor(out_re, tmp0, tmp1, ALU.subtract))
    step.settle()
    step.did(eng.tensor_tensor(tmp0, a_re, b_im, ALU.mult))
    step.did(eng.tensor_tensor(tmp1, a_im, b_re, ALU.mult))
    step.settle()
    step.did(eng.tensor_tensor(out_im, tmp0, tmp1, ALU.add))
    step.settle()


def unit_length(eng, step, c, s, tmp0, tmp1):
    step.did(eng.tensor_tensor(tmp0, c, c, ALU.mult))
    step.did(eng.tensor_tensor(tmp1, s, s, ALU.mult))
    step.settle()
    step.did(eng.tensor_tensor(tmp0, tmp0, tmp1, ALU.add))
    step.settle()
    step.did(eng.tensor_scalar(tmp0, tmp0, -0.5, 1.5, ALU.mult, ALU.add))
    step.settle()
    step.did(eng.tensor_tensor(c, c, tmp0, ALU.mult))
    step.did(eng.tensor_tensor(s, s, tmp0, ALU.mult))
    step.settle()


def exponential(vec, step, out, x, t0, t1, t2, whole):
    def op(ins):
        step.did(ins)
        step.settle()
    op(vec.tensor_scalar(t0, x, -87.0, 88.0, ALU.max, ALU.min))
    op(vec.tensor_scalar(t1, t0, 1.0 / math.log(2.0), MAGIC, ALU.mult, ALU.add))
    op(vec.tensor_scalar(t1, t1, MAGIC, None, ALU.subtract))
    op(vec.scalar_tensor_tensor(t0, t1, -LN2HI, t0, ALU.mult, ALU.add))
    op(vec.scalar_tensor_tensor(t0, t1, -LN2LO, t0, ALU.mult, ALU.add))
    op(vec.tensor_scalar(t2, t0, 1.0 / math.factorial(7), None, ALU.mult))
    for k in range(6, 0, -1):
        op(vec.scalar_tensor_tensor(t2, t2, 1.0 / math.factorial(k), t0, ALU.add, ALU.mult))
    op(vec.tensor_scalar(t2, t2, 1.0, None, ALU.add))
    op(vec.tensor_scalar(whole, t1, 127.0, None, ALU.add))
    op(vec.tensor_scalar(whole, whole, 23, None, ALU.logical_shift_left))
    op(vec.tensor_tensor(out, t2, whole.bitcast(F32), ALU.mult))


def setup_block(nc, m, ins, dr):
    at, sem = m.at, m.sem
    xn_hi = at("xn_hi", [P, KD, SEQ], 0, F32R)
    xn_lo = at("xn_lo", [P, KD, SEQ], 32, F32R)
    e_re = at("e_re", [P, PAIRS, P], 64)
    e_im = at("e_im", [P, PAIRS, P], 72)
    o_re = at("o_re", [P, PAIRS, 9, GC], 80)
    o_im = at("o_im", [P, PAIRS, 9, GC], 89)
    w_re = at("w_re", [P, PAIRS, P], 98)
    w_im = at("w_im", [P, PAIRS, P], 106)
    ident = at("ident", [P, P], 207.25)
    mag8 = at("mag8", [P, PAIRS], 196.5)
    kpad = at("kpad", [GC, GROUPS, 15 * GC], 114)
    x = at("x_rows", [P, NT, D], 146)
    t9a = at("t9a", [P, PAIRS * 9 * GC], 178)
    t9b = at("t9b", [P, PAIRS * 9 * GC], 187)
    par = at("par", [P, P], 196.75)
    ldt = at("ldt", [P, 2], 197.25)
    par_t = at("par_t", [P, 96], 197.5)
    small = at("small", [P, 24, PAIRS], 198)
    whole = at("whole", [P, PAIRS], 199.5, I32)
    pw_re = at("pw_re", [P, PAIRS, 9], 200)
    pw_im = at("pw_im", [P, PAIRS, 9], 200.75)
    b_re = at("b_re", [P, PAIRS, GC], 201.5)
    b_im = at("b_im", [P, PAIRS, GC], 202.5)
    bb_re = at("bb_re", [P, PAIRS, GC], 203.5)
    bb_im = at("bb_im", [P, PAIRS, GC], 204.5)
    c_re = at("c_re", [P, PAIRS, GC], 205.5)
    ssq = at("ssq", [P, NT], 206.75)
    rstd = at("rstd", [P, NT], 206.875)
    gmix = at("gmix", [P, KD], 207)
    c_im = at("c_im", [P, PAIRS, GC], 144)
    zk = at("zk", [P, 4, PAIRS], 145)
    craw = at("craw", [P, 2, FT, 2, NS], 114)
    wt0 = at("wt0", [P, PAIRS, 64], 146)
    wt1 = at("wt1", [P, PAIRS, 64], 150)

    s_const, s_par, s_b, s_c, s_x, s_g = (sem(f"a_{n}") for n in ("const", "par", "b", "c", "x", "g"))
    v_step, g_step, a_step = sem("a_v_step"), sem("a_g_step"), sem("a_a_step")
    s_cleared, s_par_in, s_par_t = sem("a_cleared"), sem("a_par_in"), sem("a_par_t")
    s_ct, s_phase, s_sin, s_ang = sem("a_ct"), sem("a_phase"), sem("a_sin"), sem("a_ang")
    s_e_made, s_et, s_et_copied = sem("a_e_made"), sem("a_et"), sem("a_et_copied")
    s_k_ready, s_k, s_k_copied, s_kd = sem("a_k_ready"), sem("a_k"), sem("a_k_copied"), sem("a_kd")
    s_sq, s_inv, s_xs, s_xt, s_hi, s_lo, s_zero = (sem(f"a_{n}") for n in ("sq", "inv", "xs", "xt", "hi", "lo", "zero"))

    with ExitStack() as local:
        ps = local.enter_context(nc.psum_tensor("a_ps", [P, 8, HALF], F32))
        block = local.enter_context(nc.Block())

        @block.sync
        def _(sp):
            xv = ins["x"][0].rearrange("(c p) d -> p c d", p=NT)
            for p in range(NT):
                sp.dma_start(x[:, p, :], xv[p]).then_inc(s_x, 16)
            sp.wait_ge(s_k_copied, GROUPS // 4)
            sp.dma_start(dr["kpad"], kpad[:, :, :]).then_inc(s_kd, 16)
            sp.wait_ge(s_kd, 16)

        @block.gpsimd
        def _(gp):
            step = Counted(gp, g_step)
            gp.memset(par[:, :], 0.0).then_inc(s_cleared, 1)
            step.did(gp.memset(ident[:, :], 0.0))
            step.settle()
            gp.affine_select(out=ident[:, :], in_=ident[:, :], compare_op=ALU.not_equal, fill=1.0, base=0,
                             pattern=[[-1, P]], channel_multiplier=1).then_inc(s_const, 1)
            step.did(gp.memset(w_re[:, :, 0:1], 1.0))
            step.did(gp.memset(w_im[:, :, 0:1], 0.0))
            step.settle()
            gp.wait_ge(s_phase, 1)
            gp.wait_ge(s_xt, 2 * KD)
            zr, zi, z2r, z2i = zk[:, 0, :], zk[:, 1, :], zk[:, 2, :], zk[:, 3, :]
            n = 1
            while n < P:
                shape = [P, PAIRS, n]
                complex_product(gp, step, w_re[:, :, n:2 * n], w_im[:, :, n:2 * n],
                                w_re[:, :, 0:n], w_im[:, :, 0:n],
                                bc(zr.unsqueeze(2), shape), bc(zi.unsqueeze(2), shape),
                                wt0[:, :, 0:n], wt1[:, :, 0:n])
                if 2 * n < P:
                    complex_product(gp, step, z2r, z2i, zr, zi, zr, zi, wt0[:, :, 0], wt1[:, :, 0])
                    unit_length(gp, step, z2r, z2i, wt0[:, :, 0], wt1[:, :, 0])
                    zr, zi, z2r, z2i = z2r, z2i, zr, zi
                n *= 2
            step.settle()

        @block.scalar
        def _(act):
            step = Counted(act, a_step)
            act.wait_ge(s_cleared, 1)
            pair_rows = lambda a: a[0].rearrange("(q h) n -> q (h n)", h=2)
            act.dma_start(par[0:16, :], pair_rows(ins["s5_a_re"])).then_inc(s_par, 16)
            act.dma_start(par[32:48, :], pair_rows(ins["s5_a_im"])).then_inc(s_par, 16)
            act.dma_start(ldt[64:80, :], ins["s5_log_dt"][0].rearrange("(q h) -> q h", h=2)).then_inc(s_par, 16)
            for i, name in enumerate(("s5_c_re", "s5_c_im")):
                for h in range(2):
                    act.dma_start(craw[:, i, :, h, :],
                                  ins[name][0].rearrange("(f g) c n -> (g c) f n", f=FT)).then_inc(s_c, 16)
            with nc.allow_non_contiguous_dma(reason="short vectors, channels across partitions"):
                act.dma_start(gmix[:, :], ins["norm_mix"][0].rearrange("(k p) -> p k", p=P)).then_inc(s_g, 16)
            act.dma_start(b_re[:, :, :], ins["s5_b_re"][0].rearrange("(q h) n c -> (h n) q c", h=2)).then_inc(s_b, 16)
            act.dma_start(b_im[:, :, :], ins["s5_b_im"][0].rearrange("(q h) n c -> (h n) q c", h=2)).then_inc(s_b, 16)
            for p in range(NT):
                if p == 0:
                    act.wait_ge(s_x, 16 * NT)
                step.did(act.activation(t9a[:, 0:D], x[:, p, :], ACT.Square, accum_out=ssq[:, p:p + 1]))
                step.settle()
            act.nop().then_inc(s_sq, 1)
            act.wait_ge(s_inv, 1)
            step.did(act.activation(rstd[:, :], rstd[:, :], ACT.Sqrt))
            step.settle()
            for p in range(NT):
                act.activation(x[:, p, :], x[:, p, :], ACT.Copy, scale=rstd[:, p:p + 1]).then_inc(s_xs, 1)
            act.wait_ge(s_g, 16)
            for n in range(2 * KD):
                k, half = n // 2, n % 2
                act.wait_ge(s_xt, n + 1)
                act.activation(xn_hi[:, k, half * HALF:(half + 1) * HALF], ps[:, n % 4, :], ACT.Copy,
                               scale=gmix[:, k:k + 1]).then_inc(s_hi, 1)
            act.wait_ge(s_ang, 1)
            step.did(act.activation(small[:, 2, :], small[:, 0, :], ACT.Sin))
            step.did(act.activation(small[:, 3, :], small[:, 1, :], ACT.Sin))
            step.settle()
            act.nop().then_inc(s_sin, 1)

        @block.vector
        def _(vec):
            step = Counted(vec, v_step)

            def op(instruction):
                step.did(instruction)
                step.settle()

            tt, ts, stt = vec.tensor_tensor, vec.tensor_scalar, vec.scalar_tensor_tensor
            s = lambda i: small[:, i, :]
            vec.wait_ge(s_par, 48)
            op(vec.tensor_copy(par[64:80, :].rearrange("q (h n) -> q h n", h=2),
                               bc(ldt[64:80, :].unsqueeze(2), [16, 2, NS])))
            vec.nop().then_inc(s_par_in, 1)
            vec.wait_ge(s_par_t, 1)
            op(vec.tensor_copy(par_t[:, :], ps[:, 7, 0:96]))
            are, aim, ldt_t = par_t[:, 0:16], par_t[:, 32:48], par_t[:, 64:80]
            dt, mag, ang = s(4), s(5), s(6)
            exponential(vec, step, dt, ldt_t, s(10), s(11), s(12), whole[:, :])
            op(tt(s(13), are, dt, ALU.mult))
            exponential(vec, step, mag, s(13), s(10), s(11), s(12), whole[:, :])
            op(tt(ang, aim, dt, ALU.mult))
            op(ts(s(10), ang, 1.0 / (2.0 * math.pi), MAGIC, ALU.mult, ALU.add))
            op(ts(s(10), s(10), MAGIC, None, ALU.subtract))
            op(stt(s(0), s(10), -PI2A, ang, ALU.mult, ALU.add))
            op(stt(s(0), s(10), -PI2B, s(0), ALU.mult, ALU.add))
            op(stt(s(0), s(10), -PI2C, s(0), ALU.mult, ALU.add))
            op(ts(s(0), s(0), 3.1415925, -3.1415925, ALU.min, ALU.max))
            op(ts(s(1), s(0), 0.5, None, ALU.mult))
            vec.nop().then_inc(s_ang, 1)
            vec.wait_ge(s_sq, 1)
            op(ts(rstd[:, :], ssq[:, :], 1.0 / D, EPS, ALU.mult, ALU.add))
            vec.reciprocal(rstd[:, :], rstd[:, :]).then_inc(s_inv, 1)
            vec.wait_ge(s_ct, 1)
            for i, c in enumerate((c_re, c_im)):
                for h in range(2):
                    src = ps[64 * h:64 * h + 64, 5 + i, :].rearrange("n (q h c) -> n q h c", h=2, c=GC)[:, :, h, :]
                    op(vec.tensor_copy(c[64 * h:64 * h + 64, :, :], src))
            for n in range(2 * KD):
                k, half = n // 2, n % 2
                col = slice(half * HALF, (half + 1) * HALF)
                vec.wait_ge(s_hi, n + 1)
                stt(xn_lo[:, k, col], ps[:, n % 4, :], gmix[:, k:k + 1], xn_hi[:, k, col].bitcast(F32),
                    ALU.mult, ALU.subtract).then_inc(s_lo, 1)
            vec.wait_ge(s_sin, 1)
            cs, sn = s(7), s(2)
            op(tt(s(10), s(3), s(3), ALU.mult))
            op(ts(cs, s(10), -2.0, 1.0, ALU.mult, ALU.add))
            unit_length(vec, step, cs, sn, s(10), s(11))
            op(vec.memset(pw_re[:, :, 0:1], 1.0))
            op(vec.memset(pw_im[:, :, 0:1], 0.0))
            lb_re, lb_im = pw_re[:, :, 1], pw_im[:, :, 1]
            op(tt(lb_re, mag, cs, ALU.mult))
            op(tt(lb_im, mag, sn, ALU.mult))
            src_r, src_i = cs, sn
            for i, (dst_r, dst_i) in enumerate(((s(14), s(15)), (s(16), s(17)), (zk[:, 0, :], zk[:, 1, :]))):
                complex_product(vec, step, dst_r, dst_i, src_r, src_i, src_r, src_i, s(10), s(11))
                src_r, src_i = dst_r, dst_i
                op(tt(mag8[:, :], mag if i == 0 else mag8[:, :], mag if i == 0 else mag8[:, :], ALU.mult))
            unit_length(vec, step, src_r, src_i, s(10), s(11))
            vec.nop().then_inc(s_phase, 1)
            for n in (1, 2, 4):
                shape = [P, PAIRS, n]
                complex_product(vec, step, pw_re[:, :, n + 1:2 * n + 1], pw_im[:, :, n + 1:2 * n + 1],
                                pw_re[:, :, 1:n + 1], pw_im[:, :, 1:n + 1],
                                bc(pw_re[:, :, n:n + 1], shape), bc(pw_im[:, :, n:n + 1], shape),
                                t9a[:, 0:PAIRS * n].rearrange("p (q n) -> p q n", n=n),
                                t9b[:, 0:PAIRS * n].rearrange("p (q n) -> p q n", n=n))
            op(ts(s(8), lb_re, -1.0, None, ALU.add))
            op(tt(s(10), are, are, ALU.mult))
            op(tt(s(11), aim, aim, ALU.mult))
            op(tt(s(10), s(10), s(11), ALU.add))
            op(vec.reciprocal(s(9), s(10)))
            op(tt(s(10), s(8), are, ALU.mult))
            op(tt(s(11), lb_im, aim, ALU.mult))
            op(tt(s(10), s(10), s(11), ALU.add))
            op(tt(s(18), s(10), s(9), ALU.mult))
            op(tt(s(10), lb_im, are, ALU.mult))
            op(tt(s(11), s(8), aim, ALU.mult))
            op(tt(s(10), s(10), s(11), ALU.subtract))
            op(tt(s(19), s(10), s(9), ALU.mult))
            vec.wait_ge(s_b, 32)
            shape = [P, PAIRS, GC]
            view = lambda t: t[:, 0:PAIRS * GC].rearrange("p (q c) -> p q c", c=GC)
            complex_product(vec, step, bb_re[:, :, :], bb_im[:, :, :], b_re[:, :, :], b_im[:, :, :],
                            bc(s(18).unsqueeze(2), shape), bc(s(19).unsqueeze(2), shape), view(t9a), view(t9b))
            shape = [P, PAIRS, 9, GC]
            pr, pi = bc(pw_re[:, :, :].unsqueeze(3), shape), bc(pw_im[:, :, :].unsqueeze(3), shape)
            cr, ci = bc(c_re[:, :, :].unsqueeze(2), shape), bc(c_im[:, :, :].unsqueeze(2), shape)
            view = lambda t: t[:, :].rearrange("p (q k c) -> p q k c", k=9, c=GC)
            complex_product(vec, step, o_re[:, :, :, :], o_im[:, :, :, :], pr, pi, cr, ci, view(t9a), view(t9b))
            op(ts(o_im[:, :, :, :], o_im[:, :, :, :], -1.0, None, ALU.mult))
            vec.nop().then_inc(s_k_ready, 1)
            shape = [P, PAIRS, NT, GC]
            pr, pi = (bc(w[:, :, 0:NT].unsqueeze(3), shape) for w in (pw_re, pw_im))
            br, bi = bc(bb_re[:, :, :].unsqueeze(2), shape), bc(bb_im[:, :, :].unsqueeze(2), shape)
            view = lambda t: t[:, 0:PAIRS * P].rearrange("p (q k c) -> p q k c", k=NT, c=GC)
            e4 = lambda t: t[:, :, :].rearrange("p q (k c) -> p q k c", c=GC)
            complex_product(vec, step, e4(e_re), e4(e_im), pr, pi, br, bi, view(t9a), view(t9b))
            vec.nop().then_inc(s_e_made, 1)
            op(vec.memset(kpad[:, :, 0:7 * GC], 0.0))
            kpad_v = kpad[:, :, :].rearrange("c (q h) w -> c q h w", h=2)
            for n in range(GROUPS // 4):
                a, h = n // 2, n % 2
                vec.wait_ge(s_k, n + 1)
                vec.tensor_copy(kpad_v[:, 4 * a:4 * a + 4, h, 7 * GC:],
                                ps[0:GC, 4 + n % 2, :].rearrange("c (g w) -> c g w", g=4)).then_inc(s_k_copied, 1)
            for n in range(2 * PAIRS // 4):
                vec.wait_ge(s_et, n + 1)
                e = (e_re, e_im)[n // (PAIRS // 4)]
                q = n % (PAIRS // 4) * 4
                vec.tensor_copy(e[:, q:q + 4, :], ps[:, n % 2, :].rearrange("p (q c) -> p q c", q=4)).then_inc(s_et_copied, 1)

        @block.tensor
        def _(pe):
            pe.wait_ge(s_const, 1)
            pe.wait_ge(s_par_in, 1)
            pe.transpose(ps[:, 7, 0:96], par[0:96, :], ident[0:96, 0:96]).then_inc(s_par_t, 1)
            pe.wait_ge(s_c, 64)
            for i in range(2):
                for f in range(FT):
                    last = pe.transpose(ps[:, 5 + i, f * P:(f + 1) * P],
                                        craw[:, i, f, :, :].rearrange("p h n -> p (h n)"), ident[:, :])
            last.then_inc(s_ct, 1)
            pe.wait_ge(s_xs, NT)
            for n in range(2 * KD):
                k, half = n // 2, n % 2
                if n >= 4:
                    pe.wait_ge(s_lo, n - 3)
                for j in range(4):
                    last = pe.transpose(ps[:, n % 4, j * P:(j + 1) * P],
                                        x[:, half * 4 + j, k * P:(k + 1) * P], ident[:, :])
                last.then_inc(s_xt, 1)
            pe.wait_ge(s_k_ready, 1)
            for n in range(GROUPS // 4):
                h = n % 2
                if n >= 2:
                    pe.wait_ge(s_k_copied, n - 1)
                for j in range(4):
                    q, rows = n // 2 * 4 + j, slice(64 * h, 64 * h + 64)
                    dst = ps[0:GC, 4 + n % 2, j * P:(j + 1) * P]
                    taps = [o[rows, q, 0:NT, :].rearrange("p k c -> p (k c)") for o in (o_re, o_im)]
                    pe.matmul(dst, bb_re[rows, q, :], taps[0], start=True, stop=False)
                    last = pe.matmul(dst, bb_im[rows, q, :], taps[1], start=False, stop=True)
                last.then_inc(s_k, 1)
            pe.wait_ge(s_e_made, 1)
            pe.wait_ge(s_lo, 2 * KD)
            for n in range(2 * PAIRS // 4):
                e = (e_re, e_im)[n // (PAIRS // 4)]
                if n >= 2:
                    pe.wait_ge(s_et_copied, n - 1)
                for j in range(4):
                    last = pe.transpose(ps[:, n % 2, j * P:(j + 1) * P], e[:, n % (PAIRS // 4) * 4 + j, :], ident[:, :])
                last.then_inc(s_et, 1)
    return dict(xn_hi=xn_hi, xn_lo=xn_lo, e_re=e_re, e_im=e_im, o_re=o_re, o_im=o_im, w_re=w_re, w_im=w_im,
                ident=ident, mag8=mag8)




def project_block(nc, m, ins, dr, t):
    at, sem = m.at, m.sem
    xn_hi, xn_lo, w_re, w_im, mag8 = t["xn_hi"], t["xn_lo"], t["w_re"], t["w_im"], t["mag8"]
    e_re, e_im, o_re, o_im = t["e_re"], t["e_im"], t["o_re"], t["o_im"]
    toep = at("toep", [P, GROUPS, P], 64)
    u = at("s5_in", [P, GROUPS, P], 114)
    h_re = at("h_re", [P, PAIRS, P], 130)
    h_im = at("h_im", [P, PAIRS, P], 138)
    raw = at("p_raw", [P, 2, KD, P], 146)
    w_hi = at("p_w_hi", [P, 2, KD, P], 154, F32R)
    w_lo = at("p_w_lo", [P, 2, KD, P], 162, F32R)
    out = at("p_out", [P, 2, SEQ], 170)
    tmp = at("p_tmp", [P, 4, 4, P], 178)
    zero = at("zero_rows", [P, D], 186)
    s_raw, s_stored = [sem(f"b_raw{s}") for s in range(2)], [sem(f"b_stored{s}") for s in range(2)]
    s_hi, s_split, s_acc, s_acc_free = (sem(f"b_{n}") for n in ("hi", "split", "acc", "acc_free"))
    s_zero, s_zeroed = sem("b_zero"), sem("b_zeroed")
    s_u, s_e, s_e_read, s_toep, s_h, s_y, s_y_out, s_ysc, v_step = \
        (sem(f"b_{n}") for n in ("u", "e", "e_read", "toep", "h", "y", "y_out", "ysc", "v_step"))
    TURNS = 3 * S5W // (2 * P)
    w_v = ins["w_in"][0].rearrange("(k p) c -> p k c", p=P)
    quad = lambda tile, a: tile[:, 4 * a:4 * a + 4, :]

    with ExitStack() as local:
        ps = local.enter_context(nc.psum_tensor("b_ps", [P, 8, HALF], F32))
        block = local.enter_context(nc.Block())

        @block.sync
        def _(sp):
            def load(n, s):
                sp.dma_start(raw[:, s, :, :], w_v[:, :, bass.ds(n * P, P)]).then_inc(s_raw[s], 16)

            def load_turns(first, end):
                with sp.Fori(first, end) as i:
                    for s in range(2):
                        sp.wait_ge(s_split, i * 2 + (s - 1))
                        load(i * 2 + s, s)

            load(0, 0)
            load(1, 1)
            load_turns(1, 4)
            sp.wait_ge(s_zero, 1)
            sp.dma_start(dr["yr"][EXPERTS * BLK:, :].rearrange("(b p) d -> p b d", p=P),
                         bc(zero[:, :].unsqueeze(1), [P, OVER, D])).then_inc(s_zeroed, 16)
            for s in range(2):
                sp.wait_ge(s_stored[s], 16 * (1 + 2))
            xs = dr["proj"][0:S5W, :].rearrange("(g c) (p k) -> p c g k", c=GC, p=NT)
            for p in range(NT):
                sp.dma_start(u[(NT - 1 - p) * GC:(NT - p) * GC, :, :], xs[p]).then_inc(s_u, 16)
            load_turns(4, TURNS)
            sp.wait_ge(s_e, PAIRS // 4)
            for k in range(NT):
                sp.dma_start(toep[k * GC:(k + 1) * GC, :, :], dr["kpad"][:, :, k * GC:k * GC + P]).then_inc(s_toep, 16)
            sp.wait_ge(s_y_out, GROUPS // 4)
            ys = dr["y"].rearrange("(g c) (p k) -> p c g k", c=GC, p=NT)
            for p in range(NT):
                sp.dma_start(ys[p], u[p * GC:(p + 1) * GC, :, :]).then_inc(s_ysc, 16)
            sp.wait_ge(s_ysc, 16 * NT)
            sp.wait_ge(s_zeroed, 16)
            for s in range(2):
                sp.wait_ge(s_stored[s], 16 * (1 + TURNS))

        @block.gpsimd
        def _(gp):
            gp.memset(zero[:, :], 0.0).then_inc(s_zero, 1)
            with gp.Fori(0, TURNS) as i:
                for s in range(2):
                    gp.wait_ge(s_hi, i * 2 + (s + 1))
                    gp.tensor_tensor(w_lo[:, s, :, :], raw[:, s, :, :], w_hi[:, s, :, :].bitcast(F32),
                                     ALU.subtract).then_inc(s_split, 1)

        @block.scalar
        def _(act):
            for s in range(2):
                act.nop().then_inc(s_stored[s], 16)

            def high(i, s, first=False):
                act.wait_ge(s_raw[s], i * 16 + 16)
                if not first:
                    act.wait_ge(s_acc, i * 4 + (2 * s - 2))
                act.activation(w_hi[:, s, :, :], raw[:, s, :, :], ACT.Copy).then_inc(s_hi, 1)

            def evacuate(i, s):
                act.wait_ge(s_stored[s], i * 16 + 16)
                for half in range(2):
                    act.wait_ge(s_acc, i * 4 + (2 * s + half + 1))
                    act.activation(out[:, s, half * HALF:(half + 1) * HALF], ps[:, 2 * s + half, :],
                                   ACT.Copy).then_inc(s_acc_free, 1)
                act.wait_ge(s_acc_free, i * 4 + (4 + 2 * s + 2))
                act.dma_start(dr["proj"][bass.ds((i * 2 + s) * P, P), :], out[:, s, :]).then_inc(s_stored[s], 16)

            high(0, 0, first=True)
            high(0, 1, first=True)
            with act.Fori(0, TURNS - 1) as i:
                for s in range(2):
                    evacuate(i, s)
                    high(i + 1, s)
            for s in range(2):
                evacuate(TURNS - 1, s)

        @block.vector
        def _(vec):
            step = Counted(vec, v_step)
            step.did(vec.memset(h_re[:, :, 0:1], 0.0))
            step.did(vec.memset(h_im[:, :, 0:1], 0.0))
            t0, t1, f_re, f_im = (tmp[:, i, :, :] for i in range(4))

            def product(out, a, b, c, d, op, x, y):
                step.did(vec.tensor_tensor(x, a, b, ALU.mult))
                step.did(vec.tensor_tensor(y, c, d, ALU.mult))
                step.settle()
                step.did(vec.tensor_tensor(out, x, y, op))
                step.settle()

            for a in range(PAIRS // 4):
                wr, wi = quad(w_re, a), quad(w_im, a)
                er, ei = (ps[:, 4 + 2 * (a % 2) + i, :].rearrange("p (q k) -> p q k", q=4) for i in range(2))
                vec.wait_ge(s_e, a + 1)
                product(f_re, er, wr, ei, wi, ALU.add, t0, t1)
                product(f_im, ei, wr, er, wi, ALU.subtract, t0, t1)
                vec.nop().then_inc(s_e_read, 1)
                for g, f in ((t0, f_re), (t1, f_im)):
                    for j in range(4):
                        decay = bc(mag8[:, 4 * a + j:4 * a + j + 1], [P, P])
                        step.did(vec.tensor_tensor_scan(g[:, j, :], decay, f[:, j, :], 0.0, ALU.mult, ALU.add))
                step.settle()
                cut, late = slice(0, P - 1), slice(1, P)
                g_re, g_im, wr, wi = t0[:, :, cut], t1[:, :, cut], wr[:, :, cut], wi[:, :, cut]
                x, y = f_re[:, :, cut], f_im[:, :, cut]
                product(quad(h_re, a)[:, :, late], g_re, wr, g_im, wi, ALU.subtract, x, y)
                product(quad(h_im, a)[:, :, late], g_re, wi, g_im, wr, ALU.add, x, y)
                vec.nop().then_inc(s_h, 1)
            u_v = u[:, :, :].rearrange("p (q h) k -> p q h k", h=2)
            for n in range(GROUPS // 4):
                vec.wait_ge(s_y, n + 1)
                vec.tensor_copy(u_v[:, n // 2 * 4:n // 2 * 4 + 4, n % 2, :],
                                ps[:, 4 + n % 4, :].rearrange("p (q k) -> p q k", q=4)).then_inc(s_y_out, 1)

        @block.tensor
        def _(pe):
            pe.nop().then_inc(s_acc_free, 4)

            def tile(i, s):
                pe.wait_ge(s_split, i * 2 + (s + 1))
                for half in range(2):
                    col = slice(half * HALF, (half + 1) * HALF)
                    pe.wait_ge(s_acc_free, i * 4 + (2 * s + half + 1))
                    bank = ps[:, 2 * s + half, :]
                    for k in range(KD):
                        pe.matmul(bank, w_hi[:, s, k, :], xn_hi[:, k, col], start=k == 0, stop=False)
                        pe.matmul(bank, w_hi[:, s, k, :], xn_lo[:, k, col], start=False, stop=False)
                        last = pe.matmul(bank, w_lo[:, s, k, :], xn_hi[:, k, col], start=False, stop=k == KD - 1)
                    last.then_inc(s_acc, 1)

            def turns(first, end):
                with pe.Fori(first, end) as i:
                    tile(i, 0)
                    tile(i, 1)

            def state_inputs(a):
                if a >= 2:
                    pe.wait_ge(s_e_read, a - 1)
                for i, e in enumerate((e_re, e_im)):
                    for j in range(4):
                        for h in range(2):
                            q, rows = 4 * a + j, slice(64 * h, 64 * h + 64)
                            last = pe.matmul(ps[rows, 4 + 2 * (a % 2) + i, j * P:(j + 1) * P], e[:, q, rows],
                                             u[:, 2 * q + h, :], start=True, stop=True)
                last.then_inc(s_e, 1)

            turns(0, 2)
            turns(2, 4)
            pe.wait_ge(s_u, 16 * NT)
            state_inputs(0)
            state_inputs(1)
            tile(4, 0)
            tile(4, 1)
            state_inputs(2)
            state_inputs(3)
            tile(5, 0)
            tile(5, 1)
            pe.wait_ge(s_toep, 16 * NT)
            pe.wait_ge(s_h, PAIRS // 4)
            for n in range(GROUPS // 4):
                h = n % 2
                rows = slice(64 * h, 64 * h + 64)
                if n >= 4:
                    pe.wait_ge(s_y_out, n - 3)
                for j in range(4):
                    q = n // 2 * 4 + j
                    bank = ps[:, 4 + n % 4, j * P:(j + 1) * P]
                    pe.matmul(bank, toep[:, 2 * q + h, :], u[:, 2 * q + h, :], start=True, stop=False)
                    for o, hs in ((o_re, h_re), (o_im, h_im)):
                        last = pe.matmul(bank, o[rows, q, 1:9, :].rearrange("p k c -> p (k c)"), hs[rows, q, :],
                                         start=False, stop=hs is h_im)
                last.then_inc(s_y, 1)


def gating_block(nc, m, ins, dr, t):
    at, sem = m.at, m.sem
    ident = t["ident"]
    y_hi, y_lo = at("y_hi", [P, FT, SEQ], 64, F32R), at("y_lo", [P, FT, SEQ], 80, F32R)
    us_hi, us_lo = at("us_hi", [P, FT, SEQ], 96, F32R), at("us_lo", [P, FT, SEQ], 112, F32R)
    u, v = at("u_cm", [P, HEADS, SEQ], 128), at("v_cm", [P, HEADS, SEQ], 144)
    yc, xs = at("y_conv", [P, 2, SEQ], 160), at("x_s5", [P, 2, SEQ], 168)
    v_tm = at("v_tm", [P, NT, HEADS, P], 160)
    wn, wp, ws_t = at("ws_rows", [P, HEADS, P], 176), at("ws_perm", [P, HEADS, P], 178), at("ws_t", [P, HEADS, P], 180)
    vst, vh = at("v_slice", [P, 2, HEADS, P], 182), at("v_norm", [P, 2, HEADS, P], 186)
    bn, bp, nw = at("b_rows", [P, HEADS, P], 190), at("b_perm", [P, HEADS, P], 192), at("norm_w", [P, HEADS, P], 194)
    tmp = at("c_tmp", [P, 4, HEADS * P], 197)
    dskip = at("d_skip", [P, FT], 205)
    ssq = at("c_ssq", [P, NT, HEADS], 205.25)
    rstd = at("c_rstd", [P, NT, HEADS], 205.5)
    s_par, s_w, s_uv, s_yc, s_xs, s_masked, s_wp, s_wt, s_t, s_g, s_y, s_gu, s_vst, s_vt, s_sq, s_v_done, s_inv, \
        s_rstd, s_vh, s_mix, s_us, v_step, a_step = (sem(f"c_{n}") for n in (
            "par", "w", "uv", "yc", "xs", "masked", "wp", "wt", "t", "g", "y", "gu", "vst", "vt", "sq", "v_done",
            "inv", "rstd", "vh", "mix", "us", "v_step", "a_step"))
    chunk = lambda cm, k: cm[:, :, :].rearrange("c h (p j) -> c h p j", p=NT)[:, :, :, bass.ds(k * SC, SC)]
    phased = lambda ap: ap.rearrange("c h (p j) -> c h p j", p=NT)
    permuted = lambda ap: ap.rearrange("a h (c p) -> a h p c", p=NT)

    with ExitStack() as local:
        ps = local.enter_context(nc.psum_tensor("c_ps", [P, 8, HALF], F32))
        block = local.enter_context(nc.Block())

        @block.sync
        def _(sp):
            for f in range(FT):
                if f >= 2:
                    sp.wait_ge(s_y, f - 1)
                sp.dma_start(yc[:, f % 2, :], dr["y"][f * P:(f + 1) * P, :]).then_inc(s_yc, 16)
                sp.dma_start(xs[:, f % 2, :], dr["proj"][f * P:(f + 1) * P, :]).then_inc(s_xs, 16)
                if f == 1:
                    for i, tile in enumerate((v, u)):
                        rows = dr["proj"][(2 - i) * S5W:(3 - i) * S5W, :]
                        sp.dma_start(tile[:, :, :], rows.rearrange("(f p) s -> p f s", p=P)).then_inc(s_uv, 16)
                sp.wait_ge(s_yc, 16 * (f + 1))
                sp.wait_ge(s_xs, 16 * (f + 1))

        @block.gpsimd
        def _(gp):
            gp.wait_ge(s_w, 16)
            gp.affine_select(out=wn[:, :, :], in_=wn[:, :, :], compare_op=ALU.is_ge, fill=0.0, base=0,
                             pattern=[[0, HEADS], [-1, P]], channel_multiplier=1).then_inc(s_masked, 1)

        @block.scalar
        def _(act):
            step = Counted(act, a_step)
            act.dma_start(wn[:, :, :], ins["sgu_w"][0].rearrange("h t s -> t h s")).then_inc(s_w, 16)
            with nc.allow_non_contiguous_dma(reason="a short vector, channels across partitions"):
                act.dma_start(dskip[:, :], ins["s5_d"][0].rearrange("(f p) -> p f", p=P)).then_inc(s_par, 16)
            act.dma_start(bn[:, :, :].rearrange("p h t -> p (h t)"),
                          ins["sgu_b"][0].rearrange("h t -> (h t)").partition_broadcast(P)).then_inc(s_par, 16)
            act.dma_start(nw[:, :, :].rearrange("p h t -> p (h t)"), ins["sgu_norm"][0].partition_broadcast(P)).then_inc(s_par, 16)
            for f in range(FT):
                act.wait_ge(s_t, f + 1)
                act.activation(yc[:, f % 2, :], yc[:, f % 2, :], ACT.Gelu_apprx_tanh).then_inc(s_g, 1)
            act.wait_ge(s_uv, 32)
            with act.Fori(0, NT // 2) as i:
                for s in range(2):
                    act.activation(phased(vst[:, s, :, :]), chunk(v, i * 2 + s), ACT.Gelu_apprx_tanh).then_inc(s_vst, 1)
                for s in range(2):
                    act.wait_ge(s_vt, i * 2 + (s + 1))
                    act.wait_ge(s_v_done, i * 2 + (s + 1))
                    act.activation(tmp[:, s, :], ps[:, s, :], ACT.Square).then_inc(s_sq, 1)
            act.activation(u[:, :, :], u[:, :, :], ACT.Gelu_apprx_tanh).then_inc(s_gu, 1)
            act.wait_ge(s_inv, 1)
            act.activation(rstd[:, :, :], rstd[:, :, :], ACT.Sqrt).then_inc(s_rstd, 1)

        @block.vector
        def _(vec):
            step = Counted(vec, v_step)
            vec.wait_ge(s_par, 48)
            for f in range(FT):
                vec.wait_ge(s_yc, 16 * (f + 1))
                vec.wait_ge(s_xs, 16 * (f + 1))
                if f >= 2:
                    vec.wait_ge(s_y, f - 1)
                vec.scalar_tensor_tensor(yc[:, f % 2, :], xs[:, f % 2, :], dskip[:, f:f + 1], yc[:, f % 2, :],
                                         ALU.mult, ALU.add).then_inc(s_t, 1)
                vec.wait_ge(s_g, f + 1)
                step.did(vec.tensor_copy(y_hi[:, f, :], yc[:, f % 2, :]))
                step.settle()
                vec.tensor_tensor(y_lo[:, f, :], yc[:, f % 2, :], y_hi[:, f, :].bitcast(F32), ALU.subtract).then_inc(s_y, 1)
            step.did(vec.tensor_copy(phased(bp[:, :, :]), permuted(bn[:, :, :])))
            vec.wait_ge(s_masked, 1)
            vec.tensor_copy(phased(wp[:, :, :]), permuted(wn[:, :, :])).then_inc(s_wp, 1)
            vec.wait_ge(s_wt, 1)
            step.did(vec.tensor_copy(phased(ws_t[:, :, :]), permuted(ps[:, 2, :].rearrange("s (h t) -> s h t", h=HEADS))))
            step.settle()
            with vec.Fori(0, NT // 2) as i:
                for s in range(2):
                    vec.wait_ge(s_sq, i * 2 + (s + 1))
                    vec.tensor_copy(v_tm[:, i * 2 + s, :, :], ps[:, s, :].rearrange("p (h d) -> p h d", h=HEADS))
                    vec.reduce_sum(ssq[:, i * 2 + s, :], tmp[:, s, :].rearrange("p (h d) -> p h d", h=HEADS),
                                   AX.X).then_inc(s_v_done, 1)
            vec.wait_ge(s_v_done, 2 + NT)
            step.did(vec.tensor_scalar(rstd[:, :, :], ssq[:, :, :], 1.0 / P, EPS, ALU.mult, ALU.add))
            step.settle()
            vec.reciprocal(rstd[:, :, :], rstd[:, :, :]).then_inc(s_inv, 1)
            vec.wait_ge(s_rstd, 1)
            vec.wait_ge(s_gu, 1)
            with vec.Fori(0, NT // 2) as i:
                step.loop_body(i, 2 * 4)
                for s in range(2):
                    k = i * 2 + s
                    step.did(vec.tensor_tensor(vh[:, s, :, :], v_tm[:, k, :, :],
                                               bc(rstd[:, k, :].unsqueeze(2), [P, HEADS, P]), ALU.mult))
                    step.settle()
                    vec.tensor_tensor(vh[:, s, :, :], vh[:, s, :, :], nw[:, :, :], ALU.mult).then_inc(s_vh, 1)
                for s in range(2):
                    k = i * 2 + s
                    vec.wait_ge(s_mix, i * 2 + (s + 1))
                    full = tmp[:, s, :].rearrange("p (h t) -> p h t", h=HEADS)
                    step.did(vec.tensor_tensor(full, ps[:, 4 + s, :].rearrange("p (h t) -> p h t", h=HEADS),
                                               bp[:, :, :], ALU.add))
                    step.settle()
                    step.did(vec.tensor_tensor(phased(full), phased(full), chunk(u, k), ALU.mult))
                    step.settle()
                    step.did(vec.tensor_copy(chunk(us_hi, k), phased(full)))
                    step.settle()
                    vec.tensor_tensor(chunk(us_lo, k), phased(full), chunk(us_hi, k).bitcast(F32),
                                      ALU.subtract).then_inc(s_us, 1)
            step.loop_end(NT // 2)

        @block.tensor
        def _(pe):
            pe.nop().then_inc(s_v_done, 2)
            pe.wait_ge(s_wp, 1)
            for h in range(HEADS):
                last = pe.transpose(ps[:, 2, h * P:(h + 1) * P], wp[:, h, :], ident[:, :])
            last.then_inc(s_wt, 1)
            with pe.Fori(0, NT // 2) as i:
                for s in range(2):
                    pe.wait_ge(s_vst, i * 2 + (s + 1))
                    pe.wait_ge(s_v_done, i * 2 + (s + 1))
                    for h in range(HEADS):
                        last = pe.transpose(ps[:, s, h * P:(h + 1) * P], vst[:, s, h, :], ident[:, :])
                    last.then_inc(s_vt, 1)
            with pe.Fori(0, NT // 2) as i:
                for s in range(2):
                    pe.wait_ge(s_vh, i * 2 + (s + 1))
                    for h in range(HEADS):
                        last = pe.matmul(ps[:, 4 + s, h * P:(h + 1) * P], vh[:, s, h, :], ws_t[:, h, :],
                                         start=True, stop=True)
                    last.then_inc(s_mix, 1)
    return dict(y_hi=y_hi, y_lo=y_lo, us_hi=us_hi, us_lo=us_lo)


def merge_block(nc, m, ins, dr, t):
    at, sem = m.at, m.sem
    xn, y, us = (t["xn_hi"], t["xn_lo"]), (t["y_hi"], t["y_lo"]), (t["us_hi"], t["us_lo"])
    G5, GS, ZA, ZB, PR = range(5)
    DEPTH = (KD, KD, FT, FT, FT)
    START = (0, 8, 16, 20, 24)
    SLICES = 28
    raw = at("d_raw", [P, SLICES, P], 128)
    w_hi, w_lo = at("d_w_hi", [P, SLICES, P], 142, F32R), at("d_w_lo", [P, SLICES, P], 156, F32R)
    sig = at("d_sig", [P, 3, 2, HALF], 170)
    acc = at("d_acc", [P, 2, 2, HALF], 182)
    out = at("d_out", [P, 2, SEQ], 190)
    s_raw = [sem(f"d_raw{j}") for j in range(5)]
    s_hi, s_split, s_mm, s_sig, s_pr, s_merged = (sem(f"d_{n}") for n in ("hi", "split", "mm", "sig", "pr", "merged"))
    s_out = sem("d_out")
    v_step = sem("d_v_step")
    w_in = ins["w_in"][0].rearrange("(k p) c -> p k c", p=P)
    w_glu = ins["w_glu"][0].rearrange("(k p) c -> p k c", p=P)
    w_proj = ins["w_sgu_proj"][0].rearrange("(k p) c -> p k c", p=P)
    gates = 3 * S5W
    source = ((w_in, gates), (w_in, gates + D), (w_glu, 0), (w_glu, D), (w_proj, 0))
    ORDER = (PR, G5, GS, ZB, ZA)
    BANK = {G5: 0, GS: 2, PR: 4, ZB: 6, ZA: 0}
    RANK = {j: r for r, j in enumerate(ORDER)}

    with ExitStack() as local:
        ps = local.enter_context(nc.psum_tensor("d_ps", [P, 8, HALF], F32))
        block = local.enter_context(nc.Block())

        @block.sync
        def _(sp):
            def load(j, i):
                w, first = source[j]
                sp.dma_start(raw[:, START[j]:START[j] + DEPTH[j], :],
                             w[:, :, bass.ds(i * P + first, P)]).then_inc(s_raw[j], 16)

            def load_all(i):
                for r, j in enumerate(ORDER):
                    sp.wait_ge(s_split, i * 5 + (r - 4))
                    load(j, i)

            def store(i, s):
                sp.wait_ge(s_merged, i * 2 + 2)
                sp.wait_ge(s_out, i * 16 + 16)
                sp.dma_start(dr["merged"][bass.ds(i * P, P), :], out[:, s, :]).then_inc(s_out, 16)

            for j in ORDER:
                load(j, 0)
            with sp.Fori(2, KD // 2 + 1) as turn:
                load_all(turn * 2 - 3)
                store(turn * 2 - 4, 0)
                load_all(turn * 2 - 2)
                store(turn * 2 - 3, 1)
            load_all(KD - 1)
            store(KD - 2, 0)
            store(KD - 1, 1)
            sp.wait_ge(s_out, 16 * (2 + KD))

        @block.gpsimd
        def _(gp):
            with gp.Fori(0, KD) as i:
                for r, j in enumerate(ORDER):
                    sl = slice(START[j], START[j] + DEPTH[j])
                    gp.wait_ge(s_hi, i * 5 + (r + 1))
                    gp.tensor_tensor(w_lo[:, sl, :], raw[:, sl, :], w_hi[:, sl, :].bitcast(F32),
                                     ALU.subtract).then_inc(s_split, 1)

        @block.scalar
        def _(act):
            def high(j, i, first=False):
                sl = slice(START[j], START[j] + DEPTH[j])
                act.wait_ge(s_raw[j], i * 16 + 16)
                if not first:
                    act.wait_ge(s_mm, i * 10 + (2 * RANK[j] - 8))
                act.activation(w_hi[:, sl, :], raw[:, sl, :], ACT.Copy).then_inc(s_hi, 1)

            def sigmoid(j, n, i, first=False):
                for half in range(2):
                    act.wait_ge(s_mm, i * 10 + (2 * RANK[j] + half + 1))
                    if not first:
                        act.wait_ge(s_merged, i * 2 + (half - 1))
                    act.activation(sig[:, n, half, :], ps[:, BANK[j] + half, :], ACT.Sigmoid).then_inc(s_sig, 1)

            def turn(i, first=False, last=False):
                for j, n in ((PR, None), (G5, 0), (GS, 1), (ZB, 2), (ZA, None)):
                    if n is not None:
                        sigmoid(j, n, i, first)
                    if not last:
                        high(j, i + 1)

            for j in ORDER:
                high(j, 0, first=True)
            turn(0, first=True)
            with act.Fori(1, KD - 1) as i:
                turn(i)
            turn(KD - 1, last=True)

        @block.vector
        def _(vec):
            step = Counted(vec, v_step)
            vec.nop().then_inc(s_out, 32)
            with vec.Fori(0, KD // 2) as turn:
                step.loop_body(turn, 2 * 2 * 3)
                for s in range(2):
                    i = turn * 2 + s
                    vec.wait_ge(s_out, i * 16 + 16)
                    for half in range(2):
                        vec.wait_ge(s_mm, i * 10 + (2 * RANK[PR] + half + 1))
                        vec.wait_ge(s_sig, i * 6 + (2 + half + 1))
                        vec.tensor_tensor(acc[:, 0, half, :], ps[:, BANK[PR] + half, :], sig[:, 1, half, :],
                                          ALU.mult).then_inc(s_pr, 1)
                        vec.wait_ge(s_sig, i * 6 + (4 + half + 1))
                        step.did(vec.tensor_tensor(acc[:, 1, half, :], sig[:, 0, half, :], sig[:, 2, half, :], ALU.mult))
                        step.settle()
                    for half in range(2):
                        vec.wait_ge(s_mm, i * 10 + (2 * RANK[ZA] + half + 1))
                        step.did(vec.tensor_tensor(acc[:, 1, half, :], ps[:, BANK[ZA] + half, :], acc[:, 1, half, :], ALU.mult))
                        step.settle()
                        vec.wait_ge(s_pr, i * 2 + (half + 1))
                        step.did(vec.tensor_tensor(out[:, s, half * HALF:(half + 1) * HALF], acc[:, 0, half, :],
                                                   acc[:, 1, half, :], ALU.add))
                        step.settle()
                        vec.nop().then_inc(s_merged, 1)
            step.loop_end(KD // 2)

        @block.tensor
        def _(pe):
            def product(j, i, first):
                pe.wait_ge(s_split, i * 5 + (RANK[j] + 1))
                hi, lo = {G5: xn, GS: xn, ZA: y, ZB: y, PR: us}[j]
                for half in range(2):
                    col = slice(half * HALF, (half + 1) * HALF)
                    if j == ZA:
                        pe.wait_ge(s_sig, i * 6 + (half + 1))
                    elif not first:
                        if j == PR:
                            pe.wait_ge(s_pr, i * 2 + (half - 1))
                        elif j == G5:
                            pe.wait_ge(s_merged, i * 2 + (half - 1))
                        else:
                            pe.wait_ge(s_sig, i * 6 + (half + (-3 if j == GS else -1)))
                    bank = ps[:, BANK[j] + half, :]
                    for k in range(DEPTH[j]):
                        a = START[j] + k
                        pe.matmul(bank, w_hi[:, a, :], hi[:, k, col], start=k == 0, stop=False)
                        pe.matmul(bank, w_hi[:, a, :], lo[:, k, col], start=False, stop=False)
                        last = pe.matmul(bank, w_lo[:, a, :], hi[:, k, col], start=False, stop=k == DEPTH[j] - 1)
                    last.then_inc(s_mm, 1)

            for j in ORDER:
                product(j, 0, True)
            with pe.Fori(1, KD) as i:
                for j in ORDER:
                    product(j, i, False)



def mixer_out_block(nc, m, ins, dr, t):
    at, sem = m.at, m.sem
    ident = t["ident"]
    h = at("h", [P, NT, D], 0)
    wo_hi, wo_lo = at("wo_hi", [P, KD, D], 32, F32R), at("wo_lo", [P, KD, D], 64, F32R)
    wraw = at("wo_raw", [P, 2, D], 96)
    mg = at("merged_slice", [P, 2, KD, P], 104)
    mg_hi, mg_lo = at("mg_hi", [P, 2, KD, P], 112, F32R), at("mg_lo", [P, 2, KD, P], 120, F32R)
    xt, xt_t = at("xt", [P, 2, D], 128), at("xt_t", [P, 2, KD, P], 136)
    w_r = at("w_router", [P, KD, NGRP + EXPERTS], 144)
    moe_raw = at("moe_raw", [P, 6, 4 * HALF], 148)
    g = at("g_ffn", [P, D], 197)
    logits = at("logits", [P, NT, NGRP + EXPERTS], 201)
    bias = at("router_bias", [P, NGRP + EXPERTS], 202.25)
    ssq, rstd = at("e_ssq", [P, 2], 202.5), at("e_rstd", [P, 2], 202.625)
    junk = at("e_junk", [P, D], 203)
    s_wraw, s_mg, s_out = ([sem(f"e_{n}{s}") for s in range(2)] for n in ("wraw", "mg", "out"))
    s_x, s_par, s_whi, s_wsplit, s_mg_hi, s_mg_split, s_mm, s_h, s_inv, s_rstd, s_xt, s_xtt, s_ev, s_rt, \
        s_log, v_step = (sem(f"e_{n}") for n in (
            "x", "par", "whi", "wsplit", "mg_hi", "mg_split", "mm", "h", "inv", "rstd", "xt", "xtt", "ev",
            "rt", "log", "v_step"))
    s_moe = [sem(f"moe_raw{j}") for j in range(6)]
    N_OUT = NGRP + EXPERTS

    with ExitStack() as local:
        ps = local.enter_context(nc.psum_tensor("e_ps", [P, 8, HALF], F32))
        block = local.enter_context(nc.Block())

        @block.sync
        def _(sp):
            mg_v = dr["merged"].rearrange("(k p) s -> p k s", p=P)
            xt_v = dr["xt"].rearrange("(t p) d -> t p d", p=P)

            def load(n, s):
                sp.wait_ge(s_mg_split, n + 1)
                sp.dma_start(mg[:, s, :, :], mg_v[:, :, bass.ds(n * P, P)]).then_inc(s_mg[s], 16)

            def store(n, s):
                sp.wait_ge(s_xt, n + 1)
                sp.dma_start(xt_v[bass.ds(n, 1)].rearrange("o p d -> (o p) d"), xt[:, s, :]).then_inc(s_out[s], 16)

            load(0, 0)
            for k in range(KD):
                if k >= 2:
                    sp.wait_ge(s_wsplit, k - 1)
                sp.dma_start(wraw[:, k % 2, :], ins["w_out"][0, k * P:(k + 1) * P, :]).then_inc(s_wraw[k % 2], 16)
            xv = ins["x"][0].rearrange("(c p) d -> c p d", p=NT)
            sp.dma_start(h[:, :, :], xv).then_inc(s_x, 16)
            load(1, 1)
            for j in (0, 1):
                for i, name in enumerate(("w_expert_gate", "w_expert_up")):
                    sp.dma_start(moe_raw[:, 2 * j + i, :].rearrange("p (k f) -> p k f", k=4),
                                 ins[name][0, 0].rearrange("(k p) f -> p k f", p=P)[:, 4 * j:4 * j + 4, :]).then_inc(s_moe[2 * j + i], 16)
            load(2, 0)
            with sp.Fori(1, (NT - 4) // 2 + 1) as i:
                load(i * 2 + 1, 1)
                store(i * 2 - 2, 0)
                load(i * 2 + 2, 0)
                store(i * 2 - 1, 1)
            load(NT - 1, 1)
            for n in range(NT - 4, NT):
                store(n, n % 2)
            for s in range(2):
                sp.wait_ge(s_out[s], 16 * (1 + NT // 2))
            sp.wait_ge(s_x, 16)

        @block.gpsimd
        def _(gp):
            gp.nop().then_inc(s_mg_split, 2)
            with gp.Fori(0, NT // 2) as i:
                for s in range(2):
                    gp.wait_ge(s_mg_hi, i * 2 + (s + 1))
                    gp.tensor_tensor(mg_lo[:, s, :, :], mg[:, s, :, :], mg_hi[:, s, :, :].bitcast(F32),
                                     ALU.subtract).then_inc(s_mg_split, 1)

        @block.scalar
        def _(act):
            act.dma_start(w_r[:, :, 0:NGRP], ins["w_router_group"][0].rearrange("(k p) e -> p k e", p=P)).then_inc(s_par, 16)
            act.dma_start(w_r[:, :, NGRP:], ins["w_router_expert"][0].rearrange("(k p) e -> p k e", p=P)).then_inc(s_par, 16)
            act.dma_start(bias[:, 0:NGRP], ins["b_router_group"][0].partition_broadcast(P)).then_inc(s_par, 16)
            act.dma_start(bias[:, NGRP:], ins["b_router_expert"][0].partition_broadcast(P)).then_inc(s_par, 16)
            act.dma_start(g[:, :], ins["norm_ffn"][0].partition_broadcast(P)).then_inc(s_par, 16)
            for s in range(2):
                act.nop().then_inc(s_out[s], 16)

            def high(n, s):
                act.wait_ge(s_mg[s], n * 8 + (16 - 8 * s))
                act.wait_ge(s_mm, n * 2 + 2)
                act.activation(mg_hi[:, s, :, :], mg[:, s, :, :], ACT.Copy).then_inc(s_mg_hi, 1)

            def normalise_and_copy(n, s):
                act.wait_ge(s_inv, n + 1)
                act.activation(rstd[:, s:s + 1], rstd[:, s:s + 1], ACT.Sqrt).then_inc(s_rstd, 1)
                act.wait_ge(s_rt, n + 1)
                for b in range(2):
                    act.wait_ge(s_xtt, n * 2 + (b + 1))
                    act.activation(xt_t[:, s, 4 * b:4 * b + 4, :], ps[:, 4 + b, :].rearrange("p (k c) -> p k c", k=4),
                                   ACT.Copy).then_inc(s_ev, 1)

            high(0, 0)
            for k in range(KD):
                act.wait_ge(s_wraw[k % 2], 16 * (k // 2 + 1))
                act.activation(wo_hi[:, k, :], wraw[:, k % 2, :], ACT.Copy).then_inc(s_whi, 1)
            with act.Fori(0, NT // 2 - 1) as i:
                high(i * 2 + 1, 1)
                normalise_and_copy(i * 2, 0)
                high(i * 2 + 2, 0)
                normalise_and_copy(i * 2 + 1, 1)
            high(NT - 1, 1)
            normalise_and_copy(NT - 2, 0)
            normalise_and_copy(NT - 1, 1)

        @block.vector
        def _(vec):
            step = Counted(vec, v_step)
            vec.nop().then_inc(s_h, 4)
            vec.nop().then_inc(s_log, 1)
            for k in range(KD):
                vec.wait_ge(s_whi, k + 1)
                vec.tensor_tensor(wo_lo[:, k, :], wraw[:, k % 2, :], wo_hi[:, k, :].bitcast(F32),
                                  ALU.subtract).then_inc(s_wsplit, 1)
            vec.wait_ge(s_x, 16)
            vec.wait_ge(s_par, 80)

            def residual_and_norm(n, s):
                row = h[:, bass.ds(n, 1), :].rearrange("p o d -> p (o d)")
                for half in range(2):
                    col = slice(half * HALF, (half + 1) * HALF)
                    vec.wait_ge(s_mm, n * 2 + (4 + half + 1))
                    vec.tensor_tensor(row[:, col], ps[:, 2 * s + half, :], row[:, col], ALU.add).then_inc(s_h, 1)
                one = slice(s, s + 1)
                vec.wait_ge(s_h, n * 2 + 6)
                step.did(vec.scalar_tensor_tensor(junk[:, :], row, 1.0, row, ALU.mult, ALU.mult, accum_out=ssq[:, one]))
                step.settle()
                step.did(vec.tensor_scalar(rstd[:, one], ssq[:, one], 1.0 / D, EPS, ALU.mult, ALU.add))
                step.settle()
                vec.reciprocal(rstd[:, one], rstd[:, one]).then_inc(s_inv, 1)
                vec.wait_ge(s_rstd, n + 1)
                vec.wait_ge(s_out[s], n * 8 + (16 - 8 * s))
                vec.scalar_tensor_tensor(xt[:, s, :], row, rstd[:, one], g[:, :], ALU.mult, ALU.mult).then_inc(s_xt, 1)

            def add_bias(n, s):
                vec.wait_ge(s_rt, n + 3)
                vec.tensor_tensor(logits[:, bass.ds(n, 1), :].rearrange("p o e -> p (o e)"), ps[:, 6, 0:N_OUT],
                                  bias[:, :], ALU.add).then_inc(s_log, 1)

            tile_pair_loop(vec, residual_and_norm, add_bias, step, 4)

        @block.tensor
        def _(pe):
            pe.nop().then_inc(s_mm, 4)
            pe.nop().then_inc(s_rt, 2)
            pe.nop().then_inc(s_ev, 2)

            def products(n, s, ks):
                for k in ks:
                    if isinstance(n, int) and n == 0:
                        pe.wait_ge(s_wsplit, k + 1)
                    for half in range(2):
                        if k == 0:
                            pe.wait_ge(s_h, n * 2 + (half + 1))
                        col = slice(half * HALF, (half + 1) * HALF)
                        bank = ps[:, 2 * s + half, :]
                        pe.matmul(bank, mg_hi[:, s, k, :], wo_hi[:, k, col], start=k == 0, stop=False)
                        pe.matmul(bank, mg_hi[:, s, k, :], wo_lo[:, k, col], start=False, stop=False)
                        last = pe.matmul(bank, mg_lo[:, s, k, :], wo_hi[:, k, col], start=False, stop=k == KD - 1)
                        if k == KD - 1:
                            last.then_inc(s_mm, 1)

            def transposes(n, s):
                pe.wait_ge(s_xt, n + 1)
                for b in range(2):
                    pe.wait_ge(s_ev, n * 2 + (b + 1))
                    for k in range(4 * b, 4 * b + 4):
                        last = pe.transpose(ps[:, 4 + b, (k % 4) * P:(k % 4 + 1) * P], xt[:, s, k * P:(k + 1) * P], ident[:, :])
                    last.then_inc(s_xtt, 1)

            def product_tile(n, s, before=True):
                pe.wait_ge(s_mg_split, n + 3)
                products(n, s, range(KD // 2))
                if before:
                    transposes(n - 1, 1 - s)
                products(n, s, range(KD // 2, KD))

            def router(n, s):
                pe.wait_ge(s_ev, n * 2 + 4)
                pe.wait_ge(s_log, n + 1)
                for k in range(KD):
                    last = pe.matmul(ps[:, 6, 0:N_OUT], xt_t[:, s, k, :], w_r[:, k, :], start=k == 0, stop=k == KD - 1)
                last.then_inc(s_rt, 1)

            product_tile(0, 0, before=False)
            pe.wait_ge(s_par, 80)
            with pe.Fori(0, NT // 2 - 1) as i:
                product_tile(i * 2 + 1, 1, before=True)
                router(i * 2, 0)
                product_tile(i * 2 + 2, 0, before=True)
                router(i * 2 + 1, 1)
            product_tile(NT - 1, 1)
            router(NT - 2, 0)
            transposes(NT - 1, 1)
            router(NT - 1, 1)
    return dict(h=h, logits=logits, moe_raw=moe_raw, s_moe=s_moe)


def routing_block(nc, m, ins, dr, t):
    at, sem = m.at, m.sem
    logits = t["logits"]
    weights, dest = at("weights", [P, 2, NT], 205), at("dest", [P, 2, NT], 205.125, I32)
    row_tok = at("row_tok", [P, NBLK], 205.25, I32)
    over_e, over_n = at("over_e", [1, 16], 205.5, I32), at("over_n", [1, 1], 205.5625, I32)
    place = [32.0]

    def new(name, shape):
        size = 4 * math.prod(shape[1:]) / 1024
        tile = at(name, shape, place[0])
        place[0] += math.ceil(size * 32) / 32
        return tile

    down4, down8, iota32, iota_b, iota_s = (new(n, [P, k]) for n, k in
                                            (("down4", 4), ("down8", 8), ("iota32", 32), ("iota_b", NBLK), ("iota_s", P)))
    token, steps7, ones32 = new("token", [P, NT]), new("steps7", [P, 7]), new("ones32", [P, 32])
    tri, ones = new("tri", [P, P]), new("ones", [P, P])
    a, b, c, gsum, gw = (new(f"r{i}", [P, NT]) for i in range(5))
    g4a, g4b, sel_g = (new(f"g4{i}", [P, NT, 4]) for i in range(3))
    e8a, e8b, e8c, e8d = (new(f"e8{i}", [P, NT, 8]) for i in range(4))
    sel = new("sel", [P, 2, NT, 8])
    big = new("big", [P, NT, NGRP, EPG])
    one_hot = new("one_hot", [P, 2, NT, EXPERTS])
    both, before, pos = (new(n, [P, NT, EXPERTS]) for n in ("both", "before", "pos"))
    total, cnt, extra, incl, start = (new(n, [P, EXPERTS]) for n in ("total", "cnt", "extra", "incl", "start"))
    cmp7, cmpt = new("cmp7", [P, EXPERTS, 7]), new("cmpt", [P, 2 * NT, 7])
    prod = new("prod", [P, 2 * NT, EXPERTS])
    pk, bk, ek, bx, slot, blk, tmp = (new(n, [P, 2 * NT]) for n in ("pk", "bk", "ek", "bx", "slot", "blk", "rtmp"))
    slot_hot, block_hot = new("slot_hot", [P, 2 * NT, P]), new("block_hot", [P, 2 * NT, NBLK])
    over = new("over", [1, OVER, EXPERTS])
    over_f = new("over_f", [1, OVER])
    assert place[0] <= 148
    s_const, s_tri, s_e1, s_e1d, s_e2, s_e2d, s_cum, s_cum_ps, s_hot, s_rows, v_step = (sem(f"f_{n}") for n in (
        "const", "tri", "e1", "e1d", "e2", "e2d", "cum", "cum_ps", "hot", "rows", "v_step"))

    with ExitStack() as local:
        ps = local.enter_context(nc.psum_tensor("f_ps", [P, 8, HALF], F32))
        block = local.enter_context(nc.Block())

        @block.gpsimd
        def _(gp):
            def ramp(tile, step, base, per_partition=0, n=None):
                gp.iota(tile[:, :], [[step, tile.shape[1]]], base=base, channel_multiplier=per_partition,
                        allow_small_or_imprecise_dtypes=True).then_inc(s_const, 1)

            ramp(down4, -1, 4)
            ramp(down8, -1, 8)
            ramp(iota32, 1, 0)
            ramp(iota_b, 1, 0)
            ramp(iota_s, 1, 0)
            ramp(token, P, 0, 1)
            ramp(steps7, BLK, BLK)
            gp.memset(ones32[:, :], 1.0).then_inc(s_const, 1)
            gp.memset(ones[:, :], 1.0).then_inc(s_const, 1)
            gp.wait_ge(s_const, 9)
            gp.affine_select(out=tri[:, :], in_=ones[:, :], compare_op=ALU.is_gt, fill=0.0, base=0,
                             pattern=[[1, P]], channel_multiplier=-1).then_inc(s_tri, 1)

        @block.scalar
        def _(act):
            act.wait_ge(s_e1, 1)
            act.activation(g4a[:, :, :], g4a[:, :, :], ACT.Exp).then_inc(s_e1d, 1)
            act.wait_ge(s_e2, 1)
            act.activation(c[:, :], c[:, :], ACT.Exp).then_inc(s_e2d, 1)

        @block.vector
        def _(vec):
            step = Counted(vec, v_step)
            tt, ts = vec.tensor_tensor, vec.tensor_scalar

            def op(instruction):
                step.did(instruction)
                step.settle()

            wide = lambda ap, n: bc(ap.unsqueeze(ap.ndim), list(ap.shape) + [n])
            flat = lambda tile: tile[:, :, :].rearrange("p k t -> p (k t)")

            def first_max(out, values, down, n, top, key):
                op(vec.reduce_max(top, values, AX.X))
                op(tt(key, values, wide(top, n), ALU.is_ge))
                op(tt(key, key, bc(down[:, :].unsqueeze(1), [P, NT, n]), ALU.mult))
                op(vec.reduce_max(b[:, :], key, AX.X))
                op(tt(out, key, wide(b[:, :], n), ALU.is_equal))

            vec.wait_ge(s_const, 9)
            gl, el = logits[:, :, 0:NGRP], logits[:, :, NGRP:].rearrange("p t (g e) -> p t g e", g=NGRP)
            first_max(sel_g[:, :, :], gl, down4, NGRP, a[:, :], g4b[:, :, :])
            tt(g4a[:, :, :], gl, wide(a[:, :], NGRP), ALU.subtract).then_inc(s_e1, 1)
            op(tt(big[:, :, :, :], el, wide(sel_g[:, :, :], EPG), ALU.mult))
            op(vec.reduce_sum(e8a[:, :, :], big[:, :, :, :].rearrange("p t g e -> p t e g"), AX.X))
            vec.wait_ge(s_e1d, 1)
            op(vec.reduce_sum(gsum[:, :], g4a[:, :, :], AX.X))
            op(vec.reciprocal(gw[:, :], gsum[:, :]))
            first_max(sel[:, 0, :, :], e8a[:, :, :], down8, EPG, a[:, :], e8b[:, :, :])
            op(ts(e8c[:, :, :], sel[:, 0, :, :], -1.0, 1.0, ALU.mult, ALU.add))
            op(tt(e8c[:, :, :], e8a[:, :, :], e8c[:, :, :], ALU.mult))
            op(ts(e8d[:, :, :], sel[:, 0, :, :], -3.0e38, None, ALU.mult))
            op(tt(e8c[:, :, :], e8c[:, :, :], e8d[:, :, :], ALU.add))
            op(vec.reduce_max(gsum[:, :], e8c[:, :, :], AX.X))
            op(tt(e8b[:, :, :], e8c[:, :, :], wide(gsum[:, :], EPG), ALU.is_ge))
            op(tt(e8b[:, :, :], e8b[:, :, :], bc(down8[:, :].unsqueeze(1), [P, NT, EPG]), ALU.mult))
            op(vec.reduce_max(b[:, :], e8b[:, :, :], AX.X))
            op(tt(sel[:, 1, :, :], e8b[:, :, :], wide(b[:, :], EPG), ALU.is_equal))
            tt(c[:, :], gsum[:, :], a[:, :], ALU.subtract).then_inc(s_e2, 1)
            for k in range(2):
                op(tt(one_hot[:, k, :, :].rearrange("p t (g e) -> p t g e", g=NGRP), wide(sel_g[:, :, :], EPG),
                      bc(sel[:, k, :, :].unsqueeze(2), [P, NT, NGRP, EPG]), ALU.mult))
            op(tt(both[:, :, :], one_hot[:, 0, :, :], one_hot[:, 1, :, :], ALU.add))
            op(vec.memset(before[:, 0, :], 0.0))
            for n in range(1, NT):
                op(tt(before[:, n, :], before[:, n - 1, :], both[:, n - 1, :], ALU.add))
            op(tt(total[:, :], before[:, NT - 1, :], both[:, NT - 1, :], ALU.add))
            vec.nop().then_inc(s_cum, 1)
            vec.wait_ge(s_e2d, 1)
            op(ts(a[:, :], c[:, :], 1.0, None, ALU.add))
            op(vec.reciprocal(b[:, :], a[:, :]))
            op(tt(weights[:, 0, :], b[:, :], gw[:, :], ALU.mult))
            op(tt(weights[:, 1, :], weights[:, 0, :], c[:, :], ALU.mult))
            vec.wait_ge(s_cum_ps, 1)
            op(vec.tensor_copy(pos[:, :, :], ps[:, 0, 0:NT * EXPERTS].rearrange("p (t e) -> p t e", e=EXPERTS)))
            op(vec.tensor_copy(cnt[:, :], ps[:, 1, 0:EXPERTS]))
            op(tt(cmp7[:, :, :], wide(cnt[:, :], 7), bc(steps7[:, :].unsqueeze(1), [P, EXPERTS, 7]), ALU.is_gt))
            op(vec.reduce_sum(extra[:, :], cmp7[:, :, :], AX.X))
            op(vec.tensor_tensor_scan(incl[:, :], ones32[:, :], extra[:, :], 0.0, ALU.mult, ALU.add))
            op(tt(start[:, :], incl[:, :], extra[:, :], ALU.subtract))
            op(ts(start[:, :], start[:, :], float(EXPERTS - 1), None, ALU.add))
            hot = one_hot[:, :, :, :].rearrange("p k t e -> p (k t) e")
            for k in range(2):
                op(tt(prod[:, k * NT:(k + 1) * NT, :], one_hot[:, k, :, :], pos[:, :, :], ALU.mult))
            op(vec.reduce_sum(pk[:, :], prod[:, :, :], AX.X))
            for out, per_expert in ((bk, start), (ek, iota32)):
                op(tt(prod[:, :, :], hot, bc(per_expert[:, :].unsqueeze(1), [P, 2 * NT, EXPERTS]), ALU.mult))
                op(vec.reduce_sum(out[:, :], prod[:, :, :], AX.X))
            op(tt(cmpt[:, :, :], wide(pk[:, :], 7), bc(steps7[:, :].unsqueeze(1), [P, 2 * NT, 7]), ALU.is_ge))
            op(vec.reduce_sum(bx[:, :], cmpt[:, :, :], AX.X))
            op(vec.scalar_tensor_tensor(slot[:, :], bx[:, :], -float(BLK), pk[:, :], ALU.mult, ALU.add))
            op(tt(blk[:, :], bk[:, :], bx[:, :], ALU.add))
            op(tt(blk[:, :], blk[:, :], ek[:, :], ALU.subtract))
            op(ts(tmp[:, :], bx[:, :], 1.0, None, ALU.is_ge))
            op(tt(blk[:, :], blk[:, :], tmp[:, :], ALU.mult))
            op(tt(blk[:, :], blk[:, :], ek[:, :], ALU.add))
            op(vec.scalar_tensor_tensor(flat(dest), blk[:, :], float(BLK), slot[:, :], ALU.mult, ALU.add))
            for j in range(2 * NT):
                step.did(ts(slot_hot[:, j, :], iota_s[:, :], slot[:, j:j + 1], None, ALU.is_equal))
                step.did(ts(block_hot[:, j, :], iota_b[:, :], blk[:, j:j + 1], token[:, j % NT:j % NT + 1],
                            ALU.is_equal, ALU.mult))
            step.settle()
            vec.nop().then_inc(s_hot, 1)
            one = slice(0, 1)
            op(tt(over[:, :, :], bc(incl[one, :].unsqueeze(1), [1, OVER, EXPERTS]),
                  bc(iota32[one, 0:OVER].unsqueeze(2), [1, OVER, EXPERTS]), ALU.is_le))
            op(vec.reduce_sum(over_f[:, :], over[:, :, :], AX.X))
            op(ts(over_e[:, 0:OVER], over_f[:, :], float(EXPERTS - 1), None, ALU.min))
            op(vec.tensor_copy(over_n[:, :], incl[one, EXPERTS - 1:EXPERTS]))
            vec.wait_ge(s_rows, 1)
            op(vec.tensor_copy(row_tok[:, :], ps[:, 2, 0:NBLK]))

        @block.tensor
        def _(pe):
            pe.wait_ge(s_tri, 1)
            pe.wait_ge(s_cum, 1)
            cols = ps[:, 0, 0:NT * EXPERTS]
            pe.matmul(cols, tri[:, :], both[:, :, :].rearrange("p t e -> p (t e)"), start=True, stop=False)
            pe.matmul(cols, ones[:, :], before[:, :, :].rearrange("p t e -> p (t e)"), start=False, stop=True)
            pe.matmul(ps[:, 1, 0:EXPERTS], ones[:, :], total[:, :], start=True, stop=True).then_inc(s_cum_ps, 1)
            pe.wait_ge(s_hot, 1)
            for j in range(2 * NT):
                last = pe.matmul(ps[:, 2, 0:NBLK], slot_hot[:, j, :], block_hot[:, j, :], start=j == 0, stop=j == 2 * NT - 1)
            last.then_inc(s_rows, 1)
    return dict(weights=weights, dest=dest, row_tok=row_tok, over_e=over_e, over_n=over_n)


def expert_block(nc, m, ins, dr, t):
    at, sem = m.at, m.sem
    ident, raw, s_raw = t["ident"], t["moe_raw"], t["s_moe"]
    row_tok, over_e, over_n = t["row_tok"], t["over_e"], t["over_n"]
    GU, DN = 4, 4
    gu_hi, gu_lo = at("gu_hi", [P, GU, 2, HALF], 32, F32R), at("gu_lo", [P, GU, 2, HALF], 48, F32R)
    dn_hi, dn_lo = at("dn_hi", [P, DN, 2, HALF], 64, F32R), at("dn_lo", [P, DN, 2, HALF], 80, F32R)
    xg = at("x_gathered", [P, D], 96)
    xt_hi, xt_lo = at("moe_x_hi", [P, KD, P], 100, F32R), at("moe_x_lo", [P, KD, P], 104, F32R)
    sg, hid = at("moe_sig", [P, HALF], 108), at("moe_hid", [P, HALF], 110)
    ht_hi, ht_lo = at("moe_h_hi", [P, KF, P], 112, F32R), at("moe_h_lo", [P, KF, P], 114, F32R)
    y = at("moe_y", [P, D], 116)
    names = ("gu_hi", "gu_lo", "gu_used", "dn_hi", "dn_lo", "dn_used", "xg", "xt", "xt_hi", "xt_lo", "sig",
             "t", "hid", "ht", "ht_hi", "ht_lo", "y", "y_out")
    (s_gu_hi, s_gu_lo, s_gu_used, s_dn_hi, s_dn_lo, s_dn_used, s_xg, s_xt, s_xt_hi, s_xt_lo, s_sig, s_t,
     s_hid, s_ht, s_ht_hi, s_ht_lo, s_y, s_y_out) = (sem(f"g_{n}") for n in names)
    G, U, DOWN, HT, XT = 0, 1, 2, 4, 5
    LAST = EXPERTS - 1
    gate_up = lambda k: raw[:, 2 * (k // 4):2 * (k // 4) + 2, (k % 4) * HALF:(k % 4 + 1) * HALF]
    down = lambda k: raw[:, 4 + k // 2, (k % 2) * D:(k % 2 + 1) * D].rearrange("p (h f) -> p h f", h=2)
    weight_v = [ins[n][0].rearrange("e (k p) f -> e p k f", p=P) for n in ("w_expert_gate", "w_expert_up", "w_expert_down")]

    def load(eng, j, expert):
        if j < 4:
            src, n, w = weight_v[j % 2], slice(4 * (j // 2), 4 * (j // 2) + 4), 4
        else:
            src, n, w = weight_v[2], slice(2 * (j - 4), 2 * (j - 4) + 2), 2
        eng.dma_start(raw[:, j, :].rearrange("p (k f) -> p k f", k=w),
                      src[bass.ds(expert, 1), :, n, :].rearrange("o p k f -> (o p) k f")).then_inc(s_raw[j], 16)

    def load_gate_up(eng, e, expert):
        for j in range(4):
            eng.wait_ge(s_gu_lo, e * 8 + (-4 if j < 2 else 0))
            load(eng, j, expert)

    def load_down(eng, e, expert):
        for j in (4, 5):
            eng.wait_ge(s_dn_lo, e * 4 + (2 if j == 4 else 4))
            load(eng, j, expert)

    def store(eng, e):
        eng.wait_ge(s_y, e + 2)
        eng.dma_start(dr["yr"][bass.ds(e * BLK, BLK), :], y[:, :]).then_inc(s_y_out, 16)

    def overflow(eng, body):
        n_over = eng.value_load(over_n[0:1, 0:1], min_val=0, max_val=OVER)
        with eng.Fori(0, OVER) as b:
            with eng.If(n_over > b):
                body(b)

    with ExitStack() as local:
        ps = local.enter_context(nc.psum_tensor("g_ps", [P, 8, HALF], F32))
        block = local.enter_context(nc.Block())

        @block.sync
        def _(sp):
            load_gate_up(sp, 1, 1)
            load_down(sp, 0, 0)
            with sp.Fori(3, LAST + 2) as i:
                load_gate_up(sp, i - 1, i - 1)
                load_down(sp, i - 2, i - 2)
                store(sp, i - 3)
            load_down(sp, LAST, LAST)
            store(sp, LAST - 1)
            store(sp, LAST)
            sp.wait_ge(s_y_out, 16 * (1 + EXPERTS))

        @block.gpsimd
        def _(gp):
            def gather(e):
                gp.wait_ge(s_xt, e + 1)
                gp.indirect_dma_start(out=xg[:, :], out_offset=None, in_=dr["xt"],
                                      in_offset=bass.IndirectOffsetOnAxis(ap=row_tok[:, e:e + 1].bitcast(U32), axis=0)
                                      ).then_inc(s_xg, 16)

            for e in range(EXPERTS):
                gather(e)
            n_over = gp.value_load(over_n[0:1, 0:1], min_val=0, max_val=OVER)
            for b in range(OVER):
                with gp.If(n_over > b):
                    gather(EXPERTS + b)
                    gp.wait_ge(s_y_out, 16 * (EXPERTS + b + 2))

        @block.scalar
        def _(act):
            act.nop().then_inc(s_y_out, 16)

            def gu_high(e, k):
                for j in (0, 1):
                    act.wait_ge(s_raw[2 * (k // 4) + j], e * 16 + 16)
                act.wait_ge(s_gu_used, e * 8 + (k + 1))
                act.activation(gu_hi[:, k % GU, :, :], gate_up(k), ACT.Copy).then_inc(s_gu_hi, 1)

            def dn_high(e, k):
                act.wait_ge(s_raw[4 + k // 2], e * 16 + 16)
                act.wait_ge(s_dn_used, e * 4 + (k + 1))
                act.activation(dn_hi[:, k, :, :], down(k), ACT.Copy).then_inc(s_dn_hi, 1)

            def sigmoid(e):
                act.wait_ge(s_gu_used, e * 8 + 12)
                act.wait_ge(s_hid, e + 1)
                act.activation(sg[:, :], ps[:, G, :], ACT.Sigmoid).then_inc(s_sig, 1)

            def x_high(e):
                act.wait_ge(s_xt, e + 2)
                act.activation(xt_hi[:, :, :].rearrange("p (b k) c -> p b (k c)", b=2), ps[:, XT:XT + 2, :],
                               ACT.Copy).then_inc(s_xt_hi, 1)

            def h_high(e):
                act.wait_ge(s_ht, e + 1)
                act.activation(ht_hi[:, :, :].rearrange("p k c -> p (k c)"), ps[:, HT, :], ACT.Copy).then_inc(s_ht_hi, 1)

            def y_out(e):
                act.wait_ge(s_dn_used, e * 4 + 8)
                act.wait_ge(s_y_out, e * 16 + 16)
                act.activation(y[:, :].rearrange("p (b f) -> p b f", b=2), ps[:, DOWN:DOWN + 2, :], ACT.Copy).then_inc(s_y, 1)

            def body(e, first=False, last=False):
                for k in range(2, KD):
                    gu_high(e, k)
                if not first:
                    for k in range(KF):
                        dn_high(e - 1, k)
                sigmoid(e)
                if not last:
                    x_high(e + 1)
                    gu_high(e + 1, 0)
                    gu_high(e + 1, 1)
                if not first:
                    y_out(e - 1)
                h_high(e)

            gu_high(0, 0)
            gu_high(0, 1)
            x_high(0)
            body(0, first=True)
            with act.Fori(1, LAST) as e:
                body(e)
            body(LAST, last=True)
            for k in range(KF):
                dn_high(LAST, k)
            y_out(LAST)

            def extra(b):
                e = b + EXPERTS
                expert = act.value_load(over_e[0:1, bass.ds(b, 1)], min_val=0, max_val=LAST)
                load_gate_up(act, e, expert)
                load_down(act, e, expert)
                x_high(e)
                for k in range(KD):
                    gu_high(e, k)
                sigmoid(e)
                for k in range(KF):
                    dn_high(e, k)
                h_high(e)
                y_out(e)
                store(act, e)

            overflow(act, extra)

        @block.vector
        def _(vec):
            vec.nop().then_inc(s_dn_lo, 4)
            vec.nop().then_inc(s_hid, 1)

            def gu_low(e, k):
                vec.wait_ge(s_gu_hi, e * 8 + (k + 1))
                vec.tensor_tensor(gu_lo[:, k % GU, :, :], gate_up(k), gu_hi[:, k % GU, :, :].bitcast(F32),
                                  ALU.subtract).then_inc(s_gu_lo, 1)

            def dn_low(e, k):
                vec.wait_ge(s_dn_hi, e * 4 + (k + 1))
                vec.tensor_tensor(dn_lo[:, k, :, :], down(k), dn_hi[:, k, :, :].bitcast(F32), ALU.subtract).then_inc(s_dn_lo, 1)

            def hidden(e):
                vec.wait_ge(s_sig, e + 1)
                vec.tensor_tensor(hid[:, :], ps[:, G, :], sg[:, :], ALU.mult).then_inc(s_t, 1)
                vec.wait_ge(s_t, e + 1)
                vec.tensor_tensor(hid[:, :], ps[:, U, :], hid[:, :], ALU.mult).then_inc(s_hid, 1)

            def x_low(e):
                vec.wait_ge(s_xt_hi, e + 1)
                vec.tensor_tensor(xt_lo[:, :, :].rearrange("p (b k) c -> p b (k c)", b=2), ps[:, XT:XT + 2, :],
                                  xt_hi[:, :, :].rearrange("p (b k) c -> p b (k c)", b=2).bitcast(F32),
                                  ALU.subtract).then_inc(s_xt_lo, 1)

            def h_low(e):
                vec.wait_ge(s_ht_hi, e + 1)
                vec.tensor_tensor(ht_lo[:, :, :].rearrange("p k c -> p (k c)"), ps[:, HT, :],
                                  ht_hi[:, :, :].rearrange("p k c -> p (k c)").bitcast(F32), ALU.subtract).then_inc(s_ht_lo, 1)

            def body(e, first=False, last=False):
                for k in range(2, KD):
                    gu_low(e, k)
                if not first:
                    for k in range(KF):
                        dn_low(e - 1, k)
                hidden(e)
                if not last:
                    x_low(e + 1)
                    gu_low(e + 1, 0)
                    gu_low(e + 1, 1)
                h_low(e)

            gu_low(0, 0)
            gu_low(0, 1)
            x_low(0)
            body(0, first=True)
            with vec.Fori(1, LAST) as e:
                body(e)
            body(LAST, last=True)
            for k in range(KF):
                dn_low(LAST, k)

            def extra(b):
                e = b + EXPERTS
                x_low(e)
                for k in range(KD):
                    gu_low(e, k)
                hidden(e)
                for k in range(KF):
                    dn_low(e, k)
                h_low(e)

            overflow(vec, extra)

        @block.tensor
        def _(pe):
            pe.nop().then_inc(s_gu_used, 4)
            pe.nop().then_inc(s_dn_used, 4)
            pe.nop().then_inc(s_xt, 1)
            pe.nop().then_inc(s_y, 1)

            def x_transposes(e):
                pe.wait_ge(s_xg, e * 16 + 16)
                for k in range(KD):
                    last = pe.transpose(ps[:, XT + k // 4, (k % 4) * P:(k % 4 + 1) * P], xg[:, k * P:(k + 1) * P], ident[:, :])
                last.then_inc(s_xt, 1)

            def gate_up_products(e):
                pe.wait_ge(s_xt_lo, e + 1)
                pe.wait_ge(s_hid, e + 1)
                for k in range(KD):
                    pe.wait_ge(s_gu_lo, e * 8 + (k + 1))
                    s, first, final = k % GU, k == 0, k == KD - 1
                    for i in (G, U):
                        pe.matmul(ps[:, i, :], xt_hi[:, k, :], gu_hi[:, s, i, :], start=first, stop=False)
                        pe.matmul(ps[:, i, :], xt_hi[:, k, :], gu_lo[:, s, i, :], start=False, stop=False)
                    for i in (G, U):
                        last = pe.matmul(ps[:, i, :], xt_lo[:, k, :], gu_hi[:, s, i, :], start=False, stop=final)
                    last.then_inc(s_gu_used, 1)

            def h_transposes(e):
                pe.wait_ge(s_hid, e + 2)
                for k in range(KF):
                    last = pe.transpose(ps[:, HT, k * P:(k + 1) * P], hid[:, k * P:(k + 1) * P], ident[:, :])
                last.then_inc(s_ht, 1)

            def down_products(e):
                pe.wait_ge(s_ht_lo, e + 1)
                pe.wait_ge(s_y, e + 1)
                for k in range(KF):
                    pe.wait_ge(s_dn_lo, e * 4 + (k + 5))
                    first, final = k == 0, k == KF - 1
                    for i in range(2):
                        pe.matmul(ps[:, DOWN + i, :], ht_hi[:, k, :], dn_hi[:, k, i, :], start=first, stop=False)
                        pe.matmul(ps[:, DOWN + i, :], ht_hi[:, k, :], dn_lo[:, k, i, :], start=False, stop=False)
                    for i in range(2):
                        last = pe.matmul(ps[:, DOWN + i, :], ht_lo[:, k, :], dn_hi[:, k, i, :], start=False, stop=final)
                    last.then_inc(s_dn_used, 1)

            x_transposes(0)
            gate_up_products(0)
            x_transposes(1)
            h_transposes(0)
            with pe.Fori(1, LAST) as e:
                gate_up_products(e)
                x_transposes(e + 1)
                down_products(e - 1)
                h_transposes(e)
            gate_up_products(LAST)
            down_products(LAST - 1)
            h_transposes(LAST)
            down_products(LAST)

            def extra(b):
                e = b + EXPERTS
                x_transposes(e)
                gate_up_products(e)
                h_transposes(e)
                down_products(e)

            overflow(pe, extra)
    return {}


def output_block(nc, m, ins, dr, t, out):
    at, sem = m.at, m.sem
    ident, h, weights, dest = t["ident"], t["h"], t["weights"], t["dest"]
    wg_hi, wg_lo = at("wg_hi", [P, KD, D], 32, F32R), at("wg_lo", [P, KD, D], 64, F32R)
    wp_hi, wp_lo = at("wp_hi", [P, KP, D], 96, F32R), at("wp_lo", [P, KP, D], 104, F32R)
    wraw = at("ple_raw", [P, 2, D], 112)
    y12 = at("y12", [P, 2, D], 120)
    xn = at("ple_xn", [P, D], 128)
    xt_hi, xt_lo = at("ple_x_hi", [P, 2, KD, P], 132, F32R), at("ple_x_lo", [P, 2, KD, P], 140, F32R)
    p_rows = at("p_rows", [P, 2, PLE], 148)
    pt_hi, pt_lo = at("p_hi", [P, 2, KP, P], 150, F32R), at("p_lo", [P, 2, KP, P], 152, F32R)
    sig, prod = at("ple_sig", [P, 2, HALF], 154), at("ple_prod", [P, 2, HALF], 158)
    rows_out = at("rows_out", [P, 2, D], 162)
    g_ple, g_fin = at("g_ple", [P, D], 170), at("g_final", [P, D], 174)
    junk = at("h_junk", [P, D], 178)
    ssq, rstd = at("h_ssq", [P, 2], 182), at("h_rstd", [P, 2], 182.125)
    ssq2, rstd2 = at("h_ssq2", [P, 2], 182.25), at("h_rstd2", [P, 2], 182.375)
    w_now = at("h_w", [P, 2], 182.625)
    s_wraw, s_p, s_out = ([sem(f"h_{n}{s}") for s in range(2)] for n in ("wraw", "p", "out"))
    names = ("par", "whi", "wsplit", "y1", "y2", "h1", "inv", "rstd", "xn", "xt", "x_hi", "x_lo",
             "mm", "sig", "h2", "inv2", "rstd2", "rows", "v_step", "a_step")
    (s_par, s_whi, s_wsplit, s_y1, s_y2, s_h1, s_inv, s_rstd, s_xn, s_xt, s_x_hi, s_x_lo, s_mm,
     s_sig, s_h2, s_inv2, s_rstd2, s_rows, v_step, a_step) = (sem(f"h_{n}") for n in names)
    XT, PT, GATE, PRJ = 0, 2, 4, 6
    row = lambda n: h[:, bass.ds(n, 1), :].rearrange("p o d -> p (o d)")

    with ExitStack() as local:
        ps = local.enter_context(nc.psum_tensor("h_ps", [P, 8, HALF], F32))
        block = local.enter_context(nc.Block())

        @block.sync
        def _(sp):
            p_v = ins["p"][0, 0].rearrange("(c t) e -> c t e", t=NT)
            out_v = out[0].rearrange("(c t) d -> c t d", t=NT)

            def load(n, s):
                sp.wait_ge(s_x_lo, n + 1)
                sp.dma_start(p_rows[:, s, :], p_v[:, bass.ds(n, 1), :].rearrange("c o e -> c (o e)")).then_inc(s_p[s], 16)

            def store(n, s):
                sp.wait_ge(s_rows, n + 1)
                sp.dma_start(out_v[:, bass.ds(n, 1), :].rearrange("c o d -> c (o d)"), rows_out[:, s, :]).then_inc(s_out[s], 16)

            load(0, 0)
            load(1, 1)
            for k in range(KD + KP):
                if k >= 2:
                    sp.wait_ge(s_wsplit, k - 1)
                src = ins["w_ple_gate"][0, k * P:(k + 1) * P, :] if k < KD else ins["w_ple_proj"][0, (k - KD) * P:(k - KD + 1) * P, :]
                sp.dma_start(wraw[:, k % 2, :], src).then_inc(s_wraw[k % 2], 16)
            load(2, 0)
            with sp.Fori(1, (NT - 4) // 2 + 1) as i:
                load(i * 2 + 1, 1)
                store(i * 2 - 2, 0)
                load(i * 2 + 2, 0)
                store(i * 2 - 1, 1)
            load(NT - 1, 1)
            for n in range(NT - 4, NT):
                store(n, n % 2)
            for s in range(2):
                sp.wait_ge(s_out[s], 16 * (1 + NT // 2))

        @block.gpsimd
        def _(gp):
            for n in range(NT):
                gp.wait_ge(s_h1, n + 1)
                for e, done in enumerate((s_y1, s_y2)):
                    gp.indirect_dma_start(out=y12[:, e, :], out_offset=None, in_=dr["yr"],
                                          in_offset=bass.IndirectOffsetOnAxis(ap=dest[:, e, n:n + 1].bitcast(U32), axis=0)
                                          ).then_inc(done, 16)

        @block.scalar
        def _(act):
            act.dma_start(g_ple[:, :], ins["norm_ple"][0].partition_broadcast(P)).then_inc(s_par, 16)
            act.dma_start(g_fin[:, :], ins["norm_final"].partition_broadcast(P)).then_inc(s_par, 16)
            for s in range(2):
                act.nop().then_inc(s_out[s], 16)

            def norm(n, s):
                act.wait_ge(s_inv, n + 1)
                act.activation(rstd[:, s:s + 1], rstd[:, s:s + 1], ACT.Sqrt).then_inc(s_rstd, 1)
                act.wait_ge(s_xt, n + 1)
                act.wait_ge(s_mm, n * 2 + 2)
                act.activation(xt_hi[:, s, :, :].rearrange("p (b k) c -> p b (k c)", b=2), ps[:, XT:XT + 2, :],
                               ACT.Copy).then_inc(s_x_hi, 1)
                act.activation(pt_hi[:, s, :, :], ps[:, PT, 0:KP * P].rearrange("p (k c) -> p k c", k=KP),
                               ACT.Copy).then_inc(s_x_hi, 1)

            def finish(n, s):
                for half in range(2):
                    act.wait_ge(s_mm, n * 2 + (5 + half))
                    act.wait_ge(s_h2, n * 2 + (half + 1))
                    act.activation(sig[:, half, :], ps[:, GATE + half, :], ACT.Sigmoid).then_inc(s_sig, 1)
                act.wait_ge(s_inv2, n + 1)
                act.activation(rstd2[:, s:s + 1], rstd2[:, s:s + 1], ACT.Sqrt).then_inc(s_rstd2, 1)

            for k in range(KD + KP):
                act.wait_ge(s_wraw[k % 2], 16 * (k // 2 + 1))
                hi = wg_hi[:, k, :] if k < KD else wp_hi[:, k - KD, :]
                act.activation(hi, wraw[:, k % 2, :], ACT.Copy).then_inc(s_whi, 1)
            tile_pair_loop(act, norm, finish)

        @block.vector
        def _(vec):
            step = Counted(vec, v_step)
            vec.nop().then_inc(s_h1, 1)
            vec.nop().then_inc(s_x_lo, 2)
            vec.nop().then_inc(s_h2, 2)
            for k in range(KD + KP):
                vec.wait_ge(s_whi, k + 1)
                hi, lo = (wg_hi[:, k, :], wg_lo[:, k, :]) if k < KD else (wp_hi[:, k - KD, :], wp_lo[:, k - KD, :])
                vec.tensor_tensor(lo, wraw[:, k % 2, :], hi.bitcast(F32), ALU.subtract).then_inc(s_wsplit, 1)
            vec.wait_ge(s_par, 32)

            def inverse_mean_square(n, scratch, total, dst, done):
                step.did(vec.scalar_tensor_tensor(scratch, row(n), 1.0, row(n), ALU.mult, ALU.mult, accum_out=total))
                step.settle()
                step.did(vec.tensor_scalar(dst, total, 1.0 / D, EPS, ALU.mult, ALU.add))
                step.settle()
                vec.reciprocal(dst, dst).then_inc(done, 1)

            def combine(n, s):
                vec.wait_ge(s_y1, n * 16 + 16)
                vec.wait_ge(s_y2, n * 16 + 16)
                step.did(vec.tensor_copy(w_now[:, :].unsqueeze(2), weights[:, :, bass.ds(n, 1)]))
                step.settle()
                step.did(vec.scalar_tensor_tensor(row(n), y12[:, 0, :], w_now[:, 0:1], row(n), ALU.mult, ALU.add))
                step.settle()
                vec.scalar_tensor_tensor(row(n), y12[:, 1, :], w_now[:, 1:2], row(n), ALU.mult, ALU.add).then_inc(s_h1, 1)
                vec.wait_ge(s_h1, n + 2)
                inverse_mean_square(n, junk[:, :], ssq[:, s:s + 1], rstd[:, s:s + 1], s_inv)
                vec.wait_ge(s_rstd, n + 1)
                vec.scalar_tensor_tensor(xn[:, :], row(n), rstd[:, s:s + 1], g_ple[:, :], ALU.mult, ALU.mult).then_inc(s_xn, 1)
                vec.wait_ge(s_x_hi, n * 2 + 2)
                step.did(vec.tensor_tensor(xt_lo[:, s, :, :].rearrange("p (b k) c -> p b (k c)", b=2), ps[:, XT:XT + 2, :],
                                  xt_hi[:, s, :, :].rearrange("p (b k) c -> p b (k c)", b=2).bitcast(F32), ALU.subtract))
                step.settle()
                vec.tensor_tensor(pt_lo[:, s, :, :], ps[:, PT, 0:KP * P].rearrange("p (k c) -> p k c", k=KP),
                                  pt_hi[:, s, :, :].bitcast(F32), ALU.subtract).then_inc(s_x_lo, 1)

            def gate(n, s):
                for half in range(2):
                    col = slice(half * HALF, (half + 1) * HALF)
                    vec.wait_ge(s_sig, n * 2 + (half + 1))
                    step.did(vec.tensor_tensor(prod[:, half, :], ps[:, PRJ + half, :], sig[:, half, :], ALU.mult))
                    step.settle()
                    vec.tensor_tensor(row(n)[:, col], row(n)[:, col], prod[:, half, :], ALU.add).then_inc(s_h2, 1)
                vec.wait_ge(s_h2, n * 2 + 4)
                inverse_mean_square(n, junk[:, :], ssq2[:, s:s + 1], rstd2[:, s:s + 1], s_inv2)
                vec.wait_ge(s_rstd2, n + 1)
                vec.wait_ge(s_out[s], n * 8 + (16 - 8 * s))
                vec.scalar_tensor_tensor(rows_out[:, s, :], row(n), rstd2[:, s:s + 1], g_fin[:, :], ALU.mult,
                                         ALU.mult).then_inc(s_rows, 1)

            PER = 2 * (5 + 4)
            tile_pair_loop(vec, combine, gate, step, PER)

        @block.tensor
        def _(pe):
            pe.nop().then_inc(s_mm, 4)

            def transposes(n, s):
                pe.wait_ge(s_p[s], n * 8 + (16 - 8 * s))
                pe.wait_ge(s_x_lo, n + 2)
                for k in range(KP):
                    pe.transpose(ps[:, PT, k * P:(k + 1) * P], p_rows[:, s, k * P:(k + 1) * P], ident[:, :])
                pe.wait_ge(s_xn, n + 1)
                for k in range(KD):
                    last = pe.transpose(ps[:, XT + k // 4, (k % 4) * P:(k % 4 + 1) * P], xn[:, k * P:(k + 1) * P], ident[:, :])
                last.then_inc(s_xt, 1)

            def products(n, s, ahead=True):
                pe.wait_ge(s_x_lo, n + 3)
                for half in range(2):
                    col = slice(half * HALF, (half + 1) * HALF)
                    pe.wait_ge(s_h2, n * 2 + (half + 1))
                    for hi, lo, w_hi, w_lo, depth, bank in ((pt_hi, pt_lo, wp_hi, wp_lo, KP, PRJ),
                                                            (xt_hi, xt_lo, wg_hi, wg_lo, KD, GATE)):
                        dst = ps[:, bank + half, :]
                        for k in range(depth):
                            if ahead and half == 1 and bank == GATE and k == KD // 2:
                                transposes(n + 1, 1 - s)
                            pe.matmul(dst, hi[:, s, k, :], w_hi[:, k, col], start=k == 0, stop=False)
                            pe.matmul(dst, hi[:, s, k, :], w_lo[:, k, col], start=False, stop=False)
                            last = pe.matmul(dst, lo[:, s, k, :], w_hi[:, k, col], start=False, stop=k == depth - 1)
                    last.then_inc(s_mm, 1)

            transposes(0, 0)
            pe.wait_ge(s_wsplit, KD + KP)
            with pe.Fori(0, NT // 2 - 1) as i:
                products(i * 2, 0)
                products(i * 2 + 1, 1)
            products(NT - 2, 0)
            products(NT - 1, 1, ahead=False)


def build(nc, ins, out):
    m = Map(nc)
    shapes = dict(kpad=(GC, GROUPS, 15 * GC), proj=(3 * S5W, SEQ), y=(S5W, SEQ), merged=(D, SEQ), xt=(SEQ, D),
                  yr=(NBLK * BLK, D))
    dr = {n: nc.dram_tensor(f"scratch_{n}", s, F32, kind="Internal").ap() for n, s in shapes.items()}
    t = setup_block(nc, m, ins, dr)
    project_block(nc, m, ins, dr, t)
    t |= gating_block(nc, m, ins, dr, t)
    merge_block(nc, m, ins, dr, t)
    m.reuse_semaphores()
    t |= mixer_out_block(nc, m, ins, dr, t)
    t |= routing_block(nc, m, ins, dr, t)
    expert_block(nc, m, ins, dr, t)
    output_block(nc, m, ins, dr, t, out)


_INS = ["x", "p", "norm_mix", "w_in", "s5_a_re", "s5_a_im", "s5_log_dt", "s5_b_re", "s5_b_im", "s5_c_re", "s5_c_im",
        "s5_d", "w_glu", "sgu_norm", "sgu_w", "sgu_b", "w_sgu_proj", "w_out", "norm_ffn", "w_router_group",
        "b_router_group", "w_router_expert", "b_router_expert", "w_expert_gate", "w_expert_up",
        "w_expert_down", "norm_ple", "w_ple_gate", "w_ple_proj", "norm_final"]


def kernel(**inputs):
    import numpy as np
    import concourse.bacc as bacc
    from concourse.bass_utils import run_bass_kernel_spmd

    nc = bacc.Bacc("TRN2", target_bir_lowering=False, num_devices=1)
    arrays, ins = {}, {}
    for name in _INS:
        a = np.ascontiguousarray(inputs[name])
        arrays[f"in_{name}"] = a
        ins[name] = nc.dram_tensor(f"in_{name}", a.shape, mybir.dt.from_np(a.dtype), kind="ExternalInput").ap()
    out = nc.dram_tensor("out_0", (1, SEQ, D), F32, kind="ExternalOutput").ap()
    build(nc, ins, out)
    return run_bass_kernel_spmd(nc, [arrays], core_ids=[0]).results[0]["out_0"]
```

```python
import math
from contextlib import ExitStack

import concourse.bass as bass
from concourse import mybir
from concourse.alu_op_type import AluOpType as ALU

F32, F32R, I32, U32 = mybir.dt.float32, mybir.dt.float32r, mybir.dt.int32, mybir.dt.uint32
ACT = mybir.ActivationFunctionType
AX = mybir.AxisListType

P = 128
D = 1024
KD = D // P
SEQ = 1024
NT = SEQ // P
HALF = 512
S5W, GROUPS, GC, NS = 512, 32, 16, 64
PAIRS = GROUPS // 2
FT = S5W // P
HEADS = 4
SC = P // NT
EXPERTS, NGRP, EPG, FE = 32, 4, 8, 512
KF = FE // P
BLK = 112
OVER = (2 * SEQ - 2) // BLK
STEPS = (SEQ - 1) // BLK
NBLK = EXPERTS + OVER
PLE = 256
KP = PLE // P
EPS = 1e-6
MAGIC = 12582912.0
LN2HI, LN2LO = 0.693359375, -2.12194440e-4
PI2A, PI2B, PI2C = 6.28125, 1.9350051879882812e-3, 3.0199159819e-7
GELU_A, GELU_B = 0.044715, 2.0 * math.sqrt(2.0 / math.pi)


class Counted:

    def __init__(self, eng, sem):
        self.eng, self.sem, self.base, self.n = eng, sem, 0, 0

    def did(self, ins):
        self.n += 1
        return ins.then_inc(self.sem, 1)

    def settle(self):
        self.eng.wait_ge(self.sem, self.base + self.n)

    def loop_body(self, i, per):
        self.start, self.base, self.n, self.per = self.base + self.n, self.base + self.n + i * per, 0, per

    def loop_end(self, turns):
        assert self.n == self.per, (self.n, self.per)
        self.base, self.n = self.start + turns * self.per, 0


class Map:

    def __init__(self, nc):
        self.nc, self.sems = nc, []
        self.origin = (nc.sbuf_base + 31) // 32 * 32

    def at(self, name, shape, kib, dt=F32):
        return self.nc.alloc_sbuf_tensor_at(name, shape, dt, offset=self.origin + int(kib * 1024))

    def sem(self, name):
        self.sems.append(self.nc.alloc_semaphore(name))
        return self.sems[-1]

    def reuse_semaphores(self):
        self.nc.clear_and_free_semaphores(self.sems)
        self.nc.all_engine_barrier()
        self.sems = []


def bc(ap, shape):
    return ap.to_broadcast(shape)


def tile_pair_loop(eng, first, second, counted=None, per=0):
    first(0, 0)
    with eng.Fori(0, NT // 2 - 1) as i:
        if counted:
            counted.loop_body(i, per)
        first(i * 2 + 1, 1)
        second(i * 2, 0)
        first(i * 2 + 2, 0)
        second(i * 2 + 1, 1)
    if counted:
        counted.loop_end(NT // 2 - 1)
    first(NT - 1, 1)
    second(NT - 2, 0)
    second(NT - 1, 1)


def complex_product(eng, step, out_re, out_im, a_re, a_im, b_re, b_im, tmp0, tmp1):
    step.did(eng.tensor_tensor(tmp0, a_re, b_re, ALU.mult))
    step.did(eng.tensor_tensor(tmp1, a_im, b_im, ALU.mult))
    step.settle()
    step.did(eng.tensor_tensor(out_re, tmp0, tmp1, ALU.subtract))
    step.settle()
    step.did(eng.tensor_tensor(tmp0, a_re, b_im, ALU.mult))
    step.did(eng.tensor_tensor(tmp1, a_im, b_re, ALU.mult))
    step.settle()
    step.did(eng.tensor_tensor(out_im, tmp0, tmp1, ALU.add))
    step.settle()


def unit_length(eng, step, c, s, tmp0, tmp1):
    step.did(eng.tensor_tensor(tmp0, c, c, ALU.mult))
    step.did(eng.tensor_tensor(tmp1, s, s, ALU.mult))
    step.settle()
    step.did(eng.tensor_tensor(tmp0, tmp0, tmp1, ALU.add))
    step.settle()
    step.did(eng.tensor_scalar(tmp0, tmp0, -0.5, 1.5, ALU.mult, ALU.add))
    step.settle()
    step.did(eng.tensor_tensor(c, c, tmp0, ALU.mult))
    step.did(eng.tensor_tensor(s, s, tmp0, ALU.mult))
    step.settle()


def exponential(vec, step, out, x, t0, t1, t2, whole):
    def op(ins):
        step.did(ins)
        step.settle()
    op(vec.tensor_scalar(t0, x, -87.0, 88.0, ALU.max, ALU.min))
    op(vec.tensor_scalar(t1, t0, 1.0 / math.log(2.0), MAGIC, ALU.mult, ALU.add))
    op(vec.tensor_scalar(t1, t1, MAGIC, None, ALU.subtract))
    op(vec.scalar_tensor_tensor(t0, t1, -LN2HI, t0, ALU.mult, ALU.add))
    op(vec.scalar_tensor_tensor(t0, t1, -LN2LO, t0, ALU.mult, ALU.add))
    op(vec.tensor_scalar(t2, t0, 1.0 / math.factorial(7), None, ALU.mult))
    for k in range(6, 0, -1):
        op(vec.scalar_tensor_tensor(t2, t2, 1.0 / math.factorial(k), t0, ALU.add, ALU.mult))
    op(vec.tensor_scalar(t2, t2, 1.0, None, ALU.add))
    op(vec.tensor_scalar(whole, t1, 127.0, None, ALU.add))
    op(vec.tensor_scalar(whole, whole, 23, None, ALU.logical_shift_left))
    op(vec.tensor_tensor(out, t2, whole.bitcast(F32), ALU.mult))


def setup_block(nc, m, ins, dr):
    at, sem = m.at, m.sem
    xn_hi = at("xn_hi", [P, KD, SEQ], 0, F32R)
    xn_lo = at("xn_lo", [P, KD, SEQ], 32, F32R)
    e_re = at("e_re", [P, PAIRS, P], 64)
    e_im = at("e_im", [P, PAIRS, P], 72)
    o_re = at("o_re", [P, PAIRS, 9, GC], 80)
    o_im = at("o_im", [P, PAIRS, 9, GC], 89)
    w_re = at("w_re", [P, PAIRS, P], 98)
    w_im = at("w_im", [P, PAIRS, P], 106)
    ident = at("ident", [P, P], 207.25)
    mag8 = at("mag8", [P, PAIRS], 196.5)
    kpad = at("kpad", [GC, GROUPS, 15 * GC], 114)
    x = at("x_rows", [P, NT, D], 146)
    t9a = at("t9a", [P, PAIRS * 9 * GC], 178)
    t9b = at("t9b", [P, PAIRS * 9 * GC], 187)
    par = at("par", [P, P], 196.75)
    ldt = at("ldt", [P, 2], 197.25)
    par_t = at("par_t", [P, 96], 197.5)
    small = at("small", [P, 24, PAIRS], 198)
    whole = at("whole", [P, PAIRS], 199.5, I32)
    pw_re = at("pw_re", [P, PAIRS, 9], 200)
    pw_im = at("pw_im", [P, PAIRS, 9], 200.75)
    b_re = at("b_re", [P, PAIRS, GC], 201.5)
    b_im = at("b_im", [P, PAIRS, GC], 202.5)
    bb_re = at("bb_re", [P, PAIRS, GC], 203.5)
    bb_im = at("bb_im", [P, PAIRS, GC], 204.5)
    c_re = at("c_re", [P, PAIRS, GC], 205.5)
    ssq = at("ssq", [P, NT], 206.75)
    rstd = at("rstd", [P, NT], 206.875)
    gmix = at("gmix", [P, KD], 207)
    c_im = at("c_im", [P, PAIRS, GC], 144)
    zk = at("zk", [P, 4, PAIRS], 145)
    craw = at("craw", [P, 2, FT, 2, NS], 114)
    wt0 = at("wt0", [P, PAIRS, 64], 146)
    wt1 = at("wt1", [P, PAIRS, 64], 150)
    TILES = FT + 1
    columns = [f * P for f in range(FT)] + [2 * S5W]
    p_raw = at("a_p_raw", [P, TILES, KD, P], 122)
    p_hi, p_lo = at("a_p_hi", [P, 2, KD, P], 154, F32R), at("a_p_lo", [P, 2, KD, P], 162, F32R)
    p_out = at("a_p_out", [P, 2, SEQ], 170)

    s_const, s_par, s_b, s_c, s_x, s_g = (sem(f"a_{n}") for n in ("const", "par", "b", "c", "x", "g"))
    v_step, g_step, a_step = sem("a_v_step"), sem("a_g_step"), sem("a_a_step")
    s_cleared, s_par_in, s_par_t = sem("a_cleared"), sem("a_par_in"), sem("a_par_t")
    s_ct, s_phase, s_sin, s_ang = sem("a_ct"), sem("a_phase"), sem("a_sin"), sem("a_ang")
    s_e_made, s_et, s_et_copied = sem("a_e_made"), sem("a_et"), sem("a_et_copied")
    s_k_ready, s_k, s_k_copied, s_kd = sem("a_k_ready"), sem("a_k"), sem("a_k_copied"), sem("a_kd")
    s_sq, s_inv, s_root, s_xs, s_xt, s_hi, s_lo = (sem(f"a_{n}") for n in ("sq", "inv", "root", "xs", "xt", "hi", "lo"))
    s_p_raw, s_p_hi, s_p_lo, s_p_mm, s_p_ev = (sem(f"a_p_{n}") for n in ("raw", "hi", "lo", "mm", "ev"))
    s_p_out = [sem(f"a_p_out{s}") for s in range(2)]
    next_raw, s_next_raw, s_powers = at("p_raw", [P, 2, KD, P], 146), [sem(f"b_raw{s}") for s in range(2)], sem("a_powers")

    def weights_low(eng, f):
        eng.wait_ge(s_p_hi, f + 1)
        eng.tensor_tensor(p_lo[:, f % 2, :, :], p_raw[:, f, :, :], p_hi[:, f % 2, :, :].bitcast(F32),
                          ALU.subtract).then_inc(s_p_lo, 1)

    P_BANK = (2, 6)

    with ExitStack() as local:
        ps = local.enter_context(nc.psum_tensor("a_ps", [P, 8, HALF], F32))
        block = local.enter_context(nc.Block())

        @block.sync
        def _(sp):
            xv = ins["x"][0].rearrange("(c p) d -> p c d", p=NT)
            for p in range(NT):
                sp.dma_start(x[:, p, :], xv[p]).then_inc(s_x, 16)
            sp.wait_ge(s_sq, 1)
            w_v = ins["w_in"][0].rearrange("(k p) c -> p k c", p=P)
            for f, col in enumerate(columns):
                sp.dma_start(p_raw[:, f, :, :], w_v[:, :, col:col + P]).then_inc(s_p_raw, 16)
            sp.wait_ge(s_powers, 1)
            for s in range(2):
                col = 2 * S5W + (s + 1) * P
                sp.dma_start(next_raw[:, s, :, :], w_v[:, :, col:col + P]).then_inc(s_next_raw[s], 16)
            sp.wait_ge(s_k_copied, GROUPS // 4)
            sp.dma_start(dr["kpad"], kpad[:, :, :]).then_inc(s_kd, 16)
            sp.wait_ge(s_kd, 16)

        @block.gpsimd
        def _(gp):
            step = Counted(gp, g_step)
            gp.memset(par[:, :], 0.0).then_inc(s_cleared, 1)
            step.did(gp.memset(ident[:, :], 0.0))
            step.settle()
            gp.affine_select(out=ident[:, :], in_=ident[:, :], compare_op=ALU.not_equal, fill=1.0, base=0,
                             pattern=[[-1, P]], channel_multiplier=1).then_inc(s_const, 1)
            step.did(gp.memset(w_re[:, :, 0:1], 1.0))
            step.did(gp.memset(w_im[:, :, 0:1], 0.0))
            step.settle()
            gp.wait_ge(s_xt, 2 * KD)
            gp.wait_ge(s_p_lo, 1)
            weights_low(gp, 1)
            gp.wait_ge(s_phase, 1)
            zr, zi, z2r, z2i = zk[:, 0, :], zk[:, 1, :], zk[:, 2, :], zk[:, 3, :]
            n = 1
            while n < P:
                shape = [P, PAIRS, n]
                complex_product(gp, step, w_re[:, :, n:2 * n], w_im[:, :, n:2 * n],
                                w_re[:, :, 0:n], w_im[:, :, 0:n],
                                bc(zr.unsqueeze(2), shape), bc(zi.unsqueeze(2), shape),
                                wt0[:, :, 0:n], wt1[:, :, 0:n])
                if 2 * n < P:
                    complex_product(gp, step, z2r, z2i, zr, zi, zr, zi, wt0[:, :, 0], wt1[:, :, 0])
                    unit_length(gp, step, z2r, z2i, wt0[:, :, 0], wt1[:, :, 0])
                    zr, zi, z2r, z2i = z2r, z2i, zr, zi
                if n in (4, 16, 32):
                    weights_low(gp, {4: 2, 16: 3, 32: 4}[n])
                n *= 2
            step.settle()
            gp.nop().then_inc(s_powers, 1)

        @block.scalar
        def _(act):
            step = Counted(act, a_step)
            act.wait_ge(s_cleared, 1)
            pair_rows = lambda a: a[0].rearrange("(q h) n -> q (h n)", h=2)
            act.dma_start(par[0:16, :], pair_rows(ins["s5_a_re"])).then_inc(s_par, 16)
            act.dma_start(par[32:48, :], pair_rows(ins["s5_a_im"])).then_inc(s_par, 16)
            act.dma_start(ldt[64:80, :], ins["s5_log_dt"][0].rearrange("(q h) -> q h", h=2)).then_inc(s_par, 16)
            for i, name in enumerate(("s5_c_re", "s5_c_im")):
                for h in range(2):
                    act.dma_start(craw[:, i, :, h, :],
                                  ins[name][0].rearrange("(f g) c n -> (g c) f n", f=FT)).then_inc(s_c, 16)
            with nc.allow_non_contiguous_dma(reason="short vectors, channels across partitions"):
                act.dma_start(gmix[:, :], ins["norm_mix"][0].rearrange("(k p) -> p k", p=P)).then_inc(s_g, 16)
            act.dma_start(b_re[:, :, :], ins["s5_b_re"][0].rearrange("(q h) n c -> (h n) q c", h=2)).then_inc(s_b, 16)
            act.dma_start(b_im[:, :, :], ins["s5_b_im"][0].rearrange("(q h) n c -> (h n) q c", h=2)).then_inc(s_b, 16)
            act.wait_ge(s_x, 16 * NT)
            for p in range(NT // 2):
                step.did(act.activation(t9a[:, 0:D], x[:, p, :], ACT.Square, accum_out=ssq[:, p:p + 1]))
                step.settle()
            act.nop().then_inc(s_sq, 1)
            act.wait_ge(s_inv, 1)
            act.activation(rstd[:, :], rstd[:, :], ACT.Sqrt).then_inc(s_root, 1)
            act.wait_ge(s_root, 1)
            for p in range(NT // 2):
                act.activation(x[:, p, :], x[:, p, :], ACT.Copy, scale=rstd[:, p:p + 1]).then_inc(s_xs, 1)
            act.wait_ge(s_g, 16)
            for n in range(2 * KD):
                k, half = n // 2, n % 2
                act.wait_ge(s_xt, n + 1)
                act.activation(xn_hi[:, k, half * HALF:(half + 1) * HALF], ps[:, n % 4, :], ACT.Copy,
                               scale=gmix[:, k:k + 1]).then_inc(s_hi, 1)
            act.wait_ge(s_ang, 1)
            step.did(act.activation(small[:, 2, :], small[:, 0, :], ACT.Sin))
            step.did(act.activation(small[:, 3, :], small[:, 1, :], ACT.Sin))
            step.settle()
            act.nop().then_inc(s_sin, 1)

            def weights_high(f):
                if f >= 2:
                    act.wait_ge(s_p_mm, 2 * f - 2)
                act.activation(p_hi[:, f % 2, :, :], p_raw[:, f, :, :], ACT.Copy).then_inc(s_p_hi, 1)

            act.wait_ge(s_xt, 2 * KD)
            act.wait_ge(s_p_raw, 16 * TILES)
            weights_high(0)
            weights_high(1)
            for f in range(TILES):
                if f >= 2:
                    act.wait_ge(s_p_out[f % 2], 16 * (f // 2))
                for half in range(2):
                    act.wait_ge(s_p_mm, 2 * f + half + 1)
                    act.activation(p_out[:, f % 2, half * HALF:(half + 1) * HALF], ps[:, P_BANK[f % 2] + half, :],
                                   ACT.Copy).then_inc(s_p_ev, 1)
                if f + 2 < TILES:
                    weights_high(f + 2)
                act.wait_ge(s_p_ev, 2 * f + 2)
                act.dma_start(dr["proj"][f * P:(f + 1) * P, :], p_out[:, f % 2, :]).then_inc(s_p_out[f % 2], 16)
            for s in range(2):
                act.wait_ge(s_p_out[s], 16 * ((TILES + 1 - s) // 2))

        @block.vector
        def _(vec):
            step = Counted(vec, v_step)

            def op(instruction):
                step.did(instruction)
                step.settle()

            tt, ts, stt = vec.tensor_tensor, vec.tensor_scalar, vec.scalar_tensor_tensor
            s = lambda i: small[:, i, :]
            vec.wait_ge(s_par, 48)
            op(vec.tensor_copy(par[64:80, :].rearrange("q (h n) -> q h n", h=2),
                               bc(ldt[64:80, :].unsqueeze(2), [16, 2, NS])))
            vec.nop().then_inc(s_par_in, 1)
            vec.wait_ge(s_par_t, 1)
            op(vec.tensor_copy(par_t[:, :], ps[:, 7, 0:96]))
            are, aim, ldt_t = par_t[:, 0:16], par_t[:, 32:48], par_t[:, 64:80]
            dt, mag, ang = s(4), s(5), s(6)
            exponential(vec, step, dt, ldt_t, s(10), s(11), s(12), whole[:, :])
            op(tt(s(13), are, dt, ALU.mult))
            exponential(vec, step, mag, s(13), s(10), s(11), s(12), whole[:, :])
            op(tt(ang, aim, dt, ALU.mult))
            op(ts(s(10), ang, 1.0 / (2.0 * math.pi), MAGIC, ALU.mult, ALU.add))
            op(ts(s(10), s(10), MAGIC, None, ALU.subtract))
            op(stt(s(0), s(10), -PI2A, ang, ALU.mult, ALU.add))
            op(stt(s(0), s(10), -PI2B, s(0), ALU.mult, ALU.add))
            op(stt(s(0), s(10), -PI2C, s(0), ALU.mult, ALU.add))
            op(ts(s(0), s(0), 3.1415925, -3.1415925, ALU.min, ALU.max))
            op(ts(s(1), s(0), 0.5, None, ALU.mult))
            vec.nop().then_inc(s_ang, 1)
            vec.wait_ge(s_x, 16 * NT)
            for p in range(NT // 2, NT):
                op(stt(t9b[:, 0:D], x[:, p, :], 1.0, x[:, p, :], ALU.mult, ALU.mult, accum_out=ssq[:, p:p + 1]))
            vec.wait_ge(s_sq, 1)
            op(ts(rstd[:, :], ssq[:, :], 1.0 / D, EPS, ALU.mult, ALU.add))
            vec.reciprocal(rstd[:, :], rstd[:, :]).then_inc(s_inv, 1)
            vec.wait_ge(s_root, 1)
            for p in range(NT // 2, NT):
                ts(x[:, p, :], x[:, p, :], rstd[:, p:p + 1], None, ALU.mult).then_inc(s_xs, 1)
            vec.wait_ge(s_ct, 1)
            for i, c in enumerate((c_re, c_im)):
                for h in range(2):
                    src = ps[64 * h:64 * h + 64, 5 + i, :].rearrange("n (q h c) -> n q h c", h=2, c=GC)[:, :, h, :]
                    op(vec.tensor_copy(c[64 * h:64 * h + 64, :, :], src))
            for n in range(2 * KD):
                k, half = n // 2, n % 2
                col = slice(half * HALF, (half + 1) * HALF)
                vec.wait_ge(s_hi, n + 1)
                stt(xn_lo[:, k, col], ps[:, n % 4, :], gmix[:, k:k + 1], xn_hi[:, k, col].bitcast(F32),
                    ALU.mult, ALU.subtract).then_inc(s_lo, 1)

            vec.wait_ge(s_xt, 2 * KD)
            weights_low(vec, 0)
            vec.wait_ge(s_sin, 1)
            cs, sn = s(7), s(2)
            op(tt(s(10), s(3), s(3), ALU.mult))
            op(ts(cs, s(10), -2.0, 1.0, ALU.mult, ALU.add))
            unit_length(vec, step, cs, sn, s(10), s(11))
            op(vec.memset(pw_re[:, :, 0:1], 1.0))
            op(vec.memset(pw_im[:, :, 0:1], 0.0))
            lb_re, lb_im = pw_re[:, :, 1], pw_im[:, :, 1]
            op(tt(lb_re, mag, cs, ALU.mult))
            op(tt(lb_im, mag, sn, ALU.mult))
            src_r, src_i = cs, sn
            for i, (dst_r, dst_i) in enumerate(((s(14), s(15)), (s(16), s(17)), (zk[:, 0, :], zk[:, 1, :]))):
                complex_product(vec, step, dst_r, dst_i, src_r, src_i, src_r, src_i, s(10), s(11))
                src_r, src_i = dst_r, dst_i
                op(tt(mag8[:, :], mag if i == 0 else mag8[:, :], mag if i == 0 else mag8[:, :], ALU.mult))
            unit_length(vec, step, src_r, src_i, s(10), s(11))
            vec.nop().then_inc(s_phase, 1)
            for n in (1, 2, 4):
                shape = [P, PAIRS, n]
                complex_product(vec, step, pw_re[:, :, n + 1:2 * n + 1], pw_im[:, :, n + 1:2 * n + 1],
                                pw_re[:, :, 1:n + 1], pw_im[:, :, 1:n + 1],
                                bc(pw_re[:, :, n:n + 1], shape), bc(pw_im[:, :, n:n + 1], shape),
                                t9a[:, 0:PAIRS * n].rearrange("p (q n) -> p q n", n=n),
                                t9b[:, 0:PAIRS * n].rearrange("p (q n) -> p q n", n=n))
            op(ts(s(8), lb_re, -1.0, None, ALU.add))
            op(tt(s(10), are, are, ALU.mult))
            op(tt(s(11), aim, aim, ALU.mult))
            op(tt(s(10), s(10), s(11), ALU.add))
            op(vec.reciprocal(s(9), s(10)))
            op(tt(s(10), s(8), are, ALU.mult))
            op(tt(s(11), lb_im, aim, ALU.mult))
            op(tt(s(10), s(10), s(11), ALU.add))
            op(tt(s(18), s(10), s(9), ALU.mult))
            op(tt(s(10), lb_im, are, ALU.mult))
            op(tt(s(11), s(8), aim, ALU.mult))
            op(tt(s(10), s(10), s(11), ALU.subtract))
            op(tt(s(19), s(10), s(9), ALU.mult))
            vec.wait_ge(s_b, 32)
            shape = [P, PAIRS, GC]
            view = lambda t: t[:, 0:PAIRS * GC].rearrange("p (q c) -> p q c", c=GC)
            complex_product(vec, step, bb_re[:, :, :], bb_im[:, :, :], b_re[:, :, :], b_im[:, :, :],
                            bc(s(18).unsqueeze(2), shape), bc(s(19).unsqueeze(2), shape), view(t9a), view(t9b))
            shape = [P, PAIRS // 2, 9, GC]
            for part in range(2):
                q = slice(part * PAIRS // 2, (part + 1) * PAIRS // 2)
                pr, pi = bc(pw_re[:, q, :].unsqueeze(3), shape), bc(pw_im[:, q, :].unsqueeze(3), shape)
                cr, ci = bc(c_re[:, q, :].unsqueeze(2), shape), bc(c_im[:, q, :].unsqueeze(2), shape)
                view = lambda t: t[:, 0:PAIRS // 2 * 9 * GC].rearrange("p (q k c) -> p q k c", k=9, c=GC)
                complex_product(vec, step, o_re[:, q, :, :], o_im[:, q, :, :], pr, pi, cr, ci, view(t9a), view(t9b))
                op(ts(o_im[:, q, :, :], o_im[:, q, :, :], -1.0, None, ALU.mult))
                vec.nop().then_inc(s_k_ready, 1)
            shape = [P, PAIRS, NT, GC]
            pr, pi = (bc(w[:, :, 0:NT].unsqueeze(3), shape) for w in (pw_re, pw_im))
            br, bi = bc(bb_re[:, :, :].unsqueeze(2), shape), bc(bb_im[:, :, :].unsqueeze(2), shape)
            view = lambda t: t[:, 0:PAIRS * P].rearrange("p (q k c) -> p q k c", k=NT, c=GC)
            e4 = lambda t: t[:, :, :].rearrange("p q (k c) -> p q k c", c=GC)
            complex_product(vec, step, e4(e_re), e4(e_im), pr, pi, br, bi, view(t9a), view(t9b))
            vec.nop().then_inc(s_e_made, 1)
            vec.wait_ge(s_p_lo, TILES)
            op(vec.memset(kpad[:, :, 0:7 * GC], 0.0))
            kpad_v = kpad[:, :, :].rearrange("c (q h) w -> c q h w", h=2)
            for n in range(GROUPS // 4):
                a, h = n // 2, n % 2
                vec.wait_ge(s_k, n + 1)
                vec.tensor_copy(kpad_v[:, 4 * a:4 * a + 4, h, 7 * GC:],
                                ps[0:GC, 4 + n % 2, :].rearrange("c (g w) -> c g w", g=4)).then_inc(s_k_copied, 1)
            for n in range(2 * PAIRS // 4):
                vec.wait_ge(s_et, n + 1)
                e = (e_re, e_im)[n // (PAIRS // 4)]
                q = n % (PAIRS // 4) * 4
                vec.tensor_copy(e[:, q:q + 4, :], ps[:, n % 2, :].rearrange("p (q c) -> p q c", q=4)).then_inc(s_et_copied, 1)

        @block.tensor
        def _(pe):
            pe.wait_ge(s_const, 1)
            pe.wait_ge(s_par_in, 1)
            pe.transpose(ps[:, 7, 0:96], par[0:96, :], ident[0:96, 0:96]).then_inc(s_par_t, 1)
            pe.wait_ge(s_c, 64)
            for i in range(2):
                for f in range(FT):
                    last = pe.transpose(ps[:, 5 + i, f * P:(f + 1) * P],
                                        craw[:, i, f, :, :].rearrange("p h n -> p (h n)"), ident[:, :])
            last.then_inc(s_ct, 1)
            pe.wait_ge(s_xs, NT)
            for n in range(2 * KD):
                k, half = n // 2, n % 2
                if n >= 4:
                    pe.wait_ge(s_lo, n - 3)
                for j in range(4):
                    last = pe.transpose(ps[:, n % 4, j * P:(j + 1) * P],
                                        x[:, half * 4 + j, k * P:(k + 1) * P], ident[:, :])
                last.then_inc(s_xt, 1)
            pe.wait_ge(s_lo, 2 * KD)

            def project(f):
                pe.wait_ge(s_p_lo, f + 1)
                for half in range(2):
                    col = slice(half * HALF, (half + 1) * HALF)
                    if f >= 2:
                        pe.wait_ge(s_p_ev, 2 * f + half - 3)
                    bank = ps[:, P_BANK[f % 2] + half, :]
                    for k in range(KD):
                        pe.matmul(bank, p_hi[:, f % 2, k, :], xn_hi[:, k, col], start=k == 0, stop=False)
                        pe.matmul(bank, p_hi[:, f % 2, k, :], xn_lo[:, k, col], start=False, stop=False)
                        last = pe.matmul(bank, p_lo[:, f % 2, k, :], xn_hi[:, k, col], start=False, stop=k == KD - 1)
                    last.then_inc(s_p_mm, 1)

            project(0)
            project(1)
            project(2)
            project(3)
            project(4)
            for n in range(GROUPS // 4):
                h = n % 2
                pe.wait_ge(s_k_ready, 1 if n < GROUPS // 8 else 2)
                if n >= 2:
                    pe.wait_ge(s_k_copied, n - 1)
                for j in range(4):
                    q, rows = n // 2 * 4 + j, slice(64 * h, 64 * h + 64)
                    dst = ps[0:GC, 4 + n % 2, j * P:(j + 1) * P]
                    taps = [o[rows, q, 0:NT, :].rearrange("p k c -> p (k c)") for o in (o_re, o_im)]
                    pe.matmul(dst, bb_re[rows, q, :], taps[0], start=True, stop=False)
                    last = pe.matmul(dst, bb_im[rows, q, :], taps[1], start=False, stop=True)
                last.then_inc(s_k, 1)
            pe.wait_ge(s_e_made, 1)
            for n in range(2 * PAIRS // 4):
                e = (e_re, e_im)[n // (PAIRS // 4)]
                if n >= 2:
                    pe.wait_ge(s_et_copied, n - 1)
                for j in range(4):
                    last = pe.transpose(ps[:, n % 2, j * P:(j + 1) * P], e[:, n % (PAIRS // 4) * 4 + j, :], ident[:, :])
                last.then_inc(s_et, 1)
    return dict(xn_hi=xn_hi, xn_lo=xn_lo, e_re=e_re, e_im=e_im, o_re=o_re, o_im=o_im, w_re=w_re, w_im=w_im,
                ident=ident, mag8=mag8, next_raw=next_raw, s_next_raw=s_next_raw)




def project_block(nc, m, ins, dr, t):
    at, sem = m.at, m.sem
    xn_hi, xn_lo, w_re, w_im, mag8 = t["xn_hi"], t["xn_lo"], t["w_re"], t["w_im"], t["mag8"]
    e_re, e_im, o_re, o_im = t["e_re"], t["e_im"], t["o_re"], t["o_im"]
    toep = at("toep", [P, GROUPS, P], 64)
    u = at("s5_in", [P, GROUPS, P], 114)
    h_re = at("h_re", [P, PAIRS, P], 130)
    h_im = at("h_im", [P, PAIRS, P], 138)
    raw, s_raw = t["next_raw"], t["s_next_raw"]
    w_hi = at("p_w_hi", [P, 2, KD, P], 154, F32R)
    w_lo = at("p_w_lo", [P, 2, KD, P], 162, F32R)
    out = at("p_out", [P, 2, SEQ], 170)
    tmp = at("p_tmp", [P, 4, 4, P], 178)
    s_stored = [sem(f"b_stored{s}") for s in range(2)]
    s_hi, s_split, s_acc, s_acc_free = (sem(f"b_{n}") for n in ("hi", "split", "acc", "acc_free"))
    s_u, s_e, s_e_read, s_toep, s_h, s_y, s_y_out, s_ysc, v_step = \
        (sem(f"b_{n}") for n in ("u", "e", "e_read", "toep", "h", "y", "y_out", "ysc", "v_step"))
    TURNS = FT // 2
    columns = [2 * S5W + f * P for f in range(1, FT)] + [S5W]
    u_first = at("u_first", [P, SEQ], 186)
    v = at("v_cm", [P, HEADS, SEQ], 146)
    bn, nw = at("b_rows", [P, HEADS, P], 190), at("norm_w", [P, HEADS, P], 194)
    dskip = at("d_skip", [P, FT], 205)
    s_v, s_small = sem("c_v"), sem("c_small")
    w_v = ins["w_in"][0].rearrange("(k p) c -> p k c", p=P)
    quad = lambda tile, a: tile[:, 4 * a:4 * a + 4, :]

    with ExitStack() as local:
        ps = local.enter_context(nc.psum_tensor("b_ps", [P, 8, HALF], F32))
        block = local.enter_context(nc.Block())

        @block.sync
        def _(sp):
            xs = dr["proj"][0:S5W, :].rearrange("(g c) (p k) -> p c g k", c=GC, p=NT)
            for p in range(NT):
                sp.dma_start(u[(NT - 1 - p) * GC:(NT - p) * GC, :, :], xs[p]).then_inc(s_u, 16)
            for s in range(2):
                sp.wait_ge(s_split, s + 1)
                sp.dma_start(raw[:, s, :, :], w_v[:, :, columns[2 + s]:columns[2 + s] + P]).then_inc(s_raw[s], 16)
            sp.wait_ge(s_e, PAIRS // 4)
            for k in range(NT):
                sp.dma_start(toep[k * GC:(k + 1) * GC, :, :], dr["kpad"][:, :, k * GC:k * GC + P]).then_inc(s_toep, 16)
            for s, stores in ((0, 2), (1, 1)):
                sp.wait_ge(s_stored[s], 16 * (1 + stores))
            sp.wait_ge(s_acc, 4 * TURNS)
            sp.dma_start(v[:, :, :], dr["proj"][S5W:2 * S5W, :].rearrange("(f p) s -> p f s", p=P)).then_inc(s_v, 16)
            sp.wait_ge(s_y_out, GROUPS // 4)
            ys = dr["y"].rearrange("(g c) (p k) -> p c g k", c=GC, p=NT)
            for p in range(NT):
                sp.dma_start(ys[p], u[p * GC:(p + 1) * GC, :, :]).then_inc(s_ysc, 16)
            sp.wait_ge(s_ysc, 16 * NT)

        @block.gpsimd
        def _(gp):
            for i in range(TURNS):
                for s in range(2):
                    gp.wait_ge(s_hi, i * 2 + (s + 1))
                    gp.tensor_tensor(w_lo[:, s, :, :], raw[:, s, :, :], w_hi[:, s, :, :].bitcast(F32),
                                     ALU.subtract).then_inc(s_split, 1)

        @block.scalar
        def _(act):
            for s in range(2):
                act.nop().then_inc(s_stored[s], 16)
            with nc.allow_non_contiguous_dma(reason="a short vector, channels across partitions"):
                act.dma_start(dskip[:, :], ins["s5_d"][0].rearrange("(f p) -> p f", p=P)).then_inc(s_small, 16)
            act.dma_start(bn[:, :, :].rearrange("p h t -> p (h t)"),
                          ins["sgu_b"][0].rearrange("h t -> (h t)").partition_broadcast(P)).then_inc(s_small, 16)
            act.dma_start(nw[:, :, :].rearrange("p h t -> p (h t)"), ins["sgu_norm"][0].partition_broadcast(P)).then_inc(s_small, 16)

            def high(i, s, first=False):
                act.wait_ge(s_raw[s], i * 16 + 16)
                if not first:
                    act.wait_ge(s_acc, i * 4 + (2 * s - 2))
                act.activation(w_hi[:, s, :, :], raw[:, s, :, :], ACT.Copy).then_inc(s_hi, 1)

            def evacuate(i, s):
                act.wait_ge(s_stored[s], i * 16 + 16)
                for half in range(2):
                    act.wait_ge(s_acc, i * 4 + (2 * s + half + 1))
                    target = u_first if 2 * i + s == FT - 1 else out[:, s, :]
                    act.activation(target[:, half * HALF:(half + 1) * HALF], ps[:, 2 * s + half, :],
                                   ACT.Copy).then_inc(s_acc_free, 1)
                if 2 * i + s == FT - 1:
                    return
                act.wait_ge(s_acc_free, i * 4 + (4 + 2 * s + 2))
                rows = S5W + (i * 2 + s + 1) * P
                act.dma_start(dr["proj"][rows:rows + P, :], out[:, s, :]).then_inc(s_stored[s], 16)

            high(0, 0, first=True)
            high(0, 1, first=True)
            for i in range(TURNS - 1):
                for s in range(2):
                    evacuate(i, s)
                    high(i + 1, s)
            for s in range(2):
                evacuate(TURNS - 1, s)

        @block.vector
        def _(vec):
            step = Counted(vec, v_step)
            step.did(vec.memset(h_re[:, :, 0:1], 0.0))
            step.did(vec.memset(h_im[:, :, 0:1], 0.0))
            t0, t1, f_re, f_im = (tmp[:, i, :, :] for i in range(4))

            def product(out, a, b, c, d, op, x, y):
                step.did(vec.tensor_tensor(x, a, b, ALU.mult))
                step.did(vec.tensor_tensor(y, c, d, ALU.mult))
                step.settle()
                step.did(vec.tensor_tensor(out, x, y, op))
                step.settle()

            for a in range(PAIRS // 4):
                wr, wi = quad(w_re, a), quad(w_im, a)
                er, ei = (ps[:, 4 + 2 * (a % 2) + i, :].rearrange("p (q k) -> p q k", q=4) for i in range(2))
                vec.wait_ge(s_e, a + 1)
                product(f_re, er, wr, ei, wi, ALU.add, t0, t1)
                product(f_im, ei, wr, er, wi, ALU.subtract, t0, t1)
                vec.nop().then_inc(s_e_read, 1)
                for g, f in ((t0, f_re), (t1, f_im)):
                    for j in range(4):
                        decay = bc(mag8[:, 4 * a + j:4 * a + j + 1], [P, P])
                        step.did(vec.tensor_tensor_scan(g[:, j, :], decay, f[:, j, :], 0.0, ALU.mult, ALU.add))
                step.settle()
                cut, late = slice(0, P - 1), slice(1, P)
                g_re, g_im, wr, wi = t0[:, :, cut], t1[:, :, cut], wr[:, :, cut], wi[:, :, cut]
                x, y = f_re[:, :, cut], f_im[:, :, cut]
                product(quad(h_re, a)[:, :, late], g_re, wr, g_im, wi, ALU.subtract, x, y)
                product(quad(h_im, a)[:, :, late], g_re, wi, g_im, wr, ALU.add, x, y)
                vec.nop().then_inc(s_h, 1)
            u_v = u[:, :, :].rearrange("p (q h) k -> p q h k", h=2)
            for n in range(GROUPS // 4):
                vec.wait_ge(s_y, n + 1)
                vec.tensor_copy(u_v[:, n // 2 * 4:n // 2 * 4 + 4, n % 2, :],
                                ps[:, 4 + n % 4, :].rearrange("p (q k) -> p q k", q=4)).then_inc(s_y_out, 1)

        @block.tensor
        def _(pe):
            pe.nop().then_inc(s_acc_free, 4)

            def tile(i, s):
                pe.wait_ge(s_split, i * 2 + (s + 1))
                for half in range(2):
                    col = slice(half * HALF, (half + 1) * HALF)
                    pe.wait_ge(s_acc_free, i * 4 + (2 * s + half + 1))
                    bank = ps[:, 2 * s + half, :]
                    for k in range(KD):
                        pe.matmul(bank, w_hi[:, s, k, :], xn_hi[:, k, col], start=k == 0, stop=False)
                        pe.matmul(bank, w_hi[:, s, k, :], xn_lo[:, k, col], start=False, stop=False)
                        last = pe.matmul(bank, w_lo[:, s, k, :], xn_hi[:, k, col], start=False, stop=k == KD - 1)
                    last.then_inc(s_acc, 1)

            def state_inputs(a):
                if a >= 2:
                    pe.wait_ge(s_e_read, a - 1)
                for i, e in enumerate((e_re, e_im)):
                    for j in range(4):
                        for h in range(2):
                            q, rows = 4 * a + j, slice(64 * h, 64 * h + 64)
                            last = pe.matmul(ps[rows, 4 + 2 * (a % 2) + i, j * P:(j + 1) * P], e[:, q, rows],
                                             u[:, 2 * q + h, :], start=True, stop=True)
                last.then_inc(s_e, 1)

            tile(0, 0)
            pe.wait_ge(s_u, 16 * NT)
            state_inputs(0)
            state_inputs(1)
            tile(0, 1)
            state_inputs(2)
            state_inputs(3)
            tile(1, 0)
            tile(1, 1)
            pe.wait_ge(s_toep, 16 * NT)
            pe.wait_ge(s_e_read, PAIRS // 4)
            for n in range(GROUPS // 4):
                pe.wait_ge(s_h, n // 2 + 1)
                h = n % 2
                rows = slice(64 * h, 64 * h + 64)
                if n >= 4:
                    pe.wait_ge(s_y_out, n - 3)
                for j in range(4):
                    q = n // 2 * 4 + j
                    bank = ps[:, 4 + n % 4, j * P:(j + 1) * P]
                    pe.matmul(bank, toep[:, 2 * q + h, :], u[:, 2 * q + h, :], start=True, stop=False)
                    for o, hs in ((o_re, h_re), (o_im, h_im)):
                        last = pe.matmul(bank, o[rows, q, 1:9, :].rearrange("p k c -> p (k c)"), hs[rows, q, :],
                                         start=False, stop=hs is h_im)
                last.then_inc(s_y, 1)
    return dict(v=v, u_first=u_first, bn=bn, nw=nw, dskip=dskip, s_v=s_v, s_small=s_small)


def gating_block(nc, m, ins, dr, t):
    at, sem = m.at, m.sem
    ident = t["ident"]
    y_hi, y_lo = at("y_hi", [P, FT, SEQ], 64, F32R), at("y_lo", [P, FT, SEQ], 80, F32R)
    us_hi, us_lo = at("us_hi", [P, FT, SEQ], 96, F32R), at("us_lo", [P, FT, SEQ], 112, F32R)
    v, bn, nw, dskip, s_v, s_small = (t[n] for n in ("v", "bn", "nw", "dskip", "s_v", "s_small"))
    u = at("u_cm", [P, HEADS, SEQ], 128)
    yc, xs = at("y_conv", [P, FT, SEQ], 80), at("x_s5", [P, FT, SEQ], 64)
    v_tm = at("v_tm", [P, NT, HEADS, P], 162)
    wn, wp, ws_t = at("ws_rows", [P, HEADS, P], 144), at("ws_perm", [P, HEADS, P], 178), at("ws_t", [P, HEADS, P], 180)
    vst, vh = at("v_slice", [P, 2, HEADS, P], 182), at("v_norm", [P, 2, HEADS, P], 186)
    bp = at("b_perm", [P, HEADS, P], 192)
    xn_hi, xn_lo = t["xn_hi"], t["xn_lo"]
    u_raw = at("u_raw", [P, FT, KD, P], 96)
    FIRST = 2
    uw_hi, uw_lo = at("u_w_hi", [P, 2, KD, P], 112, F32R), at("u_w_lo", [P, 2, KD, P], 120, F32R)
    U_BANK = 6
    s_u_hi, s_u_lo, s_u_mm = sem("c_u_hi"), sem("c_u_lo"), sem("c_u_mm")
    tmp = at("c_tmp", [P, 4, HEADS * P], 197)
    ssq = at("c_ssq", [P, NT, HEADS], 205.25)
    rstd = at("c_rstd", [P, NT, HEADS], 205.5)
    s_u = [sem(f"c_u{f}") for f in range(FT)]
    s_w, s_yc, s_masked, s_wp, s_wt, s_t, s_g, s_y_hi, s_y, s_gu, s_vst, s_vt, s_sq, s_v_done, \
        s_inv, s_rstd, s_vh, s_mix, s_us, v_step, g_step = (sem(f"c_{n}") for n in (
            "w", "yc", "masked", "wp", "wt", "t", "g", "y_hi", "y", "gu", "vst", "vt", "sq",
            "v_done", "inv", "rstd", "vh", "mix", "us", "v_step", "g_step"))
    Y_POOL = 2
    chunk = lambda cm, k: cm[:, :, :].rearrange("c h (p j) -> c h p j", p=NT)[:, :, :, bass.ds(k * SC, SC)]
    phased = lambda ap: ap.rearrange("c h (p j) -> c h p j", p=NT)
    permuted = lambda ap: ap.rearrange("a h (c p) -> a h p c", p=NT)

    with ExitStack() as local:
        ps = local.enter_context(nc.psum_tensor("c_ps", [P, 8, HALF], F32))
        block = local.enter_context(nc.Block())

        @block.sync
        def _(sp):
            rows = lambda ap: ap.rearrange("(f p) s -> p f s", p=P)
            sp.dma_start(wn[:, :, :], ins["sgu_w"][0].rearrange("h t s -> t h s")).then_inc(s_w, 16)
            for f in range(1, FT):
                sp.dma_start(u_raw[:, f, :, :], ins["w_in"][0].rearrange("(k p) c -> p k c", p=P)
                             [:, :, S5W + f * P:S5W + (f + 1) * P]).then_inc(s_u[f], 16)
            sp.dma_start(yc[:, :, :], rows(dr["y"])).then_inc(s_yc, 16)
            sp.dma_start(xs[:, :, :], rows(dr["proj"][0:S5W, :])).then_inc(s_yc, 16)

        @block.gpsimd
        def _(gp):
            gp.wait_ge(s_w, 16)
            gp.affine_select(out=wn[:, :, :], in_=wn[:, :, :], compare_op=ALU.is_ge, fill=0.0, base=0,
                             pattern=[[0, HEADS], [-1, P]], channel_multiplier=1).then_inc(s_masked, 1)
            for f in range(1, FT):
                gp.wait_ge(s_u_hi, f)
                gp.tensor_tensor(uw_lo[:, f % 2, :, :], u_raw[:, f, :, :], uw_hi[:, f % 2, :, :].bitcast(F32),
                                 ALU.subtract).then_inc(s_u_lo, 1)
            step = Counted(gp, g_step)
            gp.wait_ge(s_small, 48)
            gp.wait_ge(s_gu, FIRST)
            gp.wait_ge(s_rstd, 1)
            with gp.Fori(0, NT // 2) as i:
                step.loop_body(i, 2)
                for s in range(2):
                    k = i * 2 + s
                    gp.wait_ge(s_mix, i * 2 + (s + 1))
                    step.did(gp.tensor_tensor(vh[:, s, :, :], v_tm[:, k, :, :],
                                              bc(rstd[:, k, :].unsqueeze(2), [P, HEADS, P]), ALU.mult))
                    step.settle()
                    gp.tensor_tensor(vh[:, s, :, :], vh[:, s, :, :], nw[:, :, :], ALU.mult).then_inc(s_vh, 1)
            step.loop_end(NT // 2)
            for f in range(Y_POOL):
                gp.wait_ge(s_y_hi, f + 1)
                gp.tensor_tensor(y_lo[:, f, :], yc[:, f, :], y_hi[:, f, :].bitcast(F32), ALU.subtract).then_inc(s_y, 1)

        @block.scalar
        def _(act):
            def weights_high(f):
                act.wait_ge(s_u[f], 16)
                if f >= 3:
                    act.wait_ge(s_u_mm, 2 * f - 4)
                act.activation(uw_hi[:, f % 2, :, :], u_raw[:, f, :, :], ACT.Copy).then_inc(s_u_hi, 1)

            def gelu_u(n):
                act.wait_ge(s_u_mm, n + 1 - FIRST)
                act.activation(u[:, n // 2, n % 2 * HALF:(n % 2 + 1) * HALF], ps[:, U_BANK + n % 2, :],
                               ACT.Gelu_apprx_tanh).then_inc(s_gu, 1)

            act.wait_ge(s_v, 16)
            for i in range(NT // 2):
                for s in range(2):
                    act.activation(phased(vst[:, s, :, :]), chunk(v, i * 2 + s), ACT.Gelu_apprx_tanh).then_inc(s_vst, 1)
                if i == 0:
                    weights_high(1)
                    weights_high(2)
                for s in range(2):
                    act.wait_ge(s_vt, i * 2 + (s + 1))
                    act.wait_ge(s_v_done, i * 2 + (s + 1))
                    act.activation(tmp[:, s, :], ps[:, s, :], ACT.Square).then_inc(s_sq, 1)
                if i == 0:
                    act.activation(u[:, 0, :], t["u_first"][:, :], ACT.Gelu_apprx_tanh).then_inc(s_gu, FIRST)
                else:
                    gelu_u(FIRST + i - 1)
                if i == 2:
                    weights_high(3)
            act.wait_ge(s_inv, 1)
            act.activation(rstd[:, :, :], rstd[:, :, :], ACT.Sqrt).then_inc(s_rstd, 1)
            for n in range(FIRST + NT // 2 - 1, 2 * FT):
                gelu_u(n)
            for f in range(FT):
                act.wait_ge(s_t, f + 1)
                act.activation(yc[:, f, :], yc[:, f, :], ACT.Gelu_apprx_tanh).then_inc(s_g, 1)
            for f in range(FT):
                act.wait_ge(s_g, f + 1)
                act.activation(y_hi[:, f, :], yc[:, f, :], ACT.Copy).then_inc(s_y_hi, 1)

        @block.vector
        def _(vec):
            step = Counted(vec, v_step)
            vec.wait_ge(s_small, 48)
            step.did(vec.tensor_copy(phased(bp[:, :, :]), permuted(bn[:, :, :])))
            vec.wait_ge(s_masked, 1)
            vec.tensor_copy(phased(wp[:, :, :]), permuted(wn[:, :, :])).then_inc(s_wp, 1)
            vec.wait_ge(s_wt, 1)
            step.did(vec.tensor_copy(phased(ws_t[:, :, :]), permuted(ps[:, 2, :].rearrange("s (h t) -> s h t", h=HEADS))))
            step.settle()
            with vec.Fori(0, NT // 2) as i:
                for s in range(2):
                    vec.wait_ge(s_sq, i * 2 + (s + 1))
                    vec.tensor_copy(v_tm[:, i * 2 + s, :, :], ps[:, s, :].rearrange("p (h d) -> p h d", h=HEADS))
                    vec.reduce_sum(ssq[:, i * 2 + s, :], tmp[:, s, :].rearrange("p (h d) -> p h d", h=HEADS),
                                   AX.X).then_inc(s_v_done, 1)
            vec.wait_ge(s_v_done, 2 + NT)
            step.did(vec.tensor_scalar(rstd[:, :, :], ssq[:, :, :], 1.0 / P, EPS, ALU.mult, ALU.add))
            step.settle()
            vec.reciprocal(rstd[:, :, :], rstd[:, :, :]).then_inc(s_inv, 1)
            vec.wait_ge(s_yc, 32)
            for f in range(FT):
                vec.scalar_tensor_tensor(yc[:, f, :], xs[:, f, :], dskip[:, f:f + 1], yc[:, f, :],
                                         ALU.mult, ALU.add).then_inc(s_t, 1)
            vec.wait_ge(s_gu, 2 * FT)
            with vec.Fori(0, NT // 2) as i:
                step.loop_body(i, 2 * 3)
                for s in range(2):
                    k = i * 2 + s
                    vec.wait_ge(s_mix, i * 2 + (s + 3))
                    full = tmp[:, s, :].rearrange("p (h t) -> p h t", h=HEADS)
                    step.did(vec.tensor_tensor(full, ps[:, 4 + s, :].rearrange("p (h t) -> p h t", h=HEADS),
                                               bp[:, :, :], ALU.add))
                    step.settle()
                    step.did(vec.tensor_tensor(phased(full), phased(full), chunk(u, k), ALU.mult))
                    step.settle()
                    step.did(vec.tensor_copy(chunk(us_hi, k), phased(full)))
                    step.settle()
                    vec.tensor_tensor(chunk(us_lo, k), phased(full), chunk(us_hi, k).bitcast(F32),
                                      ALU.subtract).then_inc(s_us, 1)
            step.loop_end(NT // 2)
            for f in range(Y_POOL, FT):
                vec.wait_ge(s_y_hi, f + 1)
                vec.tensor_tensor(y_lo[:, f, :], yc[:, f, :], y_hi[:, f, :].bitcast(F32), ALU.subtract).then_inc(s_y, 1)

        @block.tensor
        def _(pe):
            pe.nop().then_inc(s_v_done, 2)
            pe.nop().then_inc(s_us, 2)
            pe.nop().then_inc(s_mix, 2)
            pe.wait_ge(s_wp, 1)
            for h in range(HEADS):
                last = pe.transpose(ps[:, 2, h * P:(h + 1) * P], wp[:, h, :], ident[:, :])
            last.then_inc(s_wt, 1)

            def project_u(n):
                f, half = n // 2, n % 2
                col = slice(half * HALF, (half + 1) * HALF)
                pe.wait_ge(s_u_lo, f)
                if n >= FIRST + 2:
                    pe.wait_ge(s_gu, n - 1)
                bank = ps[:, U_BANK + half, :]
                for k in range(KD):
                    pe.matmul(bank, uw_hi[:, f % 2, k, :], xn_hi[:, k, col], start=k == 0, stop=False)
                    pe.matmul(bank, uw_hi[:, f % 2, k, :], xn_lo[:, k, col], start=False, stop=False)
                    last = pe.matmul(bank, uw_lo[:, f % 2, k, :], xn_hi[:, k, col], start=False, stop=k == KD - 1)
                last.then_inc(s_u_mm, 1)

            def mix(i, s):
                pe.wait_ge(s_vh, i * 2 + (s + 1))
                pe.wait_ge(s_us, i * 2 + (s + 1))
                for h in range(HEADS):
                    last = pe.matmul(ps[:, 4 + s, h * P:(h + 1) * P], vh[:, s, h, :], ws_t[:, h, :], start=True, stop=True)
                last.then_inc(s_mix, 1)

            for i in range(NT // 2):
                for s in range(2):
                    pe.wait_ge(s_vst, i * 2 + (s + 1))
                    pe.wait_ge(s_v_done, i * 2 + (s + 1))
                    for h in range(HEADS):
                        last = pe.transpose(ps[:, s, h * P:(h + 1) * P], vst[:, s, h, :], ident[:, :])
                    last.then_inc(s_vt, 1)
                project_u(FIRST + i)
            project_u(2 * FT - 2)
            for s in range(2):
                mix(0, s)
            project_u(2 * FT - 1)
            with pe.Fori(1, NT // 2) as i:
                for s in range(2):
                    mix(i, s)
    return dict(y_hi=y_hi, y_lo=y_lo, us_hi=us_hi, us_lo=us_lo)


def merge_block(nc, m, ins, dr, t):
    at, sem = m.at, m.sem
    xn, y, us = (t["xn_hi"], t["xn_lo"]), (t["y_hi"], t["y_lo"]), (t["us_hi"], t["us_lo"])
    G5, GS, ZA, ZB, PR = range(5)
    DEPTH = (KD, KD, FT, FT, FT)
    START = (0, 8, 16, 20, 24)
    SLICES = 28
    raw = at("d_raw", [P, SLICES, P], 128)
    w_hi, w_lo = at("d_w_hi", [P, SLICES, P], 142, F32R), at("d_w_lo", [P, SLICES, P], 156, F32R)
    sig = at("d_sig", [P, 3, 2, HALF], 170)
    acc = at("d_acc", [P, 2, 2, HALF], 182)
    out = at("d_out", [P, 2, SEQ], 190)
    s_raw = [sem(f"d_raw{j}") for j in range(5)]
    s_hi, s_split, s_mm, s_sig, s_pr, s_merged = (sem(f"d_{n}") for n in ("hi", "split", "mm", "sig", "pr", "merged"))
    s_out = sem("d_out")
    v_step = sem("d_v_step")
    wo_raw, wo_hi, wo_lo = at("wo_raw", [P, KD, D], 0), at("wo_hi", [P, KD, D], 32, F32R), at("wo_lo", [P, KD, D], 96, F32R)
    s_wo = [sem(f"d_wo{j}") for j in range(KD // 2)]
    s_wo_hi, s_wo_lo = sem("d_wo_hi"), sem("d_wo_lo")
    zero, s_zero, s_zeroed = at("zero_rows", [P, D], 198), sem("d_zero"), sem("d_zeroed")
    WO_POOL = 5
    w_in = ins["w_in"][0].rearrange("(k p) c -> p k c", p=P)
    w_glu = ins["w_glu"][0].rearrange("(k p) c -> p k c", p=P)
    w_proj = ins["w_sgu_proj"][0].rearrange("(k p) c -> p k c", p=P)
    gates = 3 * S5W
    source = ((w_in, gates), (w_in, gates + D), (w_glu, 0), (w_glu, D), (w_proj, 0))
    ORDER = (PR, G5, GS, ZB, ZA)
    BANK = {G5: 0, GS: 2, PR: 4, ZB: 6, ZA: 0}
    RANK = {j: r for r, j in enumerate(ORDER)}

    with ExitStack() as local:
        ps = local.enter_context(nc.psum_tensor("d_ps", [P, 8, HALF], F32))
        block = local.enter_context(nc.Block())

        @block.sync
        def _(sp):
            def load(j, i):
                w, first = source[j]
                sp.dma_start(raw[:, START[j]:START[j] + DEPTH[j], :],
                             w[:, :, bass.ds(i * P + first, P)]).then_inc(s_raw[j], 16)

            def load_all(i):
                for r, j in enumerate(ORDER):
                    sp.wait_ge(s_split, i * 5 + (r - 4))
                    load(j, i)

            def store(i, s):
                sp.wait_ge(s_merged, i * 2 + 2)
                sp.wait_ge(s_out, i * 16 + 16)
                sp.dma_start(dr["merged"][bass.ds(i * P, P), :], out[:, s, :]).then_inc(s_out, 16)

            for j in ORDER:
                load(j, 0)
            sp.wait_ge(s_zero, 1)
            sp.dma_start(dr["yr"][EXPERTS * BLK:, :].rearrange("(b p) d -> p b d", p=BLK),
                         bc(zero[0:BLK, :].unsqueeze(1), [BLK, OVER, D])).then_inc(s_zeroed, 16)
            with sp.Fori(2, KD // 2 + 1) as turn:
                load_all(turn * 2 - 3)
                store(turn * 2 - 4, 0)
                load_all(turn * 2 - 2)
                store(turn * 2 - 3, 1)
            load_all(KD - 1)
            store(KD - 2, 0)
            sp.wait_ge(s_mm, 10 * (KD - 1) + 6)
            for j in range(KD // 2):
                sp.dma_start(wo_raw[:, 2 * j:2 * j + 2, :],
                             ins["w_out"][0, 2 * j * P:(2 * j + 2) * P, :].rearrange("(k p) d -> p k d", p=P)).then_inc(s_wo[j], 16)
            store(KD - 1, 1)
            sp.wait_ge(s_out, 16 * (2 + KD))
            sp.wait_ge(s_zeroed, 16)

        @block.gpsimd
        def _(gp):
            gp.memset(zero[:, :], 0.0).then_inc(s_zero, 1)
            with gp.Fori(0, KD) as i:
                for r, j in enumerate(ORDER):
                    sl = slice(START[j], START[j] + DEPTH[j])
                    gp.wait_ge(s_hi, i * 5 + (r + 1))
                    gp.tensor_tensor(w_lo[:, sl, :], raw[:, sl, :], w_hi[:, sl, :].bitcast(F32),
                                     ALU.subtract).then_inc(s_split, 1)
            for k in range(WO_POOL):
                gp.wait_ge(s_wo_hi, k + 1)
                gp.tensor_tensor(wo_lo[:, k, :], wo_raw[:, k, :], wo_hi[:, k, :].bitcast(F32), ALU.subtract).then_inc(s_wo_lo, 1)

        @block.scalar
        def _(act):
            def high(j, i, first=False):
                sl = slice(START[j], START[j] + DEPTH[j])
                act.wait_ge(s_raw[j], i * 16 + 16)
                if not first:
                    act.wait_ge(s_mm, i * 10 + (2 * RANK[j] - 8))
                act.activation(w_hi[:, sl, :], raw[:, sl, :], ACT.Copy).then_inc(s_hi, 1)

            def sigmoid(j, n, i, first=False):
                for half in range(2):
                    act.wait_ge(s_mm, i * 10 + (2 * RANK[j] + half + 1))
                    if not first:
                        act.wait_ge(s_merged, i * 2 + (half - 1))
                    act.activation(sig[:, n, half, :], ps[:, BANK[j] + half, :], ACT.Sigmoid).then_inc(s_sig, 1)

            def turn(i, first=False, last=False):
                for j, n in ((PR, None), (G5, 0), (GS, 1), (ZB, 2), (ZA, None)):
                    if n is not None:
                        sigmoid(j, n, i, first)
                    if not last:
                        high(j, i + 1)

            for j in ORDER:
                high(j, 0, first=True)
            turn(0, first=True)
            with act.Fori(1, KD - 1) as i:
                turn(i)
            turn(KD - 1, last=True)
            for k in range(KD):
                act.wait_ge(s_wo[k // 2], 16)
                act.activation(wo_hi[:, k, :], wo_raw[:, k, :], ACT.Copy).then_inc(s_wo_hi, 1)

        @block.vector
        def _(vec):
            step = Counted(vec, v_step)
            vec.nop().then_inc(s_out, 32)
            with vec.Fori(0, KD // 2) as turn:
                step.loop_body(turn, 2 * 2 * 3)
                for s in range(2):
                    i = turn * 2 + s
                    vec.wait_ge(s_out, i * 16 + 16)
                    for half in range(2):
                        vec.wait_ge(s_mm, i * 10 + (2 * RANK[PR] + half + 1))
                        vec.wait_ge(s_sig, i * 6 + (2 + half + 1))
                        vec.tensor_tensor(acc[:, 0, half, :], ps[:, BANK[PR] + half, :], sig[:, 1, half, :],
                                          ALU.mult).then_inc(s_pr, 1)
                        vec.wait_ge(s_sig, i * 6 + (4 + half + 1))
                        step.did(vec.tensor_tensor(acc[:, 1, half, :], sig[:, 0, half, :], sig[:, 2, half, :], ALU.mult))
                        step.settle()
                    for half in range(2):
                        vec.wait_ge(s_mm, i * 10 + (2 * RANK[ZA] + half + 1))
                        step.did(vec.tensor_tensor(acc[:, 1, half, :], ps[:, BANK[ZA] + half, :], acc[:, 1, half, :], ALU.mult))
                        step.settle()
                        vec.wait_ge(s_pr, i * 2 + (half + 1))
                        step.did(vec.tensor_tensor(out[:, s, half * HALF:(half + 1) * HALF], acc[:, 0, half, :],
                                                   acc[:, 1, half, :], ALU.add))
                        step.settle()
                        vec.nop().then_inc(s_merged, 1)
            step.loop_end(KD // 2)
            for k in range(WO_POOL, KD):
                vec.wait_ge(s_wo_hi, k + 1)
                vec.tensor_tensor(wo_lo[:, k, :], wo_raw[:, k, :], wo_hi[:, k, :].bitcast(F32), ALU.subtract).then_inc(s_wo_lo, 1)

        @block.tensor
        def _(pe):
            def product(j, i, first):
                pe.wait_ge(s_split, i * 5 + (RANK[j] + 1))
                hi, lo = {G5: xn, GS: xn, ZA: y, ZB: y, PR: us}[j]
                for half in range(2):
                    col = slice(half * HALF, (half + 1) * HALF)
                    if j == ZA:
                        pe.wait_ge(s_sig, i * 6 + (half + 1))
                    elif not first:
                        if j == PR:
                            pe.wait_ge(s_pr, i * 2 + (half - 1))
                        elif j == G5:
                            pe.wait_ge(s_merged, i * 2 + (half - 1))
                        else:
                            pe.wait_ge(s_sig, i * 6 + (half + (-3 if j == GS else -1)))
                    bank = ps[:, BANK[j] + half, :]
                    for k in range(DEPTH[j]):
                        a = START[j] + k
                        pe.matmul(bank, w_hi[:, a, :], hi[:, k, col], start=k == 0, stop=False)
                        pe.matmul(bank, w_hi[:, a, :], lo[:, k, col], start=False, stop=False)
                        last = pe.matmul(bank, w_lo[:, a, :], hi[:, k, col], start=False, stop=k == DEPTH[j] - 1)
                    last.then_inc(s_mm, 1)

            for j in ORDER:
                product(j, 0, True)
            with pe.Fori(1, KD) as i:
                for j in ORDER:
                    product(j, i, False)
    return dict(wo_hi=wo_hi, wo_lo=wo_lo)


def mixer_out_block(nc, m, ins, dr, t):
    at, sem = m.at, m.sem
    ident, wo_hi, wo_lo = t["ident"], t["wo_hi"], t["wo_lo"]
    h = at("h", [P, NT, D], 0)
    mg = at("merged_slice", [P, 2, KD, P], 64)
    mg_hi, mg_lo = at("mg_hi", [P, 2, KD, P], 72, F32R), at("mg_lo", [P, 2, KD, P], 80, F32R)
    xt, xt_t = at("xt", [P, 2, D], 128), at("xt_t", [P, 2, KD, P], 136)
    w_r = at("w_router", [P, KD, NGRP + EXPERTS], 144)
    moe_raw = at("moe_raw", [P, 6, 4 * HALF], 148)
    g = at("g_ffn", [P, D], 197)
    logits = at("logits", [P, NT, NGRP + EXPERTS], 201)
    bias = at("router_bias", [P, NGRP + EXPERTS], 202.25)
    ssq, rstd = at("e_ssq", [P, 2], 202.5), at("e_rstd", [P, 2], 202.625)
    junk = at("e_junk", [P, D], 203)
    s_mg, s_out = ([sem(f"e_{n}{s}") for s in range(2)] for n in ("mg", "out"))
    s_x, s_par, s_mg_hi, s_mg_split, s_mm, s_h, s_inv, s_rstd, s_xt, s_xtt, s_ev, s_rt, \
        s_log, v_step = (sem(f"e_{n}") for n in (
            "x", "par", "mg_hi", "mg_split", "mm", "h", "inv", "rstd", "xt", "xtt", "ev",
            "rt", "log", "v_step"))
    s_moe = [sem(f"moe_raw{j}") for j in range(6)]
    N_OUT = NGRP + EXPERTS

    with ExitStack() as local:
        ps = local.enter_context(nc.psum_tensor("e_ps", [P, 8, HALF], F32))
        block = local.enter_context(nc.Block())

        @block.sync
        def _(sp):
            mg_v = dr["merged"].rearrange("(k p) s -> p k s", p=P)
            xt_v = dr["xt"].rearrange("(t p) d -> t p d", p=P)

            def load(n, s):
                sp.wait_ge(s_mg_split, n + 1)
                sp.dma_start(mg[:, s, :, :], mg_v[:, :, bass.ds(n * P, P)]).then_inc(s_mg[s], 16)

            def store(n, s):
                sp.wait_ge(s_xt, n + 1)
                sp.dma_start(xt_v[bass.ds(n, 1)].rearrange("o p d -> (o p) d"), xt[:, s, :]).then_inc(s_out[s], 16)

            load(0, 0)
            load(1, 1)
            xv = ins["x"][0].rearrange("(c p) d -> c p d", p=NT)
            sp.dma_start(h[:, :, :], xv).then_inc(s_x, 16)
            for j in (0, 1):
                for i, name in enumerate(("w_expert_gate", "w_expert_up")):
                    sp.dma_start(moe_raw[:, 2 * j + i, :].rearrange("p (k f) -> p k f", k=4),
                                 ins[name][0, 0].rearrange("(k p) f -> p k f", p=P)[:, 4 * j:4 * j + 4, :]).then_inc(s_moe[2 * j + i], 16)
            load(2, 0)
            with sp.Fori(1, (NT - 4) // 2 + 1) as i:
                load(i * 2 + 1, 1)
                store(i * 2 - 2, 0)
                load(i * 2 + 2, 0)
                store(i * 2 - 1, 1)
            load(NT - 1, 1)
            for n in range(NT - 4, NT):
                store(n, n % 2)
            for s in range(2):
                sp.wait_ge(s_out[s], 16 * (1 + NT // 2))
            sp.wait_ge(s_x, 16)

        @block.gpsimd
        def _(gp):
            gp.nop().then_inc(s_mg_split, 2)
            with gp.Fori(0, NT // 2) as i:
                for s in range(2):
                    gp.wait_ge(s_mg_hi, i * 2 + (s + 1))
                    gp.tensor_tensor(mg_lo[:, s, :, :], mg[:, s, :, :], mg_hi[:, s, :, :].bitcast(F32),
                                     ALU.subtract).then_inc(s_mg_split, 1)

        @block.scalar
        def _(act):
            act.dma_start(w_r[:, :, 0:NGRP], ins["w_router_group"][0].rearrange("(k p) e -> p k e", p=P)).then_inc(s_par, 16)
            act.dma_start(w_r[:, :, NGRP:], ins["w_router_expert"][0].rearrange("(k p) e -> p k e", p=P)).then_inc(s_par, 16)
            act.dma_start(bias[:, 0:NGRP], ins["b_router_group"][0].partition_broadcast(P)).then_inc(s_par, 16)
            act.dma_start(bias[:, NGRP:], ins["b_router_expert"][0].partition_broadcast(P)).then_inc(s_par, 16)
            act.dma_start(g[:, :], ins["norm_ffn"][0].partition_broadcast(P)).then_inc(s_par, 16)
            for s in range(2):
                act.nop().then_inc(s_out[s], 16)

            def high(n, s):
                act.wait_ge(s_mg[s], n * 8 + (16 - 8 * s))
                act.wait_ge(s_mm, n * 2 + 2)
                act.activation(mg_hi[:, s, :, :], mg[:, s, :, :], ACT.Copy).then_inc(s_mg_hi, 1)

            def normalise_and_copy(n, s):
                act.wait_ge(s_inv, n + 1)
                act.activation(rstd[:, s:s + 1], rstd[:, s:s + 1], ACT.Sqrt).then_inc(s_rstd, 1)
                act.wait_ge(s_rt, n + 1)
                for b in range(2):
                    act.wait_ge(s_xtt, n * 2 + (b + 1))
                    act.activation(xt_t[:, s, 4 * b:4 * b + 4, :], ps[:, 4 + b, :].rearrange("p (k c) -> p k c", k=4),
                                   ACT.Copy).then_inc(s_ev, 1)

            high(0, 0)
            with act.Fori(0, NT // 2 - 1) as i:
                high(i * 2 + 1, 1)
                normalise_and_copy(i * 2, 0)
                high(i * 2 + 2, 0)
                normalise_and_copy(i * 2 + 1, 1)
            high(NT - 1, 1)
            normalise_and_copy(NT - 2, 0)
            normalise_and_copy(NT - 1, 1)

        @block.vector
        def _(vec):
            step = Counted(vec, v_step)
            vec.nop().then_inc(s_h, 4)
            vec.nop().then_inc(s_log, 1)
            vec.wait_ge(s_x, 16)
            vec.wait_ge(s_par, 80)

            def residual_and_norm(n, s):
                row = h[:, bass.ds(n, 1), :].rearrange("p o d -> p (o d)")
                for half in range(2):
                    col = slice(half * HALF, (half + 1) * HALF)
                    vec.wait_ge(s_mm, n * 2 + (4 + half + 1))
                    vec.tensor_tensor(row[:, col], ps[:, 2 * s + half, :], row[:, col], ALU.add).then_inc(s_h, 1)
                one = slice(s, s + 1)
                vec.wait_ge(s_h, n * 2 + 6)
                step.did(vec.scalar_tensor_tensor(junk[:, :], row, 1.0, row, ALU.mult, ALU.mult, accum_out=ssq[:, one]))
                step.settle()
                step.did(vec.tensor_scalar(rstd[:, one], ssq[:, one], 1.0 / D, EPS, ALU.mult, ALU.add))
                step.settle()
                vec.reciprocal(rstd[:, one], rstd[:, one]).then_inc(s_inv, 1)
                vec.wait_ge(s_rstd, n + 1)
                vec.wait_ge(s_out[s], n * 8 + (16 - 8 * s))
                vec.scalar_tensor_tensor(xt[:, s, :], row, rstd[:, one], g[:, :], ALU.mult, ALU.mult).then_inc(s_xt, 1)

            def add_bias(n, s):
                vec.wait_ge(s_rt, n + 3)
                vec.tensor_tensor(logits[:, bass.ds(n, 1), :].rearrange("p o e -> p (o e)"), ps[:, 6, 0:N_OUT],
                                  bias[:, :], ALU.add).then_inc(s_log, 1)

            tile_pair_loop(vec, residual_and_norm, add_bias, step, 4)

        @block.tensor
        def _(pe):
            pe.nop().then_inc(s_mm, 4)
            pe.nop().then_inc(s_rt, 2)
            pe.nop().then_inc(s_ev, 2)

            def products(n, s, ks):
                for k in ks:
                    for half in range(2):
                        if k == 0:
                            pe.wait_ge(s_h, n * 2 + (half + 1))
                        col = slice(half * HALF, (half + 1) * HALF)
                        bank = ps[:, 2 * s + half, :]
                        pe.matmul(bank, mg_hi[:, s, k, :], wo_hi[:, k, col], start=k == 0, stop=False)
                        pe.matmul(bank, mg_hi[:, s, k, :], wo_lo[:, k, col], start=False, stop=False)
                        last = pe.matmul(bank, mg_lo[:, s, k, :], wo_hi[:, k, col], start=False, stop=k == KD - 1)
                        if k == KD - 1:
                            last.then_inc(s_mm, 1)

            def transposes(n, s):
                pe.wait_ge(s_xt, n + 1)
                for b in range(2):
                    pe.wait_ge(s_ev, n * 2 + (b + 1))
                    for k in range(4 * b, 4 * b + 4):
                        last = pe.transpose(ps[:, 4 + b, (k % 4) * P:(k % 4 + 1) * P], xt[:, s, k * P:(k + 1) * P], ident[:, :])
                    last.then_inc(s_xtt, 1)

            def product_tile(n, s, before=True):
                pe.wait_ge(s_mg_split, n + 3)
                products(n, s, range(KD // 2))
                if before:
                    transposes(n - 1, 1 - s)
                products(n, s, range(KD // 2, KD))

            def router(n, s):
                pe.wait_ge(s_ev, n * 2 + 4)
                pe.wait_ge(s_log, n + 1)
                for k in range(KD):
                    last = pe.matmul(ps[:, 6, 0:N_OUT], xt_t[:, s, k, :], w_r[:, k, :], start=k == 0, stop=k == KD - 1)
                last.then_inc(s_rt, 1)

            product_tile(0, 0, before=False)
            pe.wait_ge(s_par, 80)
            with pe.Fori(0, NT // 2 - 1) as i:
                product_tile(i * 2 + 1, 1, before=True)
                router(i * 2, 0)
                product_tile(i * 2 + 2, 0, before=True)
                router(i * 2 + 1, 1)
            product_tile(NT - 1, 1)
            router(NT - 2, 0)
            transposes(NT - 1, 1)
            router(NT - 1, 1)
    return dict(h=h, logits=logits, moe_raw=moe_raw, s_moe=s_moe)


def routing_block(nc, m, ins, dr, t):
    at, sem = m.at, m.sem
    logits = t["logits"]
    weights, dest = at("weights", [P, 2, NT], 205), at("dest", [P, 2, NT], 205.125, I32)
    row_tok = at("row_tok", [P, NBLK], 205.25, I32)
    over_e, over_n = at("over_e", [1, OVER], 205.5, I32), at("over_n", [1, 1], 205.75, I32)
    place = [32.0]

    def new(name, shape):
        size = 4 * math.prod(shape[1:]) / 1024
        tile = at(name, shape, place[0])
        place[0] += math.ceil(size * 32) / 32
        return tile

    down4, down8, iota32, iota_b, iota_s = (new(n, [P, k]) for n, k in
                                            (("down4", 4), ("down8", 8), ("iota32", 32), ("iota_b", NBLK), ("iota_s", P)))
    token, steps, ones32 = new("token", [P, NT]), new("steps", [P, STEPS]), new("ones32", [P, 32])
    tri, ones = new("tri", [P, P]), new("ones", [P, P])
    a, b, c, gsum, gw = (new(f"r{i}", [P, NT]) for i in range(5))
    g4a, g4b, sel_g = (new(f"g4{i}", [P, NT, 4]) for i in range(3))
    e8a, e8b, e8c, e8d = (new(f"e8{i}", [P, NT, 8]) for i in range(4))
    sel = new("sel", [P, 2, NT, 8])
    big = new("big", [P, NT, NGRP, EPG])
    one_hot = new("one_hot", [P, 2, NT, EXPERTS])
    both, before, pos = (new(n, [P, NT, EXPERTS]) for n in ("both", "before", "pos"))
    total, cnt, extra, incl, start = (new(n, [P, EXPERTS]) for n in ("total", "cnt", "extra", "incl", "start"))
    over_cmp, row_cmp = new("over_cmp", [P, EXPERTS, STEPS]), new("row_cmp", [P, 2 * NT, STEPS])
    prod = new("prod", [P, 2 * NT, EXPERTS])
    pk, bk, ek, bx, slot, blk, tmp = (new(n, [P, 2 * NT]) for n in ("pk", "bk", "ek", "bx", "slot", "blk", "rtmp"))
    slot_hot, block_hot = new("slot_hot", [P, 2 * NT, P]), new("block_hot", [P, 2 * NT, NBLK])
    over = new("over", [1, OVER, EXPERTS])
    over_f = new("over_f", [1, OVER])
    assert place[0] <= 148
    s_const, s_tri, s_e1, s_e1d, s_e2, s_e2d, s_cum, s_cum_ps, s_hot, s_rows, v_step = (sem(f"f_{n}") for n in (
        "const", "tri", "e1", "e1d", "e2", "e2d", "cum", "cum_ps", "hot", "rows", "v_step"))

    with ExitStack() as local:
        ps = local.enter_context(nc.psum_tensor("f_ps", [P, 8, HALF], F32))
        block = local.enter_context(nc.Block())

        @block.gpsimd
        def _(gp):
            def ramp(tile, step, base, per_partition=0, n=None):
                gp.iota(tile[:, :], [[step, tile.shape[1]]], base=base, channel_multiplier=per_partition,
                        allow_small_or_imprecise_dtypes=True).then_inc(s_const, 1)

            ramp(down4, -1, 4)
            ramp(down8, -1, 8)
            ramp(iota32, 1, 0)
            ramp(iota_b, 1, 0)
            ramp(iota_s, 1, 0)
            ramp(token, P, 0, 1)
            ramp(steps, BLK, BLK)
            gp.memset(ones32[:, :], 1.0).then_inc(s_const, 1)
            gp.memset(ones[:, :], 1.0).then_inc(s_const, 1)
            gp.wait_ge(s_const, 9)
            gp.affine_select(out=tri[:, :], in_=ones[:, :], compare_op=ALU.is_gt, fill=0.0, base=0,
                             pattern=[[1, P]], channel_multiplier=-1).then_inc(s_tri, 1)

        @block.scalar
        def _(act):
            act.wait_ge(s_e1, 1)
            act.activation(g4a[:, :, :], g4a[:, :, :], ACT.Exp).then_inc(s_e1d, 1)
            act.wait_ge(s_e2, 1)
            act.activation(c[:, :], c[:, :], ACT.Exp).then_inc(s_e2d, 1)

        @block.vector
        def _(vec):
            step = Counted(vec, v_step)
            tt, ts = vec.tensor_tensor, vec.tensor_scalar

            def op(instruction):
                step.did(instruction)
                step.settle()

            wide = lambda ap, n: bc(ap.unsqueeze(ap.ndim), list(ap.shape) + [n])
            flat = lambda tile: tile[:, :, :].rearrange("p k t -> p (k t)")

            def first_max(out, values, down, n, top, key):
                op(vec.reduce_max(top, values, AX.X))
                op(tt(key, values, wide(top, n), ALU.is_ge))
                op(tt(key, key, bc(down[:, :].unsqueeze(1), [P, NT, n]), ALU.mult))
                op(vec.reduce_max(b[:, :], key, AX.X))
                op(tt(out, key, wide(b[:, :], n), ALU.is_equal))

            vec.wait_ge(s_const, 9)
            gl, el = logits[:, :, 0:NGRP], logits[:, :, NGRP:].rearrange("p t (g e) -> p t g e", g=NGRP)
            first_max(sel_g[:, :, :], gl, down4, NGRP, a[:, :], g4b[:, :, :])
            tt(g4a[:, :, :], gl, wide(a[:, :], NGRP), ALU.subtract).then_inc(s_e1, 1)
            op(tt(big[:, :, :, :], el, wide(sel_g[:, :, :], EPG), ALU.mult))
            op(vec.reduce_sum(e8a[:, :, :], big[:, :, :, :].rearrange("p t g e -> p t e g"), AX.X))
            vec.wait_ge(s_e1d, 1)
            op(vec.reduce_sum(gsum[:, :], g4a[:, :, :], AX.X))
            op(vec.reciprocal(gw[:, :], gsum[:, :]))
            first_max(sel[:, 0, :, :], e8a[:, :, :], down8, EPG, a[:, :], e8b[:, :, :])
            op(ts(e8c[:, :, :], sel[:, 0, :, :], -1.0, 1.0, ALU.mult, ALU.add))
            op(tt(e8c[:, :, :], e8a[:, :, :], e8c[:, :, :], ALU.mult))
            op(ts(e8d[:, :, :], sel[:, 0, :, :], -3.0e38, None, ALU.mult))
            op(tt(e8c[:, :, :], e8c[:, :, :], e8d[:, :, :], ALU.add))
            op(vec.reduce_max(gsum[:, :], e8c[:, :, :], AX.X))
            op(tt(e8b[:, :, :], e8c[:, :, :], wide(gsum[:, :], EPG), ALU.is_ge))
            op(tt(e8b[:, :, :], e8b[:, :, :], bc(down8[:, :].unsqueeze(1), [P, NT, EPG]), ALU.mult))
            op(vec.reduce_max(b[:, :], e8b[:, :, :], AX.X))
            op(tt(sel[:, 1, :, :], e8b[:, :, :], wide(b[:, :], EPG), ALU.is_equal))
            tt(c[:, :], gsum[:, :], a[:, :], ALU.subtract).then_inc(s_e2, 1)
            for k in range(2):
                op(tt(one_hot[:, k, :, :].rearrange("p t (g e) -> p t g e", g=NGRP), wide(sel_g[:, :, :], EPG),
                      bc(sel[:, k, :, :].unsqueeze(2), [P, NT, NGRP, EPG]), ALU.mult))
            op(tt(both[:, :, :], one_hot[:, 0, :, :], one_hot[:, 1, :, :], ALU.add))
            op(vec.memset(before[:, 0, :], 0.0))
            for n in range(1, NT):
                op(tt(before[:, n, :], before[:, n - 1, :], both[:, n - 1, :], ALU.add))
            op(tt(total[:, :], before[:, NT - 1, :], both[:, NT - 1, :], ALU.add))
            vec.nop().then_inc(s_cum, 1)
            vec.wait_ge(s_e2d, 1)
            op(ts(a[:, :], c[:, :], 1.0, None, ALU.add))
            op(vec.reciprocal(b[:, :], a[:, :]))
            op(tt(weights[:, 0, :], b[:, :], gw[:, :], ALU.mult))
            op(tt(weights[:, 1, :], weights[:, 0, :], c[:, :], ALU.mult))
            vec.wait_ge(s_cum_ps, 1)
            op(vec.tensor_copy(pos[:, :, :], ps[:, 0, 0:NT * EXPERTS].rearrange("p (t e) -> p t e", e=EXPERTS)))
            op(vec.tensor_copy(cnt[:, :], ps[:, 1, 0:EXPERTS]))
            op(tt(over_cmp[:, :, :], wide(cnt[:, :], STEPS), bc(steps[:, :].unsqueeze(1), [P, EXPERTS, STEPS]), ALU.is_gt))
            op(vec.reduce_sum(extra[:, :], over_cmp[:, :, :], AX.X))
            op(vec.tensor_tensor_scan(incl[:, :], ones32[:, :], extra[:, :], 0.0, ALU.mult, ALU.add))
            op(tt(start[:, :], incl[:, :], extra[:, :], ALU.subtract))
            op(ts(start[:, :], start[:, :], float(EXPERTS - 1), None, ALU.add))
            hot = one_hot[:, :, :, :].rearrange("p k t e -> p (k t) e")
            for k in range(2):
                op(tt(prod[:, k * NT:(k + 1) * NT, :], one_hot[:, k, :, :], pos[:, :, :], ALU.mult))
            op(vec.reduce_sum(pk[:, :], prod[:, :, :], AX.X))
            for out, per_expert in ((bk, start), (ek, iota32)):
                op(tt(prod[:, :, :], hot, bc(per_expert[:, :].unsqueeze(1), [P, 2 * NT, EXPERTS]), ALU.mult))
                op(vec.reduce_sum(out[:, :], prod[:, :, :], AX.X))
            op(tt(row_cmp[:, :, :], wide(pk[:, :], STEPS), bc(steps[:, :].unsqueeze(1), [P, 2 * NT, STEPS]), ALU.is_ge))
            op(vec.reduce_sum(bx[:, :], row_cmp[:, :, :], AX.X))
            op(vec.scalar_tensor_tensor(slot[:, :], bx[:, :], -float(BLK), pk[:, :], ALU.mult, ALU.add))
            op(tt(blk[:, :], bk[:, :], bx[:, :], ALU.add))
            op(tt(blk[:, :], blk[:, :], ek[:, :], ALU.subtract))
            op(ts(tmp[:, :], bx[:, :], 1.0, None, ALU.is_ge))
            op(tt(blk[:, :], blk[:, :], tmp[:, :], ALU.mult))
            op(tt(blk[:, :], blk[:, :], ek[:, :], ALU.add))
            op(vec.scalar_tensor_tensor(flat(dest), blk[:, :], float(BLK), slot[:, :], ALU.mult, ALU.add))
            for j in range(2 * NT):
                step.did(ts(slot_hot[:, j, :], iota_s[:, :], slot[:, j:j + 1], None, ALU.is_equal))
                step.did(ts(block_hot[:, j, :], iota_b[:, :], blk[:, j:j + 1], token[:, j % NT:j % NT + 1],
                            ALU.is_equal, ALU.mult))
            step.settle()
            vec.nop().then_inc(s_hot, 1)
            one = slice(0, 1)
            op(tt(over[:, :, :], bc(incl[one, :].unsqueeze(1), [1, OVER, EXPERTS]),
                  bc(iota32[one, 0:OVER].unsqueeze(2), [1, OVER, EXPERTS]), ALU.is_le))
            op(vec.reduce_sum(over_f[:, :], over[:, :, :], AX.X))
            op(ts(over_e[:, 0:OVER], over_f[:, :], float(EXPERTS - 1), None, ALU.min))
            op(vec.tensor_copy(over_n[:, :], incl[one, EXPERTS - 1:EXPERTS]))
            vec.wait_ge(s_rows, 1)
            op(vec.tensor_copy(row_tok[:, :], ps[:, 2, 0:NBLK]))

        @block.tensor
        def _(pe):
            pe.wait_ge(s_tri, 1)
            pe.wait_ge(s_cum, 1)
            cols = ps[:, 0, 0:NT * EXPERTS]
            pe.matmul(cols, tri[:, :], both[:, :, :].rearrange("p t e -> p (t e)"), start=True, stop=False)
            pe.matmul(cols, ones[:, :], before[:, :, :].rearrange("p t e -> p (t e)"), start=False, stop=True)
            pe.matmul(ps[:, 1, 0:EXPERTS], ones[:, :], total[:, :], start=True, stop=True).then_inc(s_cum_ps, 1)
            pe.wait_ge(s_hot, 1)
            for j in range(2 * NT):
                last = pe.matmul(ps[:, 2, 0:NBLK], slot_hot[:, j, :], block_hot[:, j, :], start=j == 0, stop=j == 2 * NT - 1)
            last.then_inc(s_rows, 1)
    return dict(weights=weights, dest=dest, row_tok=row_tok, over_e=over_e, over_n=over_n)


def expert_block(nc, m, ins, dr, t):
    at, sem = m.at, m.sem
    ident, raw, s_raw = t["ident"], t["moe_raw"], t["s_moe"]
    row_tok, over_e, over_n = t["row_tok"], t["over_e"], t["over_n"]
    GU, DN = 4, 4
    gu_hi, gu_lo = at("gu_hi", [P, GU, 2, HALF], 32, F32R), at("gu_lo", [P, GU, 2, HALF], 48, F32R)
    dn_hi, dn_lo = at("dn_hi", [P, DN, 2, HALF], 64, F32R), at("dn_lo", [P, DN, 2, HALF], 80, F32R)
    xg = at("x_gathered", [P, D], 96)
    xt_hi, xt_lo = at("moe_x_hi", [P, KD, P], 100, F32R), at("moe_x_lo", [P, KD, P], 104, F32R)
    sg, hid = at("moe_sig", [P, HALF], 108), at("moe_hid", [P, HALF], 110)
    ht_hi, ht_lo = at("moe_h_hi", [P, KF, P], 112, F32R), at("moe_h_lo", [P, KF, P], 114, F32R)
    y = at("moe_y", [P, D], 116)
    ple_raw, ple_raw2 = at("ple_raw", [P, 7, D], 120), at("ple_raw2", [P, 2, D], 196)
    s_ple, s_cleared = sem("ple_raw"), sem("g_cleared")
    names = ("gu_hi", "gu_lo", "gu_used", "dn_hi", "dn_lo", "dn_used", "xg", "xt", "xt_hi", "xt_lo", "sig",
             "t", "hid", "ht", "ht_hi", "ht_lo", "y", "y_out")
    (s_gu_hi, s_gu_lo, s_gu_used, s_dn_hi, s_dn_lo, s_dn_used, s_xg, s_xt, s_xt_hi, s_xt_lo, s_sig, s_t,
     s_hid, s_ht, s_ht_hi, s_ht_lo, s_y, s_y_out) = (sem(f"g_{n}") for n in names)
    G, U, DOWN, HT, XT = 0, 1, 2, 4, 5
    LAST = EXPERTS - 1
    gate_up = lambda k: raw[:, 2 * (k // 4):2 * (k // 4) + 2, (k % 4) * HALF:(k % 4 + 1) * HALF]
    down = lambda k: raw[:, 4 + k // 2, (k % 2) * D:(k % 2 + 1) * D].rearrange("p (h f) -> p h f", h=2)
    weight_v = [ins[n][0].rearrange("e (k p) f -> e p k f", p=P) for n in ("w_expert_gate", "w_expert_up", "w_expert_down")]

    def load(eng, j, expert):
        if j < 4:
            src, n, w = weight_v[j % 2], slice(4 * (j // 2), 4 * (j // 2) + 4), 4
        else:
            src, n, w = weight_v[2], slice(2 * (j - 4), 2 * (j - 4) + 2), 2
        eng.dma_start(raw[:, j, :].rearrange("p (k f) -> p k f", k=w),
                      src[bass.ds(expert, 1), :, n, :].rearrange("o p k f -> (o p) k f")).then_inc(s_raw[j], 16)

    def load_gate_up(eng, e, expert):
        for j in range(4):
            eng.wait_ge(s_gu_lo, e * 8 + (-4 if j < 2 else 0))
            load(eng, j, expert)

    def load_down(eng, e, expert):
        for j in (4, 5):
            eng.wait_ge(s_dn_lo, e * 4 + (2 if j == 4 else 4))
            load(eng, j, expert)

    def store(eng, e):
        eng.wait_ge(s_y, e + 2)
        eng.dma_start(dr["yr"][bass.ds(e * BLK, BLK), :], y[0:BLK, :]).then_inc(s_y_out, 16)

    def overflow(eng, body):
        n_over = eng.value_load(over_n[0:1, 0:1], min_val=0, max_val=OVER)
        with eng.If(n_over > 0):
            with eng.Fori(0, OVER) as b:
                with eng.If(n_over > b):
                    body(b)

    with ExitStack() as local:
        ps = local.enter_context(nc.psum_tensor("g_ps", [P, 8, HALF], F32))
        block = local.enter_context(nc.Block())

        @block.sync
        def _(sp):
            load_gate_up(sp, 1, 1)
            load_down(sp, 0, 0)
            with sp.Fori(3, LAST + 2) as i:
                load_gate_up(sp, i - 1, i - 1)
                load_down(sp, i - 2, i - 2)
                store(sp, i - 3)
            load_down(sp, LAST, LAST)
            store(sp, LAST - 1)
            gate = ins["w_ple_gate"][0].rearrange("(k p) d -> p k d", p=P)
            sp.dma_start(ple_raw[:, :, :], gate[:, 0:7, :]).then_inc(s_ple, 16)
            sp.dma_start(ple_raw2[:, 0, :], gate[:, 7, :]).then_inc(s_ple, 16)
            sp.dma_start(ple_raw2[:, 1, :], ins["w_ple_proj"][0, 0:P, :]).then_inc(s_ple, 16)
            store(sp, LAST)
            sp.wait_ge(s_y_out, 16 * (1 + EXPERTS))

        @block.gpsimd
        def _(gp):
            def gather(e):
                gp.wait_ge(s_xt, e + 1)
                gp.indirect_dma_start(out=xg[0:BLK, :], out_offset=None, in_=dr["xt"],
                                      in_offset=bass.IndirectOffsetOnAxis(ap=row_tok[0:BLK, e:e + 1].bitcast(U32), axis=0)
                                      ).then_inc(s_xg, 16)

            gp.memset(xg[:, :], 0.0).then_inc(s_cleared, 1)
            gp.wait_ge(s_cleared, 1)
            for e in range(EXPERTS):
                gather(e)
            n_over = gp.value_load(over_n[0:1, 0:1], min_val=0, max_val=OVER)
            with gp.If(n_over > 0):
                for b in range(OVER):
                    with gp.If(n_over > b):
                        gather(EXPERTS + b)
                        gp.wait_ge(s_y_out, 16 * (EXPERTS + b + 2))

        @block.scalar
        def _(act):
            act.nop().then_inc(s_y_out, 16)

            def gu_high(e, k):
                for j in (0, 1):
                    act.wait_ge(s_raw[2 * (k // 4) + j], e * 16 + 16)
                act.wait_ge(s_gu_used, e * 8 + (k + 1))
                act.activation(gu_hi[:, k % GU, :, :], gate_up(k), ACT.Copy).then_inc(s_gu_hi, 1)

            def dn_high(e, k):
                act.wait_ge(s_raw[4 + k // 2], e * 16 + 16)
                act.wait_ge(s_dn_used, e * 4 + (k + 1))
                act.activation(dn_hi[:, k, :, :], down(k), ACT.Copy).then_inc(s_dn_hi, 1)

            def sigmoid(e):
                act.wait_ge(s_gu_used, e * 8 + 12)
                act.wait_ge(s_hid, e + 1)
                act.activation(sg[:, :], ps[:, G, :], ACT.Sigmoid).then_inc(s_sig, 1)

            def x_high(e):
                act.wait_ge(s_xt, e + 2)
                act.activation(xt_hi[:, :, :].rearrange("p (b k) c -> p b (k c)", b=2), ps[:, XT:XT + 2, :],
                               ACT.Copy).then_inc(s_xt_hi, 1)

            def h_high(e):
                act.wait_ge(s_ht, e + 1)
                act.activation(ht_hi[:, :, :].rearrange("p k c -> p (k c)"), ps[:, HT, :], ACT.Copy).then_inc(s_ht_hi, 1)

            def y_out(e):
                act.wait_ge(s_dn_used, e * 4 + 8)
                act.wait_ge(s_y_out, e * 16 + 16)
                act.activation(y[:, :].rearrange("p (b f) -> p b f", b=2), ps[:, DOWN:DOWN + 2, :], ACT.Copy).then_inc(s_y, 1)

            def body(e, first=False, last=False):
                for k in range(2, KD):
                    gu_high(e, k)
                if not first:
                    for k in range(KF):
                        dn_high(e - 1, k)
                sigmoid(e)
                if not last:
                    x_high(e + 1)
                    gu_high(e + 1, 0)
                    gu_high(e + 1, 1)
                if not first:
                    y_out(e - 1)
                h_high(e)

            gu_high(0, 0)
            gu_high(0, 1)
            x_high(0)
            body(0, first=True)
            with act.Fori(1, LAST) as e:
                body(e)
            body(LAST, last=True)
            for k in range(KF):
                dn_high(LAST, k)
            y_out(LAST)

            def extra(b):
                e = b + EXPERTS
                expert = act.value_load(over_e[0:1, bass.ds(b, 1)], min_val=0, max_val=LAST)
                load_gate_up(act, e, expert)
                load_down(act, e, expert)
                x_high(e)
                for k in range(KD):
                    gu_high(e, k)
                sigmoid(e)
                for k in range(KF):
                    dn_high(e, k)
                h_high(e)
                y_out(e)
                store(act, e)

            overflow(act, extra)

        @block.vector
        def _(vec):
            vec.nop().then_inc(s_dn_lo, 4)
            vec.nop().then_inc(s_hid, 1)

            def gu_low(e, k):
                vec.wait_ge(s_gu_hi, e * 8 + (k + 1))
                vec.tensor_tensor(gu_lo[:, k % GU, :, :], gate_up(k), gu_hi[:, k % GU, :, :].bitcast(F32),
                                  ALU.subtract).then_inc(s_gu_lo, 1)

            def dn_low(e, k):
                vec.wait_ge(s_dn_hi, e * 4 + (k + 1))
                vec.tensor_tensor(dn_lo[:, k, :, :], down(k), dn_hi[:, k, :, :].bitcast(F32), ALU.subtract).then_inc(s_dn_lo, 1)

            def hidden(e):
                vec.wait_ge(s_sig, e + 1)
                vec.tensor_tensor(hid[:, :], ps[:, G, :], sg[:, :], ALU.mult).then_inc(s_t, 1)
                vec.wait_ge(s_t, e + 1)
                vec.tensor_tensor(hid[:, :], ps[:, U, :], hid[:, :], ALU.mult).then_inc(s_hid, 1)

            def x_low(e):
                vec.wait_ge(s_xt_hi, e + 1)
                vec.tensor_tensor(xt_lo[:, :, :].rearrange("p (b k) c -> p b (k c)", b=2), ps[:, XT:XT + 2, :],
                                  xt_hi[:, :, :].rearrange("p (b k) c -> p b (k c)", b=2).bitcast(F32),
                                  ALU.subtract).then_inc(s_xt_lo, 1)

            def h_low(e):
                vec.wait_ge(s_ht_hi, e + 1)
                vec.tensor_tensor(ht_lo[:, :, :].rearrange("p k c -> p (k c)"), ps[:, HT, :],
                                  ht_hi[:, :, :].rearrange("p k c -> p (k c)").bitcast(F32), ALU.subtract).then_inc(s_ht_lo, 1)

            def body(e, first=False, last=False):
                for k in range(2, KD):
                    gu_low(e, k)
                if not first:
                    for k in range(KF):
                        dn_low(e - 1, k)
                hidden(e)
                if not last:
                    x_low(e + 1)
                    gu_low(e + 1, 0)
                    gu_low(e + 1, 1)
                h_low(e)

            gu_low(0, 0)
            gu_low(0, 1)
            x_low(0)
            body(0, first=True)
            with vec.Fori(1, LAST) as e:
                body(e)
            body(LAST, last=True)
            for k in range(KF):
                dn_low(LAST, k)

            def extra(b):
                e = b + EXPERTS
                x_low(e)
                for k in range(KD):
                    gu_low(e, k)
                hidden(e)
                for k in range(KF):
                    dn_low(e, k)
                h_low(e)

            overflow(vec, extra)

        @block.tensor
        def _(pe):
            pe.nop().then_inc(s_gu_used, 4)
            pe.nop().then_inc(s_dn_used, 4)
            pe.nop().then_inc(s_xt, 1)
            pe.nop().then_inc(s_y, 1)

            def x_transposes(e):
                pe.wait_ge(s_xg, e * 16 + 16)
                for k in range(KD):
                    last = pe.transpose(ps[:, XT + k // 4, (k % 4) * P:(k % 4 + 1) * P], xg[:, k * P:(k + 1) * P], ident[:, :])
                last.then_inc(s_xt, 1)

            def gate_up_products(e):
                pe.wait_ge(s_xt_lo, e + 1)
                pe.wait_ge(s_hid, e + 1)
                for k in range(KD):
                    pe.wait_ge(s_gu_lo, e * 8 + (k + 1))
                    s, first, final = k % GU, k == 0, k == KD - 1
                    for i in (G, U):
                        pe.matmul(ps[:, i, :], xt_hi[:, k, :], gu_hi[:, s, i, :], start=first, stop=False)
                        pe.matmul(ps[:, i, :], xt_hi[:, k, :], gu_lo[:, s, i, :], start=False, stop=False)
                    for i in (G, U):
                        last = pe.matmul(ps[:, i, :], xt_lo[:, k, :], gu_hi[:, s, i, :], start=False, stop=final)
                    last.then_inc(s_gu_used, 1)

            def h_transposes(e):
                pe.wait_ge(s_hid, e + 2)
                for k in range(KF):
                    last = pe.transpose(ps[:, HT, k * P:(k + 1) * P], hid[:, k * P:(k + 1) * P], ident[:, :])
                last.then_inc(s_ht, 1)

            def down_products(e):
                pe.wait_ge(s_ht_lo, e + 1)
                pe.wait_ge(s_y, e + 1)
                for k in range(KF):
                    pe.wait_ge(s_dn_lo, e * 4 + (k + 5))
                    first, final = k == 0, k == KF - 1
                    for i in range(2):
                        pe.matmul(ps[:, DOWN + i, :], ht_hi[:, k, :], dn_hi[:, k, i, :], start=first, stop=False)
                        pe.matmul(ps[:, DOWN + i, :], ht_hi[:, k, :], dn_lo[:, k, i, :], start=False, stop=False)
                    for i in range(2):
                        last = pe.matmul(ps[:, DOWN + i, :], ht_lo[:, k, :], dn_hi[:, k, i, :], start=False, stop=final)
                    last.then_inc(s_dn_used, 1)

            x_transposes(0)
            gate_up_products(0)
            x_transposes(1)
            h_transposes(0)
            with pe.Fori(1, LAST) as e:
                gate_up_products(e)
                x_transposes(e + 1)
                down_products(e - 1)
                h_transposes(e)
            gate_up_products(LAST)
            down_products(LAST - 1)
            h_transposes(LAST)
            down_products(LAST)

            def extra(b):
                e = b + EXPERTS
                x_transposes(e)
                gate_up_products(e)
                h_transposes(e)
                down_products(e)

            overflow(pe, extra)
    return dict(ple_raw=ple_raw, ple_raw2=ple_raw2, s_ple=s_ple)


def output_block(nc, m, ins, dr, t, out):
    at, sem = m.at, m.sem
    ident, h, weights, dest = t["ident"], t["h"], t["weights"], t["dest"]
    wg_hi, wg_lo = at("wg_hi", [P, KD, D], 32, F32R), at("wg_lo", [P, KD, D], 64, F32R)
    wp_hi, wp_lo = at("wp_hi", [P, KP, D], 96, F32R), at("wp_lo", [P, KP, D], 104, F32R)
    last_raw = at("ple_raw3", [P, D], 112)
    raw = [t["ple_raw"][:, k, :] for k in range(7)] + [t["ple_raw2"][:, k, :] for k in range(2)] + [last_raw[:, :]]
    w_hi = [wg_hi[:, k, :] for k in range(KD)] + [wp_hi[:, k, :] for k in range(KP)]
    w_lo = [wg_lo[:, k, :] for k in range(KD)] + [wp_lo[:, k, :] for k in range(KP)]
    ON_POOL = (1, 3, 5)
    g_ple = at("g_ple", [P, D], 116)
    y12 = at("y12", [P, 2, D], 148)
    xn = at("ple_xn", [P, D], 156)
    xt_hi, xt_lo = at("ple_x_hi", [P, 2, KD, P], 160, F32R), at("ple_x_lo", [P, 2, KD, P], 168, F32R)
    p_rows = at("p_rows", [P, 2, PLE], 176)
    pt_hi, pt_lo = at("p_hi", [P, 2, KP, P], 178, F32R), at("p_lo", [P, 2, KP, P], 180, F32R)
    sig, prod = at("ple_sig", [P, 2, HALF], 182), at("ple_prod", [P, 2, HALF], 186)
    g_fin = at("g_final", [P, D], 190)
    ssq, rstd = at("h_ssq", [P, 2], 194), at("h_rstd", [P, 2], 194.125)
    ssq2, rstd2 = at("h_ssq2", [P, 2], 194.25), at("h_rstd2", [P, 2], 194.375)
    w_now = at("h_w", [P, 2], 194.625)
    rows_out = at("rows_out", [P, 2, D], 196)
    s_p, s_out = ([sem(f"h_{n}{s}") for s in range(2)] for n in ("p", "out"))
    names = ("par", "raw", "whi", "wsplit", "y1", "y2", "h1", "inv", "rstd", "xn", "xt", "x_hi", "x_lo",
             "mm", "sig", "h2", "inv2", "rstd2", "rows", "v_step")
    (s_par, s_raw, s_whi, s_wsplit, s_y1, s_y2, s_h1, s_inv, s_rstd, s_xn, s_xt, s_x_hi, s_x_lo, s_mm,
     s_sig, s_h2, s_inv2, s_rstd2, s_rows, v_step) = (sem(f"h_{n}") for n in names)
    XT, PT, GATE, PRJ = 0, 2, 4, 6
    row = lambda n: h[:, bass.ds(n, 1), :].rearrange("p o d -> p (o d)")

    with ExitStack() as local:
        ps = local.enter_context(nc.psum_tensor("h_ps", [P, 8, HALF], F32))
        block = local.enter_context(nc.Block())

        @block.sync
        def _(sp):
            p_v = ins["p"][0, 0].rearrange("(c t) e -> c t e", t=NT)
            out_v = out[0].rearrange("(c t) d -> c t d", t=NT)

            def load(n, s):
                sp.wait_ge(s_x_lo, n + 1)
                sp.dma_start(p_rows[:, s, :], p_v[:, bass.ds(n, 1), :].rearrange("c o e -> c (o e)")).then_inc(s_p[s], 16)

            def store(n, s):
                sp.wait_ge(s_rows, n + 1)
                sp.dma_start(out_v[:, bass.ds(n, 1), :].rearrange("c o d -> c (o d)"), rows_out[:, s, :]).then_inc(s_out[s], 16)

            sp.dma_start(last_raw[:, :], ins["w_ple_proj"][0, P:2 * P, :]).then_inc(s_raw, 16)
            load(0, 0)
            load(1, 1)
            load(2, 0)
            with sp.Fori(1, (NT - 4) // 2 + 1) as i:
                load(i * 2 + 1, 1)
                store(i * 2 - 2, 0)
                load(i * 2 + 2, 0)
                store(i * 2 - 1, 1)
            load(NT - 1, 1)
            for n in range(NT - 4, NT):
                store(n, n % 2)
            for s in range(2):
                sp.wait_ge(s_out[s], 16 * (1 + NT // 2))

        @block.gpsimd
        def _(gp):
            def split():
                for k in ON_POOL:
                    gp.wait_ge(s_whi, k + 1)
                    gp.tensor_tensor(w_lo[k], raw[k], w_hi[k].bitcast(F32), ALU.subtract).then_inc(s_wsplit, 1)

            for n in range(NT):
                if n == 1:
                    split()
                gp.wait_ge(s_h1, n + 1)
                for e, done in enumerate((s_y1, s_y2)):
                    gp.indirect_dma_start(out=y12[:, e, :], out_offset=None, in_=dr["yr"],
                                          in_offset=bass.IndirectOffsetOnAxis(ap=dest[:, e, n:n + 1].bitcast(U32), axis=0)
                                          ).then_inc(done, 16)

        @block.scalar
        def _(act):
            act.dma_start(g_ple[:, :], ins["norm_ple"][0].partition_broadcast(P)).then_inc(s_par, 16)
            act.dma_start(g_fin[:, :], ins["norm_final"].partition_broadcast(P)).then_inc(s_par, 16)
            for s in range(2):
                act.nop().then_inc(s_out[s], 16)

            def weights_high(first, end):
                for k in range(first, end):
                    if k == KD + KP - 1:
                        act.wait_ge(s_raw, 16)
                    act.activation(w_hi[k], raw[k], ACT.Copy).then_inc(s_whi, 1)

            def norm(n, s):
                act.wait_ge(s_inv, n + 1)
                act.activation(rstd[:, s:s + 1], rstd[:, s:s + 1], ACT.Sqrt).then_inc(s_rstd, 1)
                if isinstance(n, int) and n == 0:
                    weights_high(6, KD + KP)
                act.wait_ge(s_xt, n + 1)
                act.wait_ge(s_mm, n * 2 + 2)
                act.activation(xt_hi[:, s, :, :].rearrange("p (b k) c -> p b (k c)", b=2), ps[:, XT:XT + 2, :],
                               ACT.Copy).then_inc(s_x_hi, 1)
                act.activation(pt_hi[:, s, :, :], ps[:, PT, 0:KP * P].rearrange("p (k c) -> p k c", k=KP),
                               ACT.Copy).then_inc(s_x_hi, 1)

            def finish(n, s):
                for half in range(2):
                    act.wait_ge(s_mm, n * 2 + (5 + half))
                    act.wait_ge(s_h2, n * 2 + (half + 1))
                    act.activation(sig[:, half, :], ps[:, GATE + half, :], ACT.Sigmoid).then_inc(s_sig, 1)
                act.wait_ge(s_inv2, n + 1)
                act.activation(rstd2[:, s:s + 1], rstd2[:, s:s + 1], ACT.Sqrt).then_inc(s_rstd2, 1)

            act.wait_ge(t["s_ple"], 48)
            weights_high(0, 6)
            tile_pair_loop(act, norm, finish)

        @block.vector
        def _(vec):
            step = Counted(vec, v_step)
            vec.nop().then_inc(s_h1, 1)
            vec.nop().then_inc(s_x_lo, 2)
            vec.nop().then_inc(s_h2, 2)
            def split(slices):
                for k in slices:
                    if k not in ON_POOL:
                        vec.wait_ge(s_whi, k + 1)
                        vec.tensor_tensor(w_lo[k], raw[k], w_hi[k].bitcast(F32), ALU.subtract).then_inc(s_wsplit, 1)

            split(range(6))
            vec.wait_ge(s_par, 32)

            def inverse_mean_square(n, scratch, total, dst, done):
                step.did(vec.scalar_tensor_tensor(scratch, row(n), 1.0, row(n), ALU.mult, ALU.mult, accum_out=total))
                step.settle()
                step.did(vec.tensor_scalar(dst, total, 1.0 / D, EPS, ALU.mult, ALU.add))
                step.settle()
                vec.reciprocal(dst, dst).then_inc(done, 1)

            def combine(n, s):
                vec.wait_ge(s_y1, n * 16 + 16)
                vec.wait_ge(s_y2, n * 16 + 16)
                step.did(vec.tensor_copy(w_now[:, :].unsqueeze(2), weights[:, :, bass.ds(n, 1)]))
                step.settle()
                step.did(vec.scalar_tensor_tensor(row(n), y12[:, 0, :], w_now[:, 0:1], row(n), ALU.mult, ALU.add))
                step.settle()
                vec.scalar_tensor_tensor(row(n), y12[:, 1, :], w_now[:, 1:2], row(n), ALU.mult, ALU.add).then_inc(s_h1, 1)
                vec.wait_ge(s_h1, n + 2)
                inverse_mean_square(n, xn[:, :], ssq[:, s:s + 1], rstd[:, s:s + 1], s_inv)
                vec.wait_ge(s_rstd, n + 1)
                vec.scalar_tensor_tensor(xn[:, :], row(n), rstd[:, s:s + 1], g_ple[:, :], ALU.mult, ALU.mult).then_inc(s_xn, 1)
                if isinstance(n, int) and n == 0:
                    split(range(6, KD + KP))
                vec.wait_ge(s_x_hi, n * 2 + 2)
                step.did(vec.tensor_tensor(xt_lo[:, s, :, :].rearrange("p (b k) c -> p b (k c)", b=2), ps[:, XT:XT + 2, :],
                                  xt_hi[:, s, :, :].rearrange("p (b k) c -> p b (k c)", b=2).bitcast(F32), ALU.subtract))
                step.settle()
                vec.tensor_tensor(pt_lo[:, s, :, :], ps[:, PT, 0:KP * P].rearrange("p (k c) -> p k c", k=KP),
                                  pt_hi[:, s, :, :].bitcast(F32), ALU.subtract).then_inc(s_x_lo, 1)

            def gate(n, s):
                for half in range(2):
                    col = slice(half * HALF, (half + 1) * HALF)
                    vec.wait_ge(s_sig, n * 2 + (half + 1))
                    step.did(vec.tensor_tensor(prod[:, half, :], ps[:, PRJ + half, :], sig[:, half, :], ALU.mult))
                    step.settle()
                    vec.tensor_tensor(row(n)[:, col], row(n)[:, col], prod[:, half, :], ALU.add).then_inc(s_h2, 1)
                vec.wait_ge(s_h2, n * 2 + 4)
                inverse_mean_square(n, xn[:, :], ssq2[:, s:s + 1], rstd2[:, s:s + 1], s_inv2)
                vec.wait_ge(s_rstd2, n + 1)
                vec.wait_ge(s_out[s], n * 8 + (16 - 8 * s))
                vec.scalar_tensor_tensor(rows_out[:, s, :], row(n), rstd2[:, s:s + 1], g_fin[:, :], ALU.mult,
                                         ALU.mult).then_inc(s_rows, 1)

            PER = 2 * (5 + 4)
            tile_pair_loop(vec, combine, gate, step, PER)

        @block.tensor
        def _(pe):
            pe.nop().then_inc(s_mm, 4)

            def transposes(n, s):
                pe.wait_ge(s_p[s], n * 8 + (16 - 8 * s))
                pe.wait_ge(s_x_lo, n + 2)
                for k in range(KP):
                    pe.transpose(ps[:, PT, k * P:(k + 1) * P], p_rows[:, s, k * P:(k + 1) * P], ident[:, :])
                pe.wait_ge(s_xn, n + 1)
                for k in range(KD):
                    last = pe.transpose(ps[:, XT + k // 4, (k % 4) * P:(k % 4 + 1) * P], xn[:, k * P:(k + 1) * P], ident[:, :])
                last.then_inc(s_xt, 1)

            def products(n, s, ahead=True):
                pe.wait_ge(s_x_lo, n + 3)
                for half in range(2):
                    col = slice(half * HALF, (half + 1) * HALF)
                    pe.wait_ge(s_h2, n * 2 + (half + 1))
                    for hi, lo, high, low, depth, bank in ((pt_hi, pt_lo, wp_hi, wp_lo, KP, PRJ),
                                                            (xt_hi, xt_lo, wg_hi, wg_lo, KD, GATE)):
                        dst = ps[:, bank + half, :]
                        for k in range(depth):
                            if ahead and half == 1 and bank == GATE and k == KD // 2:
                                transposes(n + 1, 1 - s)
                            pe.matmul(dst, hi[:, s, k, :], high[:, k, col], start=k == 0, stop=False)
                            pe.matmul(dst, hi[:, s, k, :], low[:, k, col], start=False, stop=False)
                            last = pe.matmul(dst, lo[:, s, k, :], high[:, k, col], start=False, stop=k == depth - 1)
                    last.then_inc(s_mm, 1)

            transposes(0, 0)
            pe.wait_ge(s_wsplit, KD + KP)
            with pe.Fori(0, NT // 2 - 1) as i:
                products(i * 2, 0)
                products(i * 2 + 1, 1)
            products(NT - 2, 0)
            products(NT - 1, 1, ahead=False)


def build(nc, ins, out):
    m = Map(nc)
    shapes = dict(kpad=(GC, GROUPS, 15 * GC), proj=(2 * S5W, SEQ), y=(S5W, SEQ), merged=(D, SEQ), xt=(SEQ, D),
                  yr=(NBLK * BLK, D))
    dr = {n: nc.dram_tensor(f"scratch_{n}", s, F32, kind="Internal").ap() for n, s in shapes.items()}
    t = setup_block(nc, m, ins, dr)
    t |= project_block(nc, m, ins, dr, t)
    t |= gating_block(nc, m, ins, dr, t)
    t |= merge_block(nc, m, ins, dr, t)
    m.reuse_semaphores()
    t |= mixer_out_block(nc, m, ins, dr, t)
    t |= routing_block(nc, m, ins, dr, t)
    t |= expert_block(nc, m, ins, dr, t)
    output_block(nc, m, ins, dr, t, out)


_INS = ["x", "p", "norm_mix", "w_in", "s5_a_re", "s5_a_im", "s5_log_dt", "s5_b_re", "s5_b_im", "s5_c_re", "s5_c_im",
        "s5_d", "w_glu", "sgu_norm", "sgu_w", "sgu_b", "w_sgu_proj", "w_out", "norm_ffn", "w_router_group",
        "b_router_group", "w_router_expert", "b_router_expert", "w_expert_gate", "w_expert_up",
        "w_expert_down", "norm_ple", "w_ple_gate", "w_ple_proj", "norm_final"]


def kernel(**inputs):
    import numpy as np
    import concourse.bacc as bacc
    from concourse.bass_utils import run_bass_kernel_spmd

    nc = bacc.Bacc("TRN2", target_bir_lowering=False, num_devices=1)
    arrays, ins = {}, {}
    for name in _INS:
        a = np.ascontiguousarray(inputs[name])
        arrays[f"in_{name}"] = a
        ins[name] = nc.dram_tensor(f"in_{name}", a.shape, mybir.dt.from_np(a.dtype), kind="ExternalInput").ap()
    out = nc.dram_tensor("out_0", (1, SEQ, D), F32, kind="ExternalOutput").ap()
    build(nc, ins, out)
    return run_bass_kernel_spmd(nc, [arrays], core_ids=[0]).results[0]["out_0"]
```
